# Optimizing a Trainium2 kernel written in Bass

```python
import jax, jax.numpy as jnp
from jax import lax
import numpy as np

D_MODEL = 1024
BATCH = 1
SEQ = 128
DEPTH = 2
DEC_BATCH = 1
DEC_SEQ = 128
PAST_LEN = 128

GRID_W = 64
HEAD_DIM = 64
A_HEADS = 6
A_KV_HEADS = 2
A_GROUP = A_HEADS // A_KV_HEADS
WINDOW = 128
B_HEADS = 4
B_DK = 64
B_DV = 64
CHUNK = 64
F_BIAS = 3.0
C_HEADS = 6
C_Q_RANK = 256
C_KV_RANK = 128
C_NOPE = 64
C_ROPE = 32
C_QK = C_NOPE + C_ROPE
C_V = 64
A_Q = A_HEADS * HEAD_DIM
A_KV = A_KV_HEADS * HEAD_DIM
B_QK = B_HEADS * B_DK
B_V = B_HEADS * B_DV
C_OUT = C_HEADS * C_V
D_MIX = A_Q + B_V + C_OUT
IN_SIZES = (A_Q, A_KV, A_KV, B_QK, B_QK, B_V, B_V, 4 * B_HEADS, C_Q_RANK, C_KV_RANK, C_ROPE)
IN_SPLITS = tuple(sum(IN_SIZES[:i + 1]) for i in range(len(IN_SIZES) - 1))
D_IN = sum(IN_SIZES)
D_FF = 2816
N_EXPERTS = 8
TOP_K = 2
D_FF_EXPERT = 3584
N_DENSE = (DEPTH + 1) // 2
N_MOE = DEPTH // 2
Q_BLOCK = 128
ROPE_THETA = 10000.0
EPS = 1e-6
NEG_INF = -1e30

kernel_name = 'hybrid_diffusion_swa_mlstm_mla_step'

def rms_norm(x, g):
    xf = x.astype(jnp.float32)
    y = xf * lax.rsqrt(jnp.mean(xf * xf, axis=-1, keepdims=True) + EPS)
    return (y * g.astype(jnp.float32)).astype(x.dtype)

def grid_angles(seq_len, rot_dim):
    rows = seq_len // GRID_W
    row = jnp.repeat(jnp.arange(rows), GRID_W).astype(jnp.float32)
    col = jnp.tile(jnp.arange(GRID_W), rows).astype(jnp.float32)
    n_freq = rot_dim // 4
    freq = ROPE_THETA ** (-jnp.arange(n_freq, dtype=jnp.float32) / n_freq)
    ang = jnp.concatenate([row[:, None] * freq, col[:, None] * freq], axis=-1)
    return jnp.cos(ang), jnp.sin(ang)

def apply_rope(x, cos, sin):
    half = x.shape[-1] // 2
    shape = (1, cos.shape[0]) + (1,) * (x.ndim - 3) + (half,)
    c, s = cos.reshape(shape), sin.reshape(shape)
    x1, x2 = x[..., :half], x[..., half:]
    return jnp.concatenate([x1 * c - x2 * s, x1 * s + x2 * c], axis=-1).astype(x.dtype)

def rope_tail(x, cos, sin):
    return jnp.concatenate([x[..., :C_NOPE], apply_rope(x[..., C_NOPE:], cos, sin)], axis=-1)

def attend_block(q, k, v, bias, sink):
    scale = q.shape[-1] ** -0.5
    s = jnp.einsum('bqgrd,bkgd->bgrqk', q, k).astype(jnp.float32) * scale
    if bias is not None:
        s = s + bias
    if sink is not None:
        sk = jnp.broadcast_to(sink.astype(jnp.float32)[None, :, :, None, None], s.shape[:-1] + (1,))
        p = jax.nn.softmax(jnp.concatenate([s, sk], axis=-1), axis=-1)[..., :-1]
    else:
        p = jax.nn.softmax(s, axis=-1)
    return jnp.einsum('bgrqk,bkgd->bqgrd', p.astype(v.dtype), v)

def to_qblocks(q):
    b, s = q.shape[0], q.shape[1]
    return jnp.moveaxis(q.reshape((b, s // Q_BLOCK, Q_BLOCK) + q.shape[2:]), 1, 0)

def from_qblocks(ob, q_shape):
    return jnp.moveaxis(ob, 0, 1).reshape(q_shape[:-1] + (ob.shape[-1],))

def dense_attention(q, k, v, sink):
    ob = lax.map(lambda qi: attend_block(qi, k, v, None, sink), to_qblocks(q))
    return from_qblocks(ob, q.shape)

def window_attention(q, k, v, k_ctx, v_ctx, sink):
    s = q.shape[1]
    nb = s // Q_BLOCK
    band = Q_BLOCK + 2 * WINDOW
    pad = [(0, 0), (WINDOW, WINDOW), (0, 0), (0, 0)]
    kp, vp = jnp.pad(k, pad), jnp.pad(v, pad)
    n_ctx = k_ctx.shape[1]
    ctx_bias = jnp.zeros((Q_BLOCK, n_ctx), jnp.float32)

    def block(args):
        qi, n = args
        start = n * Q_BLOCK
        kb = lax.dynamic_slice_in_dim(kp, start, band, axis=1)
        vb = lax.dynamic_slice_in_dim(vp, start, band, axis=1)
        qpos = start + jnp.arange(Q_BLOCK)
        kpos = start - WINDOW + jnp.arange(band)
        ok = (jnp.abs(qpos[:, None] - kpos[None, :]) <= WINDOW) & ((kpos >= 0) & (kpos < s))[None, :]
        bias = jnp.concatenate([jnp.where(ok, 0.0, NEG_INF).astype(jnp.float32), ctx_bias], axis=1)
        return attend_block(qi, jnp.concatenate([kb, k_ctx.astype(kb.dtype)], axis=1),
                            jnp.concatenate([vb, v_ctx.astype(vb.dtype)], axis=1), bias, sink)

    ob = lax.map(block, (to_qblocks(q), jnp.arange(nb)))
    return from_qblocks(ob, q.shape)

def mlstm_scan(q, k, v, log_i, log_f, C0, n0, m0):
    b, s, h, _ = q.shape
    dv = v.shape[-1]
    nc = s // CHUNK

    def chunks(t):
        return jnp.moveaxis(t.astype(jnp.float32).reshape((b, nc, CHUNK) + t.shape[2:]), 1, 0)

    causal = jnp.tril(jnp.ones((CHUNK, CHUNK), bool))[None, :, :, None]

    def step(carry, xs):
        C, n, m = carry
        qt, kt, vt, li, lf = xs
        bc = jnp.cumsum(lf, axis=1)
        d = jnp.where(causal, bc[:, :, None, :] - bc[:, None, :, :] + li[:, None, :, :], NEG_INF)
        inter = bc + m[:, None, :]
        mt = jnp.maximum(inter, jnp.max(d, axis=2))
        a = jnp.exp(inter - mt)
        w = jnp.exp(d - mt[:, :, None, :]) * jnp.einsum('bthd,bshd->btsh', qt, kt)
        num = a[..., None] * jnp.einsum('bthd,bhde->bthe', qt, C) + jnp.einsum('btsh,bshe->bthe', w, vt)
        den = a * jnp.einsum('bthd,bhd->bth', qt, n) + jnp.sum(w, axis=2)
        ht = num / jnp.maximum(jnp.abs(den), jnp.exp(-mt))[..., None]
        bl = bc[:, -1, :]
        g = bl[:, None, :] - bc + li
        m_new = jnp.maximum(bl + m, jnp.max(g, axis=1))
        ws = jnp.exp(g - m_new[:, None, :])
        decay = jnp.exp(bl + m - m_new)
        C_new = decay[..., None, None] * C + jnp.einsum('bsh,bshd,bshe->bhde', ws, kt, vt)
        n_new = decay[..., None] * n + jnp.einsum('bsh,bshd->bhd', ws, kt)
        return (C_new, n_new, m_new), ht

    carry0 = (C0.astype(jnp.float32), n0.astype(jnp.float32), m0.astype(jnp.float32))
    (C, n, m), hc = lax.scan(step, carry0, (chunks(q), chunks(k), chunks(v), chunks(log_i), chunks(log_f)))
    return jnp.moveaxis(hc, 0, 1).reshape(b, s, h, dv), C, n, m

def mlstm_mixer(bq, bk, bv, bo, bg, gate_b, hn_g, C0, n0, m0):
    b, s = bq.shape[0], bq.shape[1]
    q = bq.reshape(b, s, B_HEADS, B_DK)
    k = bk.reshape(b, s, B_HEADS, B_DK) * (B_DK ** -0.5)
    v = bv.reshape(b, s, B_HEADS, B_DV)
    g = (bg.astype(jnp.float32) + gate_b.astype(jnp.float32)).reshape(b, s, 2, 2, B_HEADS)
    log_i = g[:, :, :, 0]
    log_f = jax.nn.log_sigmoid(g[:, :, :, 1])
    hf, Cf, nf, mf = mlstm_scan(q, k, v, log_i[:, :, 0], log_f[:, :, 0], C0[:, 0], n0[:, 0], m0[:, 0])
    rev = lambda t: jnp.flip(t, axis=1)
    hb, Cb, nb, mb = mlstm_scan(rev(q), rev(k), rev(v), rev(log_i[:, :, 1]), rev(log_f[:, :, 1]),
                                C0[:, 1], n0[:, 1], m0[:, 1])
    hsum = hf + rev(hb)
    out = rms_norm(hsum, hn_g) * jax.nn.sigmoid(bo.astype(jnp.float32).reshape(b, s, B_HEADS, B_DV))
    out = out.astype(bq.dtype).reshape(b, s, B_V)
    return out, jnp.stack([Cf, Cb], axis=1), jnp.stack([nf, nb], axis=1), jnp.stack([mf, mb], axis=1)

def mla_kv(ckv_n, k_rope, wukv, kn_g):
    b, s = ckv_n.shape[0], ckv_n.shape[1]
    kv = (ckv_n @ wukv).reshape(b, s, C_HEADS, C_NOPE + C_V)
    kr = jnp.broadcast_to(k_rope[:, :, None, :], (b, s, C_HEADS, C_ROPE)).astype(kv.dtype)
    k = rms_norm(jnp.concatenate([kv[..., :C_NOPE], kr], axis=-1), kn_g)
    return k, kv[..., C_NOPE:]

def token_mixer(xn, lw, ctx):
    b, s = xn.shape[0], xn.shape[1]
    aq, ak, av, bq, bk, bv, bo, bg, cq, ckv, ckr = jnp.split(xn @ lw['w_in'], IN_SPLITS, axis=-1)
    qa = rms_norm(aq.reshape(b, s, A_KV_HEADS, A_GROUP, HEAD_DIM), lw['a_qn_g'])
    ka = rms_norm(ak.reshape(b, s, A_KV_HEADS, HEAD_DIM), lw['a_kn_g'])
    va = av.reshape(b, s, A_KV_HEADS, HEAD_DIM)
    sink = lw['a_sink'].reshape(A_KV_HEADS, A_GROUP)
    ckv_n = rms_norm(ckv, lw['c_kva_g'])
    qc = rms_norm((rms_norm(cq, lw['c_qa_g']) @ lw['c_wuq']).reshape(b, s, C_HEADS, C_QK), lw['c_qn_g'])
    kc, vc = mla_kv(ckv_n, ckr, lw['c_wukv'], lw['c_kn_g'])
    if ctx is None:
        oa = dense_attention(qa, ka, va, sink)
        zC = jnp.zeros((b, 2, B_HEADS, B_DK, B_DV), jnp.float32)
        zn = jnp.zeros((b, 2, B_HEADS, B_DK), jnp.float32)
        zm = jnp.zeros((b, 2, B_HEADS), jnp.float32)
        ob, C, n, m = mlstm_mixer(bq, bk, bv, bo, bg, lw['b_gate_b'], lw['b_hn_g'], zC, zn, zm)
        oc = dense_attention(qc[:, :, :, None, :], kc, vc, None)
        new = (ka, va, ckv_n, ckr, C, n, m)
    else:
        k_ctx, v_ctx, ckv_ctx, kr_ctx, C0, n0, m0 = ctx
        cos, sin = grid_angles(s, HEAD_DIM)
        oa = window_attention(apply_rope(qa, cos, sin), apply_rope(ka, cos, sin), va, k_ctx, v_ctx, sink)
        ob, _, _, _ = mlstm_mixer(bq, bk, bv, bo, bg, lw['b_gate_b'], lw['b_hn_g'], C0, n0, m0)
        cos_r, sin_r = grid_angles(s, C_ROPE)
        kc_ctx, vc_ctx = mla_kv(ckv_ctx, kr_ctx, lw['c_wukv'], lw['c_kn_g'])
        k_all = jnp.concatenate([kc_ctx.astype(kc.dtype), rope_tail(kc, cos_r, sin_r)], axis=1)
        v_all = jnp.concatenate([vc_ctx.astype(vc.dtype), vc], axis=1)
        oc = dense_attention(rope_tail(qc, cos_r, sin_r)[:, :, :, None, :], k_all, v_all, None)
        new = None
    o = jnp.concatenate([oa.reshape(b, s, A_Q), ob.astype(oa.dtype), oc.reshape(b, s, C_OUT)], axis=-1)
    return o @ lw['w_out'], new

def swiglu(x, w1, w3, w2):
    return (jax.nn.silu(x @ w1) * (x @ w3)) @ w2

def moe_ffn(x, router, w1, w3, w2):
    logits = (x @ router).astype(jnp.float32)
    top_v, top_i = lax.top_k(logits, TOP_K)
    wts = jax.nn.softmax(top_v, axis=-1)
    gates = jnp.sum(jax.nn.one_hot(top_i, N_EXPERTS, dtype=jnp.float32) * wts[..., None], axis=-2)
    out = jnp.zeros(x.shape, jnp.float32)
    for e in range(N_EXPERTS):
        out = out + gates[..., e:e + 1] * swiglu(x, w1[e], w3[e], w2[e])
    return out.astype(x.dtype)

def setup_inputs(seed: int = 0) -> dict:
    key = jax.random.key(seed)
    keys = iter(jax.random.split(key, 40))

    def nrm(shape, scale=1.0):
        return scale * jax.random.normal(next(keys), shape, jnp.float32)

    def gain(shape):
        return 1.0 + nrm(shape, 0.05)

    gate_offset = jnp.tile(jnp.repeat(jnp.array([0.0, F_BIAS], jnp.float32), B_HEADS), 2)
    return {
        'x_prompt': nrm((BATCH, SEQ, D_MODEL)),
        'x_sample': nrm((DEC_BATCH, DEC_SEQ, D_MODEL)),
        'c': nrm((DEC_BATCH, D_MODEL)),
        'cache_swa_k': nrm((DEC_BATCH, DEPTH, PAST_LEN, A_KV_HEADS, HEAD_DIM)),
        'cache_swa_v': nrm((DEC_BATCH, DEPTH, PAST_LEN, A_KV_HEADS, HEAD_DIM)),
        'cache_mla_ckv': nrm((DEC_BATCH, DEPTH, PAST_LEN, C_KV_RANK)),
        'cache_mla_krope': nrm((DEC_BATCH, DEPTH, PAST_LEN, C_ROPE)),
        'state_mlstm_C': nrm((DEC_BATCH, DEPTH, 2, B_HEADS, B_DK, B_DV), 0.5),
        'state_mlstm_n': nrm((DEC_BATCH, DEPTH, 2, B_HEADS, B_DK), 0.5),
        'state_mlstm_m': nrm((DEC_BATCH, DEPTH, 2, B_HEADS), 0.1),
        'c_ctx': nrm((D_MODEL,)),
        'ada_w': nrm((DEPTH, D_MODEL, 6 * D_MODEL), 0.5 * D_MODEL ** -0.5),
        'ada_b': nrm((DEPTH, 6 * D_MODEL), 0.02),
        'norm1_g': gain((DEPTH, D_MODEL)),
        'norm2_g': gain((DEPTH, D_MODEL)),
        'w_in': nrm((DEPTH, D_MODEL, D_IN), D_MODEL ** -0.5),
        'a_qn_g': gain((DEPTH, HEAD_DIM)),
        'a_kn_g': gain((DEPTH, HEAD_DIM)),
        'a_sink': nrm((DEPTH, A_HEADS), 0.5),
        'b_gate_b': nrm((DEPTH, 4 * B_HEADS), 0.1) + gate_offset,
        'b_hn_g': gain((DEPTH, B_DV)),
        'c_qa_g': gain((DEPTH, C_Q_RANK)),
        'c_kva_g': gain((DEPTH, C_KV_RANK)),
        'c_wuq': nrm((DEPTH, C_Q_RANK, C_HEADS * C_QK), C_Q_RANK ** -0.5),
        'c_wukv': nrm((DEPTH, C_KV_RANK, C_HEADS * (C_NOPE + C_V)), C_KV_RANK ** -0.5),
        'c_qn_g': gain((DEPTH, C_QK)),
        'c_kn_g': gain((DEPTH, C_QK)),
        'w_out': nrm((DEPTH, D_MIX, D_MODEL), D_MIX ** -0.5),
        'ffn_w1': nrm((N_DENSE, D_MODEL, D_FF), D_MODEL ** -0.5),
        'ffn_w3': nrm((N_DENSE, D_MODEL, D_FF), D_MODEL ** -0.5),
        'ffn_w2': nrm((N_DENSE, D_FF, D_MODEL), D_FF ** -0.5),
        'moe_router': nrm((N_MOE, D_MODEL, N_EXPERTS), D_MODEL ** -0.5),
        'moe_w1': nrm((N_MOE, N_EXPERTS, D_MODEL, D_FF_EXPERT), D_MODEL ** -0.5),
        'moe_w3': nrm((N_MOE, N_EXPERTS, D_MODEL, D_FF_EXPERT), D_MODEL ** -0.5),
        'moe_w2': nrm((N_MOE, N_EXPERTS, D_FF_EXPERT, D_MODEL), D_FF_EXPERT ** -0.5),
    }

def reference(x_prompt, x_sample, c, cache_swa_k, cache_swa_v, cache_mla_ckv, cache_mla_krope,
              state_mlstm_C, state_mlstm_n, state_mlstm_m, c_ctx, ada_w, ada_b, norm1_g, norm2_g,
              w_in, a_qn_g, a_kn_g, a_sink, b_gate_b, b_hn_g, c_qa_g, c_kva_g, c_wuq, c_wukv,
              c_qn_g, c_kn_g, w_out, ffn_w1, ffn_w3, ffn_w2, moe_router, moe_w1, moe_w3, moe_w2):

    def channel(xn, l):
        i = l // 2
        if l % 2 == 0:
            return swiglu(xn, ffn_w1[i], ffn_w3[i], ffn_w2[i])
        return moe_ffn(xn, moe_router[i], moe_w1[i], moe_w3[i], moe_w2[i])

    def block(x, cvec, l, ctx):
        lw = {'w_in': w_in[l], 'a_qn_g': a_qn_g[l], 'a_kn_g': a_kn_g[l], 'a_sink': a_sink[l],
              'b_gate_b': b_gate_b[l], 'b_hn_g': b_hn_g[l], 'c_qa_g': c_qa_g[l], 'c_kva_g': c_kva_g[l],
              'c_wuq': c_wuq[l], 'c_wukv': c_wukv[l], 'c_qn_g': c_qn_g[l], 'c_kn_g': c_kn_g[l],
              'w_out': w_out[l]}
        mod = (jax.nn.silu(cvec) @ ada_w[l] + ada_b[l])[:, None, :]
        sh1, sc1, g1, sh2, sc2, g2 = jnp.split(mod, 6, axis=-1)
        o, new = token_mixer(rms_norm(x, norm1_g[l]) * (1 + sc1) + sh1, lw, ctx)
        x = x + g1 * o
        x = x + g2 * channel(rms_norm(x, norm2_g[l]) * (1 + sc2) + sh2, l)
        return x, new

    y_prompt, y_sample = x_prompt, x_sample
    news = []
    for l in range(DEPTH):
        y_prompt, new = block(y_prompt, c_ctx[None, :], l, None)
        news.append(new)
        ctx = (cache_swa_k[:, l], cache_swa_v[:, l], cache_mla_ckv[:, l], cache_mla_krope[:, l],
               state_mlstm_C[:, l], state_mlstm_n[:, l], state_mlstm_m[:, l])
        y_sample, _ = block(y_sample, c, l, ctx)

    def stack(j):
        return jnp.stack([nw[j] for nw in news], axis=1)

    new_swa_k = stack(0)
    new_swa_v = stack(1)
    new_mla_ckv = stack(2)
    new_mla_krope = stack(3)
    new_mlstm_C = stack(4)
    new_mlstm_n = stack(5)
    new_mlstm_m = stack(6)
    return (y_prompt, y_sample, new_swa_k, new_swa_v, new_mla_ckv, new_mla_krope, new_mlstm_C, new_mlstm_n, new_mlstm_m)


_drawn_inputs = setup_inputs


def setup_inputs(seed=0):
    import zlib

    import numpy as np

    out = dict(_drawn_inputs(seed))
    spreads = {}
    factors = {'cache_mla_krope': 5.127,
     'state_mlstm_n': 3.588,
     'state_mlstm_m': 8.0,
     'a_qn_g': 8.0,
     'a_sink': 64.0,
     'b_hn_g': 4.41,
     'c_qa_g': 8.0,
     'c_qn_g': 8.0,
     'c_kn_g': 8.0}
    for name, (base, spread) in spreads.items():
        noise = np.random.default_rng([zlib.crc32(name.encode()), seed]).standard_normal(out[name].shape)
        drawn = base * np.exp(spread * noise) if base else spread * noise
        out[name] = __import__('jax').numpy.asarray(drawn.astype(out[name].dtype))
    for name, factor in factors.items():
        out[name] = (out[name] * factor).astype(out[name].dtype)
    return out
```

```python
import concourse.bass as bass
from concourse import mybir
from contextlib import ExitStack
import numpy as np

D = 1024
TOK = 128
DEPTH = 2
KD = D // 128
HD = 64
A_H, A_KV, A_G = 6, 2, 3
B_H = 4
C_H, C_NOPE, C_ROPE, C_V = 6, 64, 32, 64
C_QK = C_NOPE + C_ROPE
C_QR, C_KVR = 256, 128
SIZES = (A_H * HD, A_KV * HD, A_KV * HD, 256, 256, 256, 256, 4 * B_H, C_QR, C_KVR, C_ROPE)
(AQ, AK, AV, BQ, BK, BV, BO, BG, CQ, CKV, CKR), D_IN = [sum(SIZES[:i]) for i in range(11)], sum(SIZES)
D_FF, N_EXP, D_FFE = 2816, 8, 3584
EPS = 1e-6
GRID_W, THETA, BIG = 64, 10000.0, 1e30

IN_CUTS = [0, 420, 840, 1260, 1680, D_IN]
FF = 256
N_FF = D_FF // FF
FE = 512
N_FE = D_FFE // FE
SLOT, N_SLOT = 2048, 7
PER_EXPERT = 6 * N_FE

CONST = {}
_at = 0
for _n, _w in (("ident", 128), ("s_le_t", 128), ("s_ge_t", 128), ("s_lt_t", 128), ("ones", 128), ("row_last", 128),
               ("row_first", 128), ("iota", 128), ("mask", 256), ("pick", 1024), ("cosA", 32), ("sinA", 32),
               ("cosC", 16), ("sinC", 16), ("iota8", 8)):
    CONST[_n] = (_at, _at + _w)
    _at += _w
N_CONST = _at

GAIN = {}
_at = 0
for _n, _w in (("a_qn_g", 64), ("a_kn_g", 64), ("c_qa_g", 256), ("c_kva_g", 128), ("c_qn_g", 96), ("c_kn_g", 96),
               ("b_hn_g", 64), ("b_gate_b", 16), ("a_sink", 6), ("m0", 8)):
    GAIN[_n] = (_at, _at + _w)
    _at += _w
N_GAIN = _at


def constants():
    t = np.zeros((128, N_CONST), np.float32)
    i = np.arange(128)

    def put(name, what):
        t[:what.shape[0], CONST[name][0]:CONST[name][1]] = what

    put("ident", np.eye(128))
    put("s_le_t", i[:, None] <= i[None, :])
    put("s_ge_t", i[:, None] >= i[None, :])
    put("s_lt_t", i[:, None] < i[None, :])
    put("ones", np.ones((128, 128)))
    put("row_last", np.repeat((i == 127)[:, None], 128, 1))
    put("row_first", np.repeat((i == 0)[:, None], 128, 1))
    put("iota", np.repeat(i[None, :], 128, 0))
    put("mask", BIG * np.concatenate([i[:, None] > i[None, :], i[:, None] < i[None, :]], 1))
    put("pick", np.repeat(np.eye(8)[:, :, None], 128, 2).reshape(8, 1024))
    put("iota8", np.repeat(np.arange(8)[None, :], 128, 0))
    for name, dim in (("A", HD), ("C", C_ROPE)):
        n = dim // 4
        freq = (np.float32(THETA) ** (-np.arange(n, dtype=np.float32) / np.float32(n))).astype(np.float32)
        row, col = (i // GRID_W).astype(np.float32), (i % GRID_W).astype(np.float32)
        ang = np.concatenate([row[:, None] * freq, col[:, None] * freq], 1).astype(np.float32)
        put("cos" + name, np.cos(ang))
        put("sin" + name, np.sin(ang))
    return t


def build_program(nc, I, O):
    f32, i32, u32 = mybir.dt.float32, mybir.dt.int32, mybir.dt.uint32
    ALU, ACT, AX = mybir.AluOpType, mybir.ActivationFunctionType, mybir.AxisListType
    ctx = ExitStack()
    with ctx:
        def sb(name, shape, dt=f32):
            return ctx.enter_context(nc.sbuf_tensor(name, shape, dt))

        def sem(name):
            return ctx.enter_context(nc.semaphore(name))

        ring = sb("ring", [128, N_SLOT, SLOT])
        x = sb("x", [128, 2, D])
        xr = sb("xr", [128, 2, D])
        xnT = sb("xnT", [128, KD, 2 * TOK])
        h = sb("h", [128, 2, D_IN])
        o = sb("o", [128, 2, D])
        cst = sb("cst", [128, N_CONST])
        gain = sb("gain", [128, DEPTH, N_GAIN])
        ctx_k = sb("ctx_k", [128, DEPTH, 128])
        ctx_v = sb("ctx_v", [128, DEPTH, 128])
        ctx_ckv = sb("ctx_ckv", [128, DEPTH, 128])
        ctx_kr = sb("ctx_kr", [128, DEPTH, C_ROPE])
        C0n0 = sb("C0n0", [128, DEPTH, 2, 2, HD + 1])
        m0row = sb("m0row", [8, 1 + DEPTH])
        gate = sb("gate", [128, 2, 2, D])
        modT = sb("modT", [128, 4, KD, 2])
        modS = sb("modS", [128, 2, KD, 2])
        modrow = sb("modrow", [2, 2, 512])
        crow = sb("crow", [2 * KD, 128])
        cT = sb("cT", [128, 2 * KD])
        ngrow = sb("ngrow", [4 * KD, 128])
        ngT = sb("ngT", [128, 4 * KD])
        router = sb("router", [128, KD, N_EXP])
        SCR = 6912
        scr = sb("scr", [128, 2, SCR])
        small = sb("small", [128, 2, 320])
        ka_out = sb("ka_out", [128, 128])
        ckv_out = sb("ckv_out", [128, 128])
        n_pass = sb("n_pass", [128, 1], i32)
        PS = ctx.enter_context(nc.psum_tensor("PS", [128, 8, 512], f32))

        def K(name, rows=128):
            return cst[0:rows, CONST[name][0]:CONST[name][1]]

        def G(l, name):
            return gain[:, l, GAIN[name][0]:GAIN[name][1]]

        def R(s, a, n, parts=128):
            return scr[0:parts, s, a:a + n]

        def SM(s, a, n, parts=128):
            return small[0:parts, s, a:a + n]

        def bank(b, n=512, parts=128, a=0):
            return PS[0:parts, b, a:a + n]

        def banks(b, n, parts=128):
            return PS[0:parts, :, :].rearrange("p b n -> p (b n)")[:, b * 512:b * 512 + n]

        ident = K("ident")
        PICK = K("pick", 8).rearrange("p (c t) -> p c t", c=8)

        SQ, QK, QKT, VC = 0, 1728, 3456, 5760
        V1, KW, KS, NUM, H8 = QKT + 512, QKT + 772, QKT + 1284, QKT + 1540, VC
        SIG, BSQ = QK + 1024, QK + 1280
        ST = 1024
        W = scr[:, :, :].rearrange("p s n -> p (s n)")
        F_H, F_T, F_Y, F_XE, F_ACC, F_P, F_PG, F_PT = 0, 1024, 2048, 3072, 4096, 6144, 6400, 6656

        cols = {}
        at = 0
        for name, w in (("var", 18), ("rs", 18), ("tmp", 18), ("bits", 18), ("mx", 6), ("nm", 6), ("ls", 6), ("es", 6),
                        ("g16", 16), ("absf", 8), ("expl", 8), ("lf", 8), ("m16", 16), ("u", 8), ("em", 8), ("a", 8),
                        ("mo", 8), ("ws", 8), ("lg", 8), ("v8", 8), ("i8", 8), ("if", 2), ("sel", 8), ("gt", 8),
                        ("eq", 8), ("posm", 8), ("ssq", 1), ("e2", 1), ("w1", 1), ("w2", 1), ("cnt", 1), ("rinv", 6)):
            cols[name] = (at, w)
            at += w
        assert at <= 320
        MFB = sb("MFB", [8, 2, 3, 128])

        def c_(s, name, n=None):
            a, w = cols[name]
            return SM(s, a, n or w)

        def slot(n, words=SLOT):
            return ring[:, n % N_SLOT, 0:words]

        loads = []

        def add(words, src, **dims):
            n = len(loads)
            loads.append((slot(n, words).rearrange("p (a c) -> p a c", **dims), src))
            return n

        def rows(w, k0, k1, c0, c1):
            return w[128 * k0:128 * k1, c0:c1].rearrange("(k p) c -> p k c", p=128)

        first = {}
        for l in range(DEPTH):
            first["ada", l] = len(loads)
            for n in range(12):
                for k in (0, 4):
                    add(2048, rows(I["ada_w"][l], k, k + 4, 512 * n, 512 * n + 512), a=4)
            first["in", l] = len(loads)
            for n in range(5):
                c0, c1 = IN_CUTS[n:n + 2]
                for k in (0, 4):
                    add(4 * (c1 - c0), rows(I["w_in"][l], k, k + 4, c0, c1), a=4)
            first["uq", l] = add(2 * C_H * C_QK, rows(I["c_wuq"][l], 0, 2, 0, C_H * C_QK), a=2)
            first["ukv", l] = add(C_H * 128, rows(I["c_wukv"][l], 0, 1, 0, C_H * 128), a=1)
            first["out", l] = len(loads)
            for n in range(2):
                for k in (0, 4):
                    add(2048, rows(I["w_out"][l], k, k + 4, 512 * n, 512 * n + 512), a=4)
            if l == 0:
                def w2_load(f):
                    first["w2", f] = add(2048, rows(I["ffn_w2"][0], 2 * f, 2 * f + 2, 0, D), a=2)

                for f in range(N_FF):
                    first["w1", f] = add(2048, rows(I["ffn_w1"][0], 0, KD, FF * f, FF * f + FF), a=KD)
                    first["w3", f] = add(2048, rows(I["ffn_w3"][0], 0, KD, FF * f, FF * f + FF), a=KD)
                    if f:
                        w2_load(f - 1)
                w2_load(N_FF - 1)
        W0 = len(loads)
        expert_order = []
        for f in range(N_FE):
            expert_order += [("w1", f, 0), ("w1", f, 1), ("w3", f, 0), ("w3", f, 1)]
            if f:
                expert_order += [("w2", f - 1, 0), ("w2", f - 1, 1)]
        expert_order += [("w2", N_FE - 1, 0), ("w2", N_FE - 1, 1)]
        expert_at = {key: j for j, key in enumerate(expert_order)}
        assert len(expert_order) == PER_EXPERT and PER_EXPERT % N_SLOT == 0
        FULL_PER_EXPERT = 16 * PER_EXPERT // N_SLOT

        slot_full = [sem(f"slot_full{i}") for i in range(N_SLOT)]
        slot_used = sem("slot_used")
        first_in, small_in, adab_in = sem("first_in"), sem("small_in"), [sem("adab_in0"), sem("adab_in1")]
        out_sem = [sem("out_sem0"), sem("out_sem1")]
        state_out = [sem("state_out0"), sem("state_out1")]
        y_out = sem("y_out")
        dve_chain, act_chain = sem("dve_chain"), sem("act_chain")
        setup_T, c_ready, ng_ready, zeros_ready = sem("setup_T"), sem("c_ready"), sem("ng_ready"), sem("zeros_ready")
        names = ["modrow_ready", "mod_T", "mod_ready", "gate_bc", "gate_copied",
                 "ssq_ready", "xr_ready", "xr_T", "xnT_a", "xnT_d", "x_done",
                 "in_mm", "h_ready",
                 "qkA_ready", "TA", "TA_ready", "SA", "nmA", "PA", "PTA", "PTA_a", "PTA_d", "OA", "oA",
                 "cn_ready", "TC", "TC_ready", "C_mm", "C_heads", "C_headsx", "qkC_ready", "TC1", "TC1_a",
                 "TC1_d", "TC2", "TC2_a", "SC", "nmC", "PC", "PTC", "PTC_a", "PTC_d", "OC", "oC",
                 "absf_ready", "log_ready", "lf_ready", "bc_T", "u_ready", "qkB_T", "uT_S", "run_ready", "M_mm",
                 "Earg_ready", "E_ready", "last_mm", "WT_ready", "ws_arg", "ws_ready", "kw_ready", "num_mm",
                 "state_copied", "oB", "o_T", "oT_a", "oT_d", "out_mm",
                 "up_mm", "silu_ready", "hid_ready", "hid_T", "hT_ready", "down_mm",
                 "xn_T", "xn_a", "xn_d", "logits_mm", "gap_ready", "gap_exp", "sel_ready", "pos_mm", "pass_ready",
                 "P_ready", "gather_mm", "Pg_T", "xe_a", "xe_d", "Pg_a", "e_silu", "e_hid", "e_T", "e_hT",
                 "y_a", "y_d", "scat_mm", "acc_done", "places_moved"]
        Q = {n: sem(n) for n in names}

        def summed(eng, n, it=None):
            eng.wait_ge(slot_used, n + 1 if it is None else it * PER_EXPERT + (n + 1))

        block = ctx.enter_context(nc.Block())

        @block.sync
        def _(sp):
            for n, (dst, src) in enumerate(loads):
                if n >= N_SLOT:
                    sp.wait_ge(slot_used, n - N_SLOT + 1)
                sp.dma_start(dst, src).then_inc(slot_full[n % N_SLOT], 16)
            sp.wait_ge(Q["pass_ready"], 1)
            passes = sp.value_load(n_pass[0:1, 0:1], min_val=1, max_val=2)
            with sp.Fori(0, passes) as p:
                with sp.Fori(0, N_EXP) as e:
                    it = p * N_EXP + e
                    for j, (kind, f, half) in enumerate(expert_order):
                        n = W0 + j
                        dst = slot(n)
                        if kind == "w2":
                            r0 = FE * f + 256 * half
                            src = I["moe_w2"][0][bass.ds(e, 1), r0:r0 + 256, :]
                            src = src.rearrange("e (k p) c -> p (e k) c", p=128)
                            dst = dst.rearrange("p (a c) -> p a c", a=2)
                        else:
                            w = I["moe_" + kind][0]
                            src = w[bass.ds(e, 1), 512 * half:512 * half + 512, FE * f:FE * f + FE]
                            src = src.rearrange("e (k p) c -> p (e k) c", p=128)
                            dst = dst.rearrange("p (a c) -> p a c", a=4)
                        sp.wait_ge(slot_used, it * PER_EXPERT + (n - N_SLOT + 1))
                        sp.dma_start(dst, src).then_inc(slot_full[n % N_SLOT], 16)
            sp.wait_ge(y_out, 32)
            for l in range(DEPTH):
                sp.wait_ge(out_sem[l], 16 * 4)
                sp.wait_ge(state_out[l], 16 * 3)

        N_FIRST = 6
        N_SMALL = DEPTH * (len(GAIN) + 4 + 2 * 2 * 2 + 1) + 2

        @block.gpsimd
        def _(pool):
            def load(dst, src, s=small_in, **how):
                pool.dma_start(dst, src, **how).then_inc(s, 16)

            load(cst[:, :], I["consts"], first_in)
            load(crow[0:KD, :], I["c_ctx"].rearrange("(k p) -> k p", p=128), first_in)
            load(crow[KD:2 * KD, :], I["c"].rearrange("a (k p) -> (a k) p", p=128), first_in)
            load(ngrow[0:2 * KD, :], I["norm1_g"].rearrange("l (k p) -> (l k) p", p=128), first_in)
            load(ngrow[2 * KD:4 * KD, :], I["norm2_g"].rearrange("l (k p) -> (l k) p", p=128), first_in)
            load(R(0, 0, 6144, 2), I["ada_b"][0:1, :].broadcast_to([2, 6144]), adab_in[0])
            load(x[:, 0, :], I["x_prompt"][0], first_in)
            load(x[:, 1, :], I["x_sample"][0], small_in)
            for l in range(DEPTH):
                for name in GAIN:
                    if name == "m0":
                        src = I["state_mlstm_m"][0:1, l, :, :].rearrange("a d h -> a (d h)")
                    else:
                        src = I[name][l:l + 1, :]
                    load(G(l, name), src.broadcast_to([128, src.shape[1]]))
                load(ctx_k[:, l, :], I["cache_swa_k"][0, l].rearrange("t g d -> t (g d)"))
                load(ctx_v[:, l, :], I["cache_swa_v"][0, l].rearrange("t g d -> t (g d)"))
                load(ctx_ckv[:, l, :], I["cache_mla_ckv"][0, l])
                load(ctx_kr[:, l, :], I["cache_mla_krope"][0, l])
                for par in range(2):
                    for d in range(2):
                        dst = C0n0[64 * par:64 * par + 64, l, d, :, :]
                        load(dst[:, :, 0:HD], I["state_mlstm_C"][0, l, d, par:B_H:2].rearrange("h k v -> k h v"))
                        load(dst[:, :, HD:HD + 1],
                             I["state_mlstm_n"][0, l, d, par:B_H:2].rearrange("h (k o) -> k h o", o=1),
                             allow_slow_non_contiguous=True)
                load(m0row[:, 1 + l:2 + l], I["state_mlstm_m"][0, l].rearrange("d (h o) -> (d h) o", o=1))
            load(router[:, :, :], I["moe_router"][0].rearrange("(k p) e -> p k e", p=128))
            for l in range(DEPTH):
                u = 2 * l

                def store(dst, src, s=out_sem[l], **how):
                    pool.dma_start(dst, src, **how).then_inc(s, 16)

                pool.wait_ge(Q["h_ready"], 10 * l + 9)
                store(O["new_swa_v"][0, l].rearrange("t g d -> t (g d)"), h[:, 0, AV:AV + 128])
                store(O["new_mla_krope"][0, l], h[:, 0, CKR:CKR + C_ROPE])
                pool.wait_ge(Q["qkA_ready"], u + 1)
                store(O["new_swa_k"][0, l].rearrange("t g d -> t (g d)"), ka_out[:, :])
                pool.wait_ge(Q["state_copied"], l + 1)
                st = R(0, ST, 8 * (HD + 1), 64).rearrange("p (c n) -> p c n", c=8)
                store(O["new_mlstm_C"][0, l].rearrange("d h k v -> k (d h) v"), st[:, :, 0:HD], state_out[l])
                store(O["new_mlstm_n"][0, l].rearrange("d h (k o) -> k (d h) o", o=1), st[:, :, HD:HD + 1], state_out[l],
                      allow_slow_non_contiguous=True)
                store(O["new_mlstm_m"][0:1, l].rearrange("a d h -> a (d h)"), c_(0, "mo")[0:1, :], state_out[l])
                pool.wait_ge(Q["cn_ready"], u + 1)
                store(O["new_mla_ckv"][0, l], ckv_out[:, :])
                if l == 0:
                    pool.wait_ge(Q["x_done"], 4)
                    load(R(0, 0, 6144, 2), I["ada_b"][1:2, :].broadcast_to([2, 6144]), adab_in[1])
            for s, name in ((0, "y_prompt"), (1, "y_sample")):
                pool.wait_ge(Q["x_done"], 7 + s)
                pool.dma_start(O[name][0], x[:, s, :]).then_inc(y_out, 16)

        @block.tensor
        def _(pe):
            mm, tr = nc.tensor.matmul, nc.tensor.transpose

            def wait(name, v):
                pe.wait_ge(Q[name], v)

            def weights(n):
                pe.wait_ge(slot_full[n % N_SLOT], 16 * (n // N_SLOT + 1))
                return loads[n][0]

            def T(out, src, last_of=None):
                k = src.shape[0]
                return tr(out, src, ident[0:k, 0:k])

            pe.wait_ge(first_in, 16 * N_FIRST)
            T(bank(0, 2 * KD), crow[:, :])
            T(bank(1, 4 * KD), ngrow[:, :]).then_inc(setup_T, 1)
            pe.wait_ge(c_ready, 1)
            pe.wait_ge(ng_ready, 1)

            def modulation(l):
                n_gate = [0]

                def rows_of(n):
                    if n >= 2:
                        wait("modrow_ready", 12 * l + n - 1)
                    for k in range(KD):
                        w = weights(first["ada", l] + 2 * n + k // 4)
                        last = mm(bank(n % 2, parts=2), cT[:, k:2 * KD:KD], w[:, k % 4, :], start=(k == 0), stop=(k == KD - 1))
                        if k % 4 == 3 and k < 7:
                            last.then_inc(slot_used, 1)
                    last.then_inc(slot_used, 1)

                def spread(n):
                    wait("modrow_ready", 12 * l + n + 1)
                    j, half = n // 2, n % 2
                    row = modrow[:, n % 2, :]
                    if j in (2, 5):
                        for s in range(2):
                            b = n_gate[0]
                            if b >= 2:
                                wait("gate_copied", 8 * l + b - 1)
                            mm(bank(3 + b % 2), PICK[0:2, s, :], row, start=True, stop=True).then_inc(Q["gate_bc"], 1)
                            n_gate[0] += 1
                    else:
                        jj = j if j < 2 else j - 1
                        for c in range(4):
                            a = 16 * jj + 2 * (4 * half + c)
                            last = T(bank(2, 2, a=a), row[:, 128 * c:128 * c + 128])
                        last.then_inc(Q["mod_T"], 1)

                for n in range(12):
                    rows_of(n)
                    if n:
                        spread(n - 1)
                spread(11)

            def norm_T(l, j, s):
                nu = 4 * l + 2 * j + s
                wait("xr_ready", nu + 1)
                for k in range(KD):
                    last = T(bank(4 * s + k // 4, 128, a=128 * (k % 4)), xr[:, s, 128 * k:128 * k + 128])
                last.then_inc(Q["xr_T"], 1)
                wait("xnT_a", nu + 1)
                wait("xnT_d", nu + 1)

            def in_proj(l):
                for n in range(5):
                    c = IN_CUTS[n + 1] - IN_CUTS[n]
                    for s in range(2):
                        i = 2 * n + s
                        if i >= 8:
                            wait("h_ready", 10 * l + i - 7)
                        for k in range(KD):
                            w = weights(first["in", l] + 2 * n + k // 4)
                            last = mm(bank(i % 8, c), xnT[:, k, 128 * s:128 * s + 128], w[:, k % 4, :],
                                      start=(k == 0), stop=(k == KD - 1))
                            if s == 1 and k == 3:
                                last.then_inc(slot_used, 1)
                        last.then_inc(Q["in_mm"] if s == 0 else slot_used, 1)

            def scores_softmax_out(l, s, X, qT, kT, v, n_kt):
                u = 2 * l + s
                b0 = 4 * s
                for hi in range(6):
                    for kt in range(n_kt):
                        a = (hi % 3 * n_kt + kt) * 128
                        last = mm(bank(b0 + hi // 3 * 2 + a // 512, 128, a=a % 512), qT(hi), kT(hi, kt),
                                  start=True, stop=True)
                last.then_inc(Q["S" + X], 1)
                yield
                wait("P" + X, u + 1)
                p = R(s, SQ, 6 * n_kt * 128)
                for i in range(6 * n_kt):
                    last = T(bank(b0 + i // 4, 128, a=128 * (i % 4)), p[:, 128 * i:128 * i + 128])
                last.then_inc(Q["PT" + X], 1)
                yield
                wait("PT" + X + "_a", u + 1)
                wait("PT" + X + "_d", u + 1)
                pT = R(s, QK, 6 * n_kt * 128)
                for hi in range(6):
                    for kt in range(n_kt):
                        i = hi * n_kt + kt
                        last = mm(bank(b0 + 3, HD, a=HD * hi), pT[:, 128 * i:128 * i + 128], v(hi, kt),
                                  start=(kt == 0), stop=(kt == n_kt - 1))
                last.then_inc(Q["O" + X], 1)
                yield

            def group_A(l, s):
                u = 2 * l + s
                wait("qkA_ready", u + 1)
                wait("h_ready", 10 * l + 10)
                qk = R(s, QK + 512 * s, 512)
                b0 = 4 * s
                for r in range(3):
                    T(bank(b0, 128, a=128 * r), qk[:, 128 * r:128 * r + 128])
                if s == 0:
                    last = T(bank(b0, 128, a=384), ka_out[:, :])
                else:
                    T(bank(b0, 128, a=384), qk[:, 384:512])
                    last = T(bank(b0 + 1, 128), ctx_k[:, l, :])
                last.then_inc(Q["TA"], 1)
                yield
                wait("TA_ready", u + 1)
                t = R(s, QKT, 640)

                def qT(hi):
                    g, r = hi // 3, hi % 3
                    return t[64 * g:64 * g + 64, 128 * r:128 * r + 128]

                def kT(hi, kt):
                    g = hi // 3
                    a = 384 if kt == 0 else 512
                    return t[64 * g:64 * g + 64, a:a + 128]

                def v(hi, kt):
                    g = hi // 3
                    return h[:, s, AV + 64 * g:AV + 64 * g + 64] if kt == 0 else ctx_v[:, l, 64 * g:64 * g + 64]

                yield from scores_softmax_out(l, s, "A", qT, kT, v, 1 + s)

            def group_B(l, s):
                u = 2 * l + s
                b0 = 4 * s
                wait("lf_ready", u + 1)
                wait("oA", u + 1)
                lf = c_(s, "lf")
                mm(bank(b0, 4), K("s_le_t"), lf[:, 0:4], start=True, stop=True)
                mm(bank(b0, 4, a=4), K("s_ge_t"), lf[:, 4:8], start=True, stop=True)
                for i in range(2):
                    T(bank(b0 + 1, 128, a=128 * i), h[:, s, BQ + 128 * i:BQ + 128 * i + 128])
                for i in range(2):
                    last = T(bank(b0 + 1, 128, a=256 + 128 * i), R(s, KS, 256)[:, 128 * i:128 * i + 128])
                last.then_inc(Q["bc_T"], 1)
                yield
                wait("u_ready", u + 1)
                T(bank(b0 + 2, 128, parts=8), c_(s, "u"))
                wait("qkB_T", u + 1)
                t = R(s, QKT, 512)

                def head(a, hh):
                    return t[64 * (hh % 2):64 * (hh % 2) + 64, a + 128 * (hh // 2):a + 128 * (hh // 2) + 128]

                for hh in range(B_H):
                    last = mm(bank(b0 + 3 * (hh % 2), 128, a=128 * (hh // 2)), head(256, hh), head(0, hh),
                              start=True, stop=True)
                last.then_inc(Q["uT_S"], 1)
                yield
                wait("run_ready", u + 1)
                run = MFB[:, s, :, :]
                for d in range(2):
                    mm(bank(b0, 4, a=256 + 4 * d), run[:, 1 + d, :], ident[0:8, 4 * d:4 * d + 4], start=True, stop=True)
                for c in range(8):
                    last = mm(bank(b0 + 1 + c // 4, 128, a=128 * (c % 4)), PICK[:, c, :], run[:, 1 + c // 4, :],
                              start=True, stop=True)
                last.then_inc(Q["M_mm"], 1)
                yield
                if s == 0:
                    wait("Earg_ready", u + 1)
                    m16 = c_(s, "m16").rearrange("p (a c) -> p a c", a=2)
                    out = bank(b0, 16, a=288).rearrange("p (a c) -> p a c", a=2)
                    mm(out[:, :, 0:4], K("row_last"), m16[:, :, 0:4], start=True, stop=True)
                    mm(out[:, :, 4:8], K("row_first"), m16[:, :, 4:8], start=True, stop=True).then_inc(Q["last_mm"], 1)
                yield
                wait("WT_ready", u + 1)
                v1 = R(s, V1, 4 * 65).rearrange("p (h n) -> p h n", h=4)
                wT = R(s, QK, 1024)
                for c in range(8):
                    last = mm(bank(b0 + 1 + c // 4, 65, a=65 * (c % 4)), wT[:, 128 * c:128 * c + 128], v1[:, c % 4, :],
                              start=True, stop=True)
                if s == 1:
                    for c in range(8):
                        hh, d = c % 4, c // 4
                        p0 = 64 * (hh % 2)
                        last = mm(bank(b0 + 3 * (hh % 2), 65, a=65 * (2 * d + hh // 2)), head(0, hh),
                                  C0n0[p0:p0 + 64, l, d, hh // 2, :], start=True, stop=True)
                else:
                    wait("kw_ready", l + 1)
                    kw = R(0, KW, 512)
                    for c in range(8):
                        last = mm(bank(b0 if c >= 4 else b0 + 3, 65, parts=64, a=65 * (c % 4)),
                                  kw[:, 64 * c:64 * c + 64], v1[:, c % 4, :], start=True, stop=True)
                last.then_inc(Q["num_mm"], 1)
                yield

            def group_C(l, s):
                u = 2 * l + s
                b0 = 4 * s
                wait("cn_ready", u + 1)
                wait("oB", u + 1)
                if s == 0:
                    wait("state_copied", l + 1)
                cn = R(s, VC, 384)
                T(bank(b0 + 3, 128), cn[:, 0:128])
                T(bank(b0 + 3, 128, a=128), cn[:, 128:256])
                if s == 0:
                    last = T(bank(b0 + 3, 128, a=256), ckv_out[:, :])
                else:
                    T(bank(b0 + 3, 128, a=256), cn[:, 256:384])
                    last = T(bank(b0 + 3, 128, a=384), ctx_ckv[:, l, :])
                last.then_inc(Q["TC"], 1)
                yield
                wait("TC_ready", u + 1)
                t = R(s, QKT, 512)
                uq, ukv = weights(first["uq", l]), weights(first["ukv", l])
                for n in range(2):
                    for k in range(2):
                        last = mm(bank(b0 + n, 288), t[:, 128 * k:128 * k + 128], uq[:, k, 288 * n:288 * n + 288],
                                  start=(k == 0), stop=(k == 1))
                if s == 1:
                    last.then_inc(slot_used, 1)
                for n in range(2):
                    last = mm(bank(b0 + 2 + n, 384), t[:, 256:384], ukv[:, 0, 384 * n:384 * n + 384], start=True, stop=True)
                last.then_inc(Q["C_mm"], 1)
                yield
                if s == 1:
                    wait("C_heads", u + 1)
                    for n in range(2):
                        last = mm(bank(b0 + 2 + n, 384), t[:, 384:512], ukv[:, 0, 384 * n:384 * n + 384],
                                  start=True, stop=True)
                    last.then_inc(slot_used, 1)
                yield
                wait("qkC_ready", u + 1)
                nh = 12 + 6 * s
                qk = R(s, QK, nh * 96).rearrange("p (h d) -> p h d", h=nh)
                for i in range(min(nh, 16)):
                    last = T(bank(b0 + i // 4, 128, 96, 128 * (i % 4)), qk[:, i, :])
                last.then_inc(Q["TC1"], 1)
                yield
                wait("TC1_a", u + 1)
                wait("TC1_d", u + 1)
                if s == 1:
                    for i in range(16, nh):
                        last = T(bank(b0, 128, 96, 128 * (i % 4)), qk[:, i, :])
                    last.then_inc(Q["TC2"], 1)
                    wait("TC2_a", l + 1)
                qkT = R(s, QKT, nh * 128, 96)

                def qT(hi):
                    return qkT[:, 128 * hi:128 * hi + 128]

                def kT(hi, kt):
                    return qkT[:, 128 * (6 + 6 * kt + hi):128 * (7 + 6 * kt + hi)]

                def v(hi, kt):
                    return R(s, VC + 384 * kt + 64 * hi, 64)

                yield from scores_softmax_out(l, s, "C", qT, kT, v, 1 + s)

            def both(group, l):
                a, b = group(l, 0), group(l, 1)
                for _ in a:
                    next(b)

            def out_proj(l):
                for s in range(2):
                    wait("oC", 2 * l + s + 1)
                    for k in range(KD):
                        last = T(bank(4 * s + k // 4, 128, a=128 * (k % 4)), o[:, s, 128 * k:128 * k + 128])
                    last.then_inc(Q["o_T"], 1)
                for n in range(2):
                    for s in range(2):
                        if n == 0:
                            wait("oT_a", 2 * l + s + 1)
                            wait("oT_d", 2 * l + s + 1)
                        t = R(s, QKT, 1024)
                        for k in range(KD):
                            w = weights(first["out", l] + 2 * n + k // 4)
                            last = mm(bank(4 * s + 2 + n), t[:, 128 * k:128 * k + 128], w[:, k % 4, :],
                                      start=(k == 0), stop=(k == KD - 1))
                            if s == 1 and k == 3:
                                last.then_inc(slot_used, 1)
                        last.then_inc(Q["out_mm"] if s == 0 else slot_used, 1)

            def dense_ffn():
                def up(t):
                    f, s = t // 2, t % 2
                    if t >= 2:
                        wait("hid_ready", t - 1)
                    for j, kind in enumerate(("w1", "w3")):
                        w = weights(first[kind, f])
                        for k in range(KD):
                            last = mm(bank(s, FF, a=FF * j), xnT[:, k, 128 * s:128 * s + 128], w[:, k, :],
                                      start=(k == 0), stop=(k == KD - 1))
                        if s == 1:
                            last.then_inc(slot_used, 1)
                    if s == 0:
                        last.then_inc(Q["up_mm"], 1)

                def turn(t):
                    wait("hid_ready", t + 1)
                    if t >= 2:
                        wait("hT_ready", t - 1)
                    for c in range(2):
                        last = T(bank(2 + t % 2, 128, a=128 * c), W[:, F_H + 512 * (t % 2) + 128 * c:F_H + 512 * (t % 2) + 128 * c + 128])
                    last.then_inc(Q["hid_T"], 1)

                def down(t):
                    f, s = t // 2, t % 2
                    wait("hT_ready", t + 1)
                    w = weights(first["w2", f])
                    for n in range(2):
                        for c in range(2):
                            last = mm(bank(4 + 2 * s + n), W[:, F_T + 512 * (t % 2) + 128 * c:F_T + 512 * (t % 2) + 128 * c + 128],
                                      w[:, c, 512 * n:512 * n + 512], start=(f == 0 and c == 0), stop=(f == N_FF - 1 and c == 1))
                    last.then_inc(Q["down_mm"] if s == 0 else slot_used, 1)

                steps = 2 * N_FF
                for t in range(steps + 2):
                    if t < steps:
                        up(t)
                    if 1 <= t <= steps:
                        turn(t - 1)
                    if t >= 2:
                        down(t - 2)

            def routing():
                for s in range(2):
                    for k in range(KD):
                        last = T(bank(4 * s + k // 4, 128, a=128 * (k % 4)), xnT[:, k, 128 * s:128 * s + 128])
                    last.then_inc(Q["xn_T"], 1)
                    for k in range(KD):
                        last = mm(bank(4 * s + 2, N_EXP), xnT[:, k, 128 * s:128 * s + 128], router[:, k, :],
                                  start=(k == 0), stop=(k == KD - 1))
                    last.then_inc(Q["logits_mm"], 1)
                wait("sel_ready", 2)
                sel = [c_(0, "sel"), c_(1, "sel")]
                mm(bank(3, 8), K("s_lt_t"), sel[0], start=True, stop=True)
                mm(bank(3, 8, a=8), K("s_lt_t"), sel[1], start=True, stop=False)
                mm(bank(3, 8, a=8), K("ones"), sel[0], start=False, stop=True)
                mm(bank(3, 8, a=16), K("ones"), sel[0], start=True, stop=False)
                mm(bank(3, 8, a=16), K("ones"), sel[1], start=False, stop=True).then_inc(Q["pos_mm"], 1)

            def experts():
                wait("pass_ready", 1)
                wait("xn_a", 2)
                wait("xn_d", 2)
                passes = pe.value_load(n_pass[0:1, 0:1], min_val=1, max_val=2)
                with pe.Fori(0, passes) as p:
                    with pe.Fori(0, N_EXP) as e:
                        it = p * N_EXP + e

                        def wait_it(name, per, v):
                            pe.wait_ge(Q[name], it * per + v)

                        def expert_weights(key, a):
                            n = W0 + expert_at[key]
                            pe.wait_ge(slot_full[n % N_SLOT], it * FULL_PER_EXPERT + 16 * (n // N_SLOT + 1))
                            return slot(n).rearrange("p (a c) -> p a c", a=a)

                        wait_it("P_ready", 1, 1)
                        for half in range(2):
                            for k in range(4):
                                for s in range(2):
                                    last = mm(bank(6 + half, 128, a=128 * k), xr[:, s, 512 * half + 128 * k:512 * half + 128 * k + 128],
                                              W[:, F_P + 128 * s:F_P + 128 * s + 128], start=(s == 0), stop=(s == 1))
                            last.then_inc(Q["gather_mm"], 1)
                        wait_it("acc_done", 4, 1)
                        for s in range(2):
                            last = T(bank(1, 128, a=128 * s), W[:, F_PG + 128 * s:F_PG + 128 * s + 128])
                        last.then_inc(Q["Pg_T"], 1)
                        xe = W[:, F_XE:F_XE + 1024].rearrange("p (k t) -> p k t", k=KD)

                        def up(kind, f):
                            b = 2 * (f % 2) + (kind == "w3")
                            if f >= 2:
                                wait_it("e_hid", N_FE, f - 1)
                            elif kind == "w3" and f == 0:
                                wait_it("Pg_a", 1, 1)
                            for half in range(2):
                                if f == 0 and kind == "w1":
                                    wait_it("xe_a" if half == 0 else "xe_d", 1, 1)
                                w = expert_weights((kind, f, half), 4)
                                for k in range(4):
                                    last = mm(bank(b), xe[:, 4 * half + k, :], w[:, k, :], start=(half == 0 and k == 0),
                                              stop=(half == 1 and k == 3))
                                last.then_inc(slot_used, 1)

                        def turn(f):
                            wait_it("e_hid", N_FE, f + 1)
                            if f >= 2:
                                wait_it("e_hT", N_FE, f - 1)
                            for c in range(4):
                                a = F_H + 512 * (f % 2) + 128 * c
                                last = T(bank(6 + f % 2, 128, a=128 * c), W[:, a:a + 128])
                            last.then_inc(Q["e_T"], 1)

                        def down(f):
                            wait_it("e_hT", N_FE, f + 1)
                            for half in range(2):
                                w = expert_weights(("w2", f, half), 2)
                                for n in range(2):
                                    for c in range(2):
                                        a = F_T + 512 * (f % 2) + 128 * (2 * half + c)
                                        last = mm(bank(4 + n), W[:, a:a + 128], w[:, c, 512 * n:512 * n + 512],
                                                  start=(f == 0 and half == 0 and c == 0),
                                                  stop=(f == N_FE - 1 and half == 1 and c == 1))
                                last.then_inc(slot_used, 1)

                        for f in range(N_FE):
                            up("w1", f)
                            if f:
                                turn(f - 1)
                            up("w3", f)
                            if f:
                                down(f - 1)
                        turn(N_FE - 1)
                        down(N_FE - 1)
                        wait_it("y_a", 1, 1)
                        wait_it("y_d", 1, 1)
                        for s in range(2):
                            for n in range(2):
                                mm(bank(2 * s + n), W[:, F_PT + 128 * s:F_PT + 128 * s + 128],
                                   W[:, F_Y + 512 * n:F_Y + 512 * n + 512], start=True, stop=True).then_inc(Q["scat_mm"], 1)

            for l in range(DEPTH):
                modulation(l)
                wait("mod_ready", l + 1)
                norm_T(l, 0, 0)
                norm_T(l, 0, 1)
                in_proj(l)
                both(group_A, l)
                both(group_B, l)
                both(group_C, l)
                out_proj(l)
                norm_T(l, 1, 0)
                norm_T(l, 1, 1)
                if l == 0:
                    dense_ffn()
                else:
                    routing()
                    experts()

        @block.scalar
        def _(act):
            A = nc.scalar.activation
            chain = [0]

            def wait(name, v):
                act.wait_ge(Q[name], v)

            def link(ins):
                chain[0] += 1
                ins.then_inc(act_chain, 1)
                act.wait_ge(act_chain, chain[0])

            act.wait_ge(setup_T, 1)
            A(cT[:, :], bank(0, 2 * KD), ACT.Silu).then_inc(c_ready, 1)
            act.wait_ge(small_in, 16 * N_SMALL)

            def norm(l, j, s):
                nu = 4 * l + 2 * j + s
                if nu >= 2:
                    wait("x_done", nu - 1)
                A(xr[:, s, :], x[:, s, :], ACT.Square, accum_out=c_(s, "ssq")).then_inc(Q["ssq_ready"], 1)

            def norm_out(l, j, s):
                nu = 4 * l + 2 * j + s
                wait("xr_T", nu + 1)
                wait("mod_ready", l + 1)
                for k in range(4):
                    last = A(xnT[:, k, 128 * s:128 * s + 128], bank(4 * s, 128, a=128 * k), ACT.Identity,
                             scale=modS[:, j, k, s:s + 1], bias=modT[:, 2 * j, k, s:s + 1])
                last.then_inc(Q["xnT_a"], 1)

            def in_proj(l):
                for n in range(5):
                    for s in range(2):
                        i = 2 * n + s
                        if s == 0:
                            wait("in_mm", 5 * l + n + 1)
                        else:
                            summed(act, first["in", l] + 2 * n + 1)
                        c0, c1 = IN_CUTS[n:n + 2]
                        A(h[:, s, c0:c1], bank(i % 8, c1 - c0), ACT.Copy).then_inc(Q["h_ready"], 1)

            def softmax(l, s, X, scale, n_kt):
                u = 2 * l + s
                wait("nm" + X, u + 1)
                p = R(s, SQ, 6 * n_kt * 128)
                w = 128 * n_kt
                for hi in range(6):
                    last = A(p[:, w * hi:w * hi + w], banks(4 * s + hi // 3 * 2, 3 * w)[:, w * (hi % 3):w * (hi % 3) + w], ACT.Exp,
                             bias=c_(s, "nm")[:, hi:hi + 1], scale=scale, accum_out=c_(s, "ls")[:, hi:hi + 1])
                if X == "A":
                    last = A(c_(s, "es"), c_(s, "es"), ACT.Exp)
                last.then_inc(Q["P" + X], 1)
                yield
                wait("PT" + X, u + 1)
                n = 512 * n_kt
                A(R(s, QK, n), banks(4 * s, n), ACT.Copy).then_inc(Q["PT" + X + "_a"], 1)
                yield

            def group_A(l, s):
                u = 2 * l + s
                wait("TA", u + 1)
                n = 512 + 128 * s
                A(R(s, QKT, n), banks(4 * s, n), ACT.Copy).then_inc(Q["TA_ready"], 1)
                yield
                yield from softmax(l, s, "A", HD ** -0.5, 1 + s)

            def group_B(l, s):
                u = 2 * l + s
                wait("absf_ready", u + 1)
                link(A(c_(s, "expl"), c_(s, "absf"), ACT.Exp, scale=-1.0))
                A(c_(s, "expl"), c_(s, "expl"), ACT.Ln, bias=1.0).then_inc(Q["log_ready"], 1)
                yield
                wait("bc_T", u + 1)
                A(R(s, QKT, 512), bank(4 * s + 1), ACT.Copy).then_inc(Q["qkB_T"], 1)
                yield
                wait("Earg_ready", u + 1)
                A(R(s, SQ, 1024), R(s, SQ, 1024), ACT.Exp, scale=-1.0)
                A(c_(s, "em"), c_(s, "em"), ACT.Exp, scale=-1.0)
                if s == 1:
                    A(c_(s, "a"), c_(s, "a"), ACT.Exp)
                A(R(s, SIG, 256), h[:, s, BO:BO + 256], ACT.Exp, scale=-1.0).then_inc(Q["E_ready"], 1)
                yield
                if s == 0:
                    wait("ws_arg", l + 1)
                    A(c_(0, "ws"), c_(0, "ws"), ACT.Exp).then_inc(Q["ws_ready"], 1)
                    wait("num_mm", u + 1)
                    st = R(0, ST, 520, 64)
                    A(st[:, 0:260], bank(3, 260, 64), ACT.Copy)
                    A(st[:, 260:520], bank(0, 260, 64), ACT.Copy).then_inc(Q["state_copied"], 1)
                yield

            def group_C(l, s):
                u = 2 * l + s
                b0 = 4 * s
                wait("TC", u + 1)
                A(R(s, QKT, 384 + 128 * s), bank(b0 + 3, 384 + 128 * s), ACT.Copy).then_inc(Q["TC_ready"], 1)
                yield
                wait("C_mm", u + 1)
                heads = R(s, QK, 18 * 96).rearrange("p (h d) -> p h d", h=18)

                def halves(b, n):
                    return PS[:, b:b + 2, 0:n]

                A(R(s, QK, 576).rearrange("p (a n) -> p a n", a=2), halves(b0, 288), ACT.Copy)

                def kv(set_):
                    src = halves(b0 + 2, 384).rearrange("p a (h d) -> p a h d", h=3)
                    dst = heads[:, 6 + 6 * set_:12 + 6 * set_, 0:C_NOPE].rearrange("p (a h) d -> p a h d", a=2)
                    A(dst, src[:, :, :, 0:C_NOPE], ACT.Copy)
                    dst = R(s, VC + 384 * set_, 384).rearrange("p (a h d) -> p a h d", a=2, h=3)
                    kr = h[:, s, CKR:CKR + C_ROPE] if set_ == 0 else ctx_kr[:, l, :]
                    A(heads[:, 6 + 6 * set_:12 + 6 * set_, C_NOPE:C_QK],
                      kr.unsqueeze(1).broadcast_to([128, 6, C_ROPE]), ACT.Copy)
                    return A(dst, src[:, :, :, C_NOPE:128], ACT.Copy)

                kv(0).then_inc(Q["C_heads"], 1)
                yield
                if s == 1:
                    summed(act, first["ukv", l])
                    kv(1).then_inc(Q["C_headsx"], 1)
                yield
                wait("TC1", u + 1)
                A(R(s, QKT, 1024, 96), banks(b0, 1024, 96), ACT.Copy).then_inc(Q["TC1_a"], 1)
                if s == 1:
                    wait("TC2", l + 1)
                    A(R(s, QKT + 2048, 256, 96), bank(b0, 256, 96), ACT.Copy).then_inc(Q["TC2_a"], 1)
                yield
                yield from softmax(l, s, "C", C_QK ** -0.5, 1 + s)

            def both(group, l):
                a, b = group(l, 0), group(l, 1)
                for _ in a:
                    next(b)

            def out_proj(l):
                for s in range(2):
                    wait("o_T", 2 * l + s + 1)
                    A(R(s, QKT, 512), bank(4 * s), ACT.Copy).then_inc(Q["oT_a"], 1)

            def dense_ffn():
                for t in range(2 * N_FF):
                    if t % 2 == 0:
                        wait("up_mm", t // 2 + 1)
                    else:
                        summed(act, first["w3", t // 2])
                    if t >= 2:
                        wait("hid_ready", t - 1)
                    A(W[:, F_H + 512 * (t % 2) + 256:F_H + 512 * (t % 2) + 512], bank(t % 2, FF), ACT.Silu)\
                        .then_inc(Q["silu_ready"], 1)
                    if t:
                        turned(t - 1)
                turned(2 * N_FF - 1)

            def turned(t):
                wait("hid_T", t + 1)
                if t >= 2:
                    if t % 2 == 0:
                        wait("down_mm", t // 2)
                    else:
                        summed(act, first["w2", t // 2 - 1])
                A(W[:, F_T + 512 * (t % 2):F_T + 512 * (t % 2) + 256], bank(2 + t % 2, 256), ACT.Copy)\
                    .then_inc(Q["hT_ready"], 1)

            def routing():
                for s in range(2):
                    wait("xn_T", s + 1)
                    A(xr[:, s, 0:512], bank(4 * s), ACT.Copy).then_inc(Q["xn_a"], 1)
                    wait("gap_ready", s + 1)
                    A(c_(s, "e2"), c_(s, "e2"), ACT.Exp).then_inc(Q["gap_exp"], 1)

            def experts():
                act.wait_ge(Q["pass_ready"], 1)
                passes = act.value_load(n_pass[0:1, 0:1], min_val=1, max_val=2)
                with act.Fori(0, passes) as p:
                    with act.Fori(0, N_EXP) as e:
                        it = p * N_EXP + e

                        def wait_it(name, per, v):
                            act.wait_ge(Q[name], it * per + v)

                        wait_it("gather_mm", 2, 1)
                        A(W[:, F_XE:F_XE + 512], bank(6), ACT.Copy).then_inc(Q["xe_a"], 1)
                        wait_it("Pg_T", 1, 1)
                        A(W[:, F_PT:F_PT + 256], bank(1, 256), ACT.Copy).then_inc(Q["Pg_a"], 1)

                        def silu(f):
                            summed(act, W0 + expert_at["w1", f, 1], it)
                            if f >= 2:
                                wait_it("e_T", N_FE, f - 1)
                            A(W[:, F_H + 512 * (f % 2):F_H + 512 * (f % 2) + 512], bank(2 * (f % 2)), ACT.Silu)\
                                .then_inc(Q["e_silu"], 1)

                        def turned(f):
                            wait_it("e_T", N_FE, f + 1)
                            if f >= 2:
                                summed(act, W0 + expert_at["w2", f - 2, 1], it)
                            A(W[:, F_T + 512 * (f % 2):F_T + 512 * (f % 2) + 512], bank(6 + f % 2), ACT.Copy)\
                                .then_inc(Q["e_hT"], 1)

                        for f in range(N_FE):
                            silu(f)
                            if f:
                                turned(f - 1)
                        turned(N_FE - 1)
                        summed(act, W0 + PER_EXPERT - 1, it)
                        A(W[:, F_Y:F_Y + 512], bank(4), ACT.Copy).then_inc(Q["y_a"], 1)

            for l in range(DEPTH):
                norm(l, 0, 0)
                norm(l, 0, 1)
                norm_out(l, 0, 0)
                norm_out(l, 0, 1)
                in_proj(l)
                both(group_A, l)
                both(group_B, l)
                both(group_C, l)
                out_proj(l)
                norm(l, 1, 0)
                norm(l, 1, 1)
                norm_out(l, 1, 0)
                norm_out(l, 1, 1)
                if l == 0:
                    dense_ffn()
                else:
                    routing()
                    experts()

        @block.vector
        def _(dve):
            v = nc.vector
            TT, TS, STT, RED = v.tensor_tensor, v.tensor_scalar, v.scalar_tensor_tensor, v.tensor_reduce
            chain = [0]

            def wait(name, n):
                dve.wait_ge(Q[name], n)

            def link(ins):
                chain[0] += 1
                ins.then_inc(dve_chain, 1)
                dve.wait_ge(dve_chain, chain[0])

            def rsqrt(s, n):
                y, t, w, bits = c_(s, "rs", n), c_(s, "tmp", n), c_(s, "var", n), c_(s, "bits", n).bitcast(i32)
                link(v.tensor_single_scalar(bits, w.bitcast(i32), 1, op=ALU.logical_shift_right))
                link(TS(y.bitcast(i32), bits, -1.0, float(0x5F3759DF), ALU.mult, ALU.add))
                for _ in range(3):
                    link(TT(t, y, y, ALU.mult))
                    link(STT(t, t, -0.5, w, ALU.mult, ALU.mult))
                    link(STT(y, t, 1.5, y, ALU.add, ALU.mult))
                return y

            v.memset(m0row[:, 0:1], 0.0).then_inc(zeros_ready, 1)
            dve.wait_ge(zeros_ready, 1)
            dve.wait_ge(setup_T, 1)
            v.tensor_copy(ngT[:, :], bank(1, 4 * KD)).then_inc(ng_ready, 1)
            dve.wait_ge(ng_ready, 1)
            dve.wait_ge(small_in, 16 * N_SMALL)

            def modulation(l):
                dve.wait_ge(adab_in[l], 16)
                b_ = [0]

                def copies(n):
                    j, half = n // 2, n % 2
                    if j not in (2, 5):
                        return
                    for s in range(2):
                        b = b_[0]
                        wait("gate_bc", 8 * l + b + 1)
                        v.tensor_copy(gate[:, s, j // 5, 512 * half:512 * half + 512], bank(3 + b % 2))\
                            .then_inc(Q["gate_copied"], 1)
                        b_[0] += 1

                def spread_done(n):
                    j = n // 2
                    if j in (2, 5):
                        return "gate_bc", 8 * l + 4 * (j // 5) + 2 * (n % 2) + 2
                    return "mod_T", 8 * l + [0, 2, None, 4, 6][j] + n % 2 + 1

                for n in range(12):
                    summed(dve, first["ada", l] + 2 * n + 1)
                    if n >= 2:
                        wait(*spread_done(n - 2))
                    TT(modrow[:, n % 2, :], bank(n % 2, parts=2), R(0, 512 * n, 512, 2), ALU.add)\
                        .then_inc(Q["modrow_ready"], 1)
                    if n:
                        copies(n - 1)
                copies(11)
                wait("mod_T", 8 * l + 8)
                link(v.tensor_copy(modT[:, :, :, :].rearrange("p j k s -> p (j k s)"), bank(2, 64)))
                for j in range(2):
                    g = ngT[:, 2 * KD * j + KD * l:2 * KD * j + KD * l + KD].unsqueeze(2).broadcast_to([128, KD, 2])
                    last = STT(modS[:, j, :, :], modT[:, 2 * j + 1, :, :], 1.0, g, ALU.add, ALU.mult)
                last.then_inc(Q["mod_ready"], 1)
                wait("mod_ready", l + 1)

            def norm(l, j, s):
                nu = 4 * l + 2 * j + s
                wait("ssq_ready", nu + 1)
                link(TS(c_(s, "var", 1), c_(s, "ssq"), 1.0 / D, EPS, ALU.mult, ALU.add))
                r = rsqrt(s, 1)
                TS(xr[:, s, :], x[:, s, :], r, None, ALU.mult).then_inc(Q["xr_ready"], 1)

            def norm_out(l, j, s):
                nu = 4 * l + 2 * j + s
                wait("xr_T", nu + 1)
                for k in range(4, KD):
                    last = TS(xnT[:, k, 128 * s:128 * s + 128], bank(4 * s + 1, 128, a=128 * (k - 4)),
                              modS[:, j, k, s:s + 1], modT[:, 2 * j, k, s:s + 1], ALU.mult, ALU.add)
                last.then_inc(Q["xnT_d"], 1)

            def rope(x_, out, cos, sin, n, half, tmp):
                x1, x2 = x_[:, :, 0:half], x_[:, :, half:2 * half]
                c = cos.unsqueeze(1).broadcast_to([128, n, half])
                s_ = sin.unsqueeze(1).broadcast_to([128, n, half])
                TT(tmp[0], x1, c, ALU.mult)
                TT(tmp[1], x2, s_, ALU.mult)
                TT(tmp[2], x1, s_, ALU.mult)
                link(TT(tmp[3], x2, c, ALU.mult))
                TT(out[:, :, 0:half], tmp[0], tmp[1], ALU.subtract)
                return TT(out[:, :, half:2 * half], tmp[2], tmp[3], ALU.add)

            def softmax(l, s, X, scale, n_kt):
                u = 2 * l + s
                w = 128 * n_kt
                wait("S" + X, u + 1)
                lots = banks(4 * s, 2048).rearrange("p (a n) -> p a n", a=2)[:, :, 0:3 * w]
                link(RED(c_(s, "mx").rearrange("p (a h) -> p a h", a=2), lots.rearrange("p a (h n) -> p a h n", h=3),
                         AX.X, ALU.max))
                if X == "A":
                    sink, mx = G(l, "a_sink"), c_(s, "mx")
                    link(STT(mx, mx, scale, sink, ALU.mult, ALU.max))
                    TT(c_(s, "es"), sink, mx, ALU.subtract)
                    TS(c_(s, "nm"), c_(s, "mx"), -1.0, None, ALU.mult).then_inc(Q["nm" + X], 1)
                else:
                    TS(c_(s, "nm"), c_(s, "mx"), -scale, None, ALU.mult).then_inc(Q["nm" + X], 1)
                yield
                wait("P" + X, u + 1)
                if X == "A":
                    link(TT(c_(s, "ls"), c_(s, "ls"), c_(s, "es"), ALU.add))
                link(v.reciprocal(c_(s, "rinv"), c_(s, "ls")))
                wait("PT" + X, u + 1)
                n, all_ = 512 * n_kt, 768 * n_kt
                v.tensor_copy(R(s, QK + n, all_ - n), banks(4 * s, all_)[:, n:all_]).then_inc(Q["PT" + X + "_d"], 1)
                yield
                wait("O" + X, u + 1)
                a = 0 if X == "A" else 640
                TT(o[:, s, a:a + 384].rearrange("p (h d) -> p h d", d=HD), bank(4 * s + 3, 384).rearrange("p (h d) -> p h d", d=HD),
                   c_(s, "rinv").unsqueeze(2).broadcast_to([128, 6, HD]), ALU.mult).then_inc(Q["o" + X], 1)
                yield

            def group_A(l, s):
                u = 2 * l + s
                wait("h_ready", 10 * l + 2 + s + 1)
                a8 = h[:, s, 0:512]
                link(TT(R(s, SQ, 512), a8, a8, ALU.mult))
                link(RED(c_(s, "tmp", 8), R(s, SQ, 512).rearrange("p (h d) -> p h d", h=8), AX.X, ALU.add))
                link(TS(c_(s, "var", 8), c_(s, "tmp", 8), 1.0 / HD, EPS, ALU.mult, ALU.add))
                r = rsqrt(s, 8)
                link(TT(R(s, SQ, 512).rearrange("p (h d) -> p h d", h=8), a8.rearrange("p (h d) -> p h d", h=8),
                        r.unsqueeze(2).broadcast_to([128, 8, HD]), ALU.mult))
                qg = G(l, "a_qn_g").unsqueeze(1).broadcast_to([128, 3, HD])
                kg = G(l, "a_kn_g").unsqueeze(1).broadcast_to([128, 2, HD])
                for g in range(2):
                    TT(R(s, QK, 384).rearrange("p (r g d) -> p r g d", g=2, d=HD)[:, :, g, :],
                       R(s, SQ + 192 * g, 192).rearrange("p (r d) -> p r d", d=HD), qg, ALU.mult)
                if s == 0 and l == 1:
                    dve.wait_ge(out_sem[0], 16 * 4)
                kdst = ka_out[:, :] if s == 0 else R(s, QK + 384, 128)
                last = TT(kdst.rearrange("p (g d) -> p g d", d=HD),
                          R(s, SQ + 384, 128).rearrange("p (g d) -> p g d", d=HD), kg, ALU.mult)
                if s == 1:
                    link(last)
                    last = rope(R(s, QK, 512).rearrange("p (h d) -> p h d", h=8),
                                R(s, QK + 512, 512).rearrange("p (h d) -> p h d", h=8), K("cosA"), K("sinA"), 8, 32,
                                [R(s, SQ + 256 * i, 256).rearrange("p (h d) -> p h d", h=8) for i in range(4)])
                last.then_inc(Q["qkA_ready"], 1)
                yield
                yield from softmax(l, s, "A", HD ** -0.5, 1 + s)

            def group_B(l, s):
                u = 2 * l + s
                g16 = c_(s, "g16")
                wait("h_ready", 10 * l + 6 + s + 1)
                wait("oA", u + 1)
                link(TT(g16, h[:, s, BG:BG + 16], G(l, "b_gate_b"), ALU.add))
                gates = g16.rearrange("p (d k h) -> p d k h", d=2, k=2)
                li, fg = gates[:, :, 0, :], gates[:, :, 1, :]

                def two(name):
                    return c_(s, name).rearrange("p (d h) -> p d h", d=2)

                STT(two("absf"), fg, -1.0, fg, ALU.mult, ALU.max).then_inc(Q["absf_ready"], 1)
                TS(R(s, KS, 256), h[:, s, BK:BK + 256], HD ** -0.5, None, ALU.mult)
                v1 = R(s, V1, 4 * 65).rearrange("p (h n) -> p h n", h=4)
                v.memset(v1[:, :, HD:HD + 1], 1.0)
                v.tensor_copy(v1[:, :, 0:HD], h[:, s, BV:BV + 256].rearrange("p (h d) -> p h d", h=4))
                wait("log_ready", u + 1)
                STT(two("lf"), fg, 0.0, two("expl"), ALU.min, ALU.subtract).then_inc(Q["lf_ready"], 1)
                yield
                wait("bc_T", u + 1)
                m16 = c_(s, "m16")
                v.tensor_copy(m16[:, 8:16], bank(4 * s, 8))
                TT(two("u"), li, bank(4 * s, 8).rearrange("p (d h) -> p d h", d=2), ALU.subtract).then_inc(Q["u_ready"], 1)
                yield
                wait("uT_S", u + 1)
                run = MFB[:, s, :, :]
                link(v.tensor_copy(run[:, 0, :], bank(4 * s + 2, 128, 8)))
                m0 = m0row[:, (1 + l) * s:(1 + l) * s + 1]
                v.tensor_tensor_scan(run[:, 1, :], run[:, 0, :], run[:, 0, :], m0, ALU.max, ALU.max)
                v.tensor_tensor_scan(run[:, 2, ::-1], run[:, 0, ::-1], run[:, 0, ::-1], m0, ALU.max, ALU.max)\
                    .then_inc(Q["run_ready"], 1)
                yield
                wait("M_mm", u + 1)
                link(v.tensor_copy(m16[:, 0:8], bank(4 * s, 8, a=256)))
                if s == 1:
                    TT(c_(s, "a"), G(l, "m0"), m16[:, 0:8], ALU.subtract)
                TT(c_(s, "em"), m16[:, 0:8], m16[:, 8:16], ALU.add)
                mask = K("mask").rearrange("p (d t) -> p d t", d=2)
                for c in range(8):
                    last = STT(R(s, SQ + 128 * c, 128), bank(4 * s + 1 + c // 4, 128, a=128 * (c % 4)),
                               c_(s, "u")[:, c:c + 1], mask[:, c // 4, :], ALU.subtract, ALU.add)
                last.then_inc(Q["Earg_ready"], 1)
                if s == 0:
                    wait("last_mm", l + 1)
                    TT(c_(0, "ws"), c_(0, "u"), bank(0, 8, a=288), ALU.subtract).then_inc(Q["ws_arg"], 1)
                    tot = c_(0, "mo")
                    link(v.tensor_copy(tot, bank(0, 8, a=296)))
                    TT(tot, tot, bank(0, 8, a=288), ALU.add)
                yield
                wait("E_ready", u + 1)
                for par in range(2):
                    def heads_of(a):
                        return R(s, a, 1024).rearrange("p (d a b t) -> p d a b t", d=2, a=2, b=2)[:, :, :, par, :]

                    sT = bank(4 * s + 3 * par, 256).rearrange("p (a t) -> p a t", a=2)
                    last = TT(heads_of(QK), heads_of(SQ), sT.unsqueeze(1).broadcast_to([128, 2, 2, 128]), ALU.mult)
                last.then_inc(Q["WT_ready"], 1)
                if s == 0:
                    wait("ws_ready", l + 1)
                    for d in range(2):
                        last = TT(R(0, KW + 256 * d, 256).rearrange("p (h d) -> p h d", h=4),
                                  R(0, KS, 256).rearrange("p (h d) -> p h d", h=4),
                                  c_(0, "ws")[:, 4 * d:4 * d + 4].unsqueeze(2).broadcast_to([128, 4, HD]), ALU.mult)
                    last.then_inc(Q["kw_ready"], 1)
                yield
                wait("num_mm", u + 1)
                num = R(s, NUM, 520).rearrange("p (c n) -> p c n", c=8)

                def four(b):
                    return bank(b, 260).rearrange("p (c n) -> p c n", c=4)

                for d in range(2):
                    if s == 0:
                        last = v.tensor_copy(num[:, 4 * d:4 * d + 4, :], four(4 * s + 1 + d))
                    else:
                        if d == 0:
                            for par in range(2):
                                last = TT(num.rearrange("p (a b) n -> p a b n", b=2)[:, :, par, :], four(4 * s + 3 * par),
                                          c_(s, "a").rearrange("p (a b) -> p a b", b=2)[:, :, par].unsqueeze(2)
                                          .broadcast_to([128, 4, HD + 1]), ALU.mult)
                            link(last)
                        last = TT(num[:, 4 * d:4 * d + 4, :], num[:, 4 * d:4 * d + 4, :], four(4 * s + 1 + d), ALU.add)
                link(last)
                den, t8, r8 = num[:, :, HD], c_(s, "tmp", 8), c_(s, "rs", 8)
                link(STT(t8, den, -1.0, den, ALU.mult, ALU.max))
                link(TT(t8, t8, c_(s, "em"), ALU.max))
                link(v.reciprocal(r8, t8))
                h8 = R(s, H8, 512)
                link(TT(h8.rearrange("p (c d) -> p c d", c=8), num[:, :, 0:HD],
                        r8.unsqueeze(2).broadcast_to([128, 8, HD]), ALU.mult))
                hs = R(s, H8 + 512, 256)
                link(TT(hs, h8[:, 0:256], h8[:, 256:512], ALU.add))
                link(TT(R(s, BSQ, 256), hs, hs, ALU.mult))
                link(RED(t8[:, 0:4], R(s, BSQ, 256).rearrange("p (h d) -> p h d", h=4), AX.X, ALU.add))
                link(TS(c_(s, "var", 4), t8[:, 0:4], 1.0 / HD, EPS, ALU.mult, ALU.add))
                r4 = rsqrt(s, 4)
                sig = R(s, SIG, 256)
                link(TS(sig, sig, 1.0, None, ALU.add))
                link(v.reciprocal(sig, sig))
                hs4 = hs.rearrange("p (h d) -> p h d", h=4)
                link(TT(hs4, hs4, r4.unsqueeze(2).broadcast_to([128, 4, HD]), ALU.mult))
                link(TT(hs4, hs4, G(l, "b_hn_g").unsqueeze(1).broadcast_to([128, 4, HD]), ALU.mult))
                TT(o[:, s, 384:640], hs, sig, ALU.mult).then_inc(Q["oB"], 1)
                yield

            def group_C(l, s):
                u = 2 * l + s
                wait("h_ready", 10 * l + 8 + s + 1)
                wait("oB", u + 1)
                lat = h[:, s, CQ:CQ + 384]
                link(TT(R(s, SQ, 384), lat, lat, ALU.mult))
                RED(c_(s, "tmp")[:, 0:1], R(s, SQ, 256), AX.X, ALU.add)
                link(RED(c_(s, "tmp")[:, 1:2], R(s, SQ + 256, 128), AX.X, ALU.add))
                TS(c_(s, "var")[:, 0:1], c_(s, "tmp")[:, 0:1], 1.0 / C_QR, EPS, ALU.mult, ALU.add)
                link(TS(c_(s, "var")[:, 1:2], c_(s, "tmp")[:, 1:2], 1.0 / C_KVR, EPS, ALU.mult, ALU.add))
                r = rsqrt(s, 2)
                STT(R(s, VC, 256), lat[:, 0:256], r[:, 0:1], G(l, "c_qa_g"), ALU.mult, ALU.mult)
                STT(ckv_out[:, :] if s == 0 else R(s, VC + 256, 128), lat[:, 256:384], r[:, 1:2], G(l, "c_kva_g"),
                    ALU.mult, ALU.mult).then_inc(Q["cn_ready"], 1)
                yield
                yield
                wait("C_heads", u + 1)
                if s == 1:
                    wait("C_headsx", l + 1)
                if s == 0:
                    dve.wait_ge(state_out[l], 16 * 3)
                nh = 12 + 6 * s
                qk = R(s, QK, nh * 96).rearrange("p (h d) -> p h d", h=nh)
                sq = R(s, SQ, nh * 96).rearrange("p (h d) -> p h d", h=nh)
                link(TT(sq, qk, qk, ALU.mult))
                link(RED(c_(s, "tmp", nh), sq, AX.X, ALU.add))
                link(TS(c_(s, "var", nh), c_(s, "tmp", nh), 1.0 / C_QK, EPS, ALU.mult, ALU.add))
                r = rsqrt(s, nh)
                link(TT(qk, qk, r.unsqueeze(2).broadcast_to([128, nh, C_QK]), ALU.mult))
                TT(qk[:, 0:6, :], qk[:, 0:6, :], G(l, "c_qn_g").unsqueeze(1).broadcast_to([128, 6, C_QK]), ALU.mult)
                last = TT(qk[:, 6:nh, :], qk[:, 6:nh, :], G(l, "c_kn_g").unsqueeze(1).broadcast_to([128, nh - 6, C_QK]),
                          ALU.mult)
                if s == 1:
                    link(last)
                    tail = qk[:, 0:12, C_NOPE:C_QK]
                    last = rope(tail, tail, K("cosC"), K("sinC"), 12, 16,
                                [R(s, SQ + 192 * i, 192).rearrange("p (h d) -> p h d", h=12) for i in range(4)])
                last.then_inc(Q["qkC_ready"], 1)
                yield
                wait("TC1", u + 1)
                n = 128 * min(nh, 16)
                v.tensor_copy(R(s, QKT + 1024, n - 1024, 96), banks(4 * s, n, 96)[:, 1024:n]).then_inc(Q["TC1_d"], 1)
                yield
                yield from softmax(l, s, "C", C_QK ** -0.5, 1 + s)

            def both(group, l):
                a, b = group(l, 0), group(l, 1)
                for _ in a:
                    next(b)

            def residual(l, j, s, n, src, tmp):
                xs = x[:, s, 512 * n:512 * n + 512]
                link(TT(tmp, src, gate[:, s, j, 512 * n:512 * n + 512], ALU.mult))
                last = TT(xs, xs, tmp, ALU.add)
                if n == 1:
                    last.then_inc(Q["x_done"], 1)
                    wait("x_done", 4 * l + 2 * j + s + 1)
                else:
                    link(last)

            def out_proj(l):
                for s in range(2):
                    wait("o_T", 2 * l + s + 1)
                    v.tensor_copy(R(s, QKT + 512, 512), bank(4 * s + 1)).then_inc(Q["oT_d"], 1)
                for n in range(2):
                    for s in range(2):
                        if s == 0:
                            wait("out_mm", 2 * l + n + 1)
                        else:
                            summed(dve, first["out", l] + 2 * n + 1)
                        residual(l, 0, s, n, bank(4 * s + 2 + n), R(s, SQ, 512))

            def dense_ffn():
                for t in range(2 * N_FF):
                    wait("silu_ready", t + 1)
                    if t >= 2:
                        wait("hid_T", t - 1)
                    a = F_H + 512 * (t % 2)
                    TT(W[:, a:a + 256], W[:, a + 256:a + 512], bank(t % 2, FF, a=FF), ALU.mult).then_inc(Q["hid_ready"], 1)
                summed(dve, first["w2", N_FF - 1])
                for s in range(2):
                    for n in range(2):
                        residual(0, 1, s, n, bank(4 + 2 * s + n), W[:, F_ACC:F_ACC + 512])

            def routing():
                for s in range(2):
                    wait("xn_T", s + 1)
                    v.tensor_copy(xr[:, s, 512:1024], bank(4 * s + 1)).then_inc(Q["xn_d"], 1)
                    wait("logits_mm", s + 1)
                    lg, v8, i8, idx = c_(s, "lg"), c_(s, "v8"), c_(s, "i8").bitcast(u32), c_(s, "if")
                    link(v.tensor_copy(lg, bank(4 * s + 2, 8)))
                    link(v.max(v8, lg))
                    link(v.max_index(i8, v8, lg))
                    v.tensor_copy(idx, i8[:, 0:2])
                    TT(c_(s, "e2"), v8[:, 1:2], v8[:, 0:1], ALU.subtract).then_inc(Q["gap_ready"], 1)
                    wait("gap_exp", s + 1)
                    link(TS(c_(s, "w1"), c_(s, "e2"), 1.0, None, ALU.add))
                    link(v.reciprocal(c_(s, "w1"), c_(s, "w1")))
                    link(TT(c_(s, "w2"), c_(s, "w1"), c_(s, "e2"), ALU.mult))
                    i1, i2 = idx[:, 0:1], idx[:, 1:2]
                    TS(c_(s, "eq"), K("iota8"), i2, None, ALU.is_equal)
                    TS(c_(s, "gt"), K("iota8"), i1, c_(s, "w1"), ALU.is_equal, ALU.mult)
                    link(TS(c_(s, "sel"), K("iota8"), i1, None, ALU.is_equal))
                    STT(c_(s, "gt"), c_(s, "eq"), c_(s, "w2"), c_(s, "gt"), ALU.mult, ALU.add)
                    TT(c_(s, "sel"), c_(s, "sel"), c_(s, "eq"), ALU.add).then_inc(Q["sel_ready"], 1)
                wait("sel_ready", 2)
                wait("pos_mm", 1)
                for s in range(2):
                    link(STT(c_(s, "posm"), bank(3, 8, a=8 * s), 1.0, c_(s, "sel"), ALU.add, ALU.mult))
                    link(TS(c_(s, "posm"), c_(s, "posm"), -1.0, None, ALU.add))
                link(RED(c_(0, "cnt"), bank(3, 8, a=16), AX.X, ALU.max))
                link(TS(c_(0, "cnt"), c_(0, "cnt"), float(TOK), 1.0, ALU.is_gt, ALU.add))
                v.tensor_copy(n_pass[:, :], c_(0, "cnt")).then_inc(Q["pass_ready"], 1)

            def experts():
                v.memset(W[:, F_ACC:F_ACC + 2048], 0.0).then_inc(Q["acc_done"], 1)
                wait("pass_ready", 1)
                passes = dve.value_load(n_pass[0:1, 0:1], min_val=1, max_val=2)
                with dve.Fori(0, passes) as p:
                    with dve.Fori(0, N_EXP) as e:
                        it = p * N_EXP + e

                        def wait_it(name, per, n):
                            dve.wait_ge(Q[name], it * per + n)

                        for s in range(2):
                            pos = c_(s, "posm")[:, bass.ds(e, 1)]
                            TS(W[:, F_P + 128 * s:F_P + 128 * s + 128], K("iota"), pos, None, ALU.is_equal)
                            last = TS(W[:, F_PG + 128 * s:F_PG + 128 * s + 128], K("iota"), pos,
                                      c_(s, "gt")[:, bass.ds(e, 1)], ALU.is_equal, ALU.mult)
                        last.then_inc(Q["P_ready"], 1)
                        wait_it("gather_mm", 2, 2)
                        v.tensor_copy(W[:, F_XE + 512:F_XE + 1024], bank(7)).then_inc(Q["xe_d"], 1)
                        for f in range(N_FE):
                            wait_it("e_silu", N_FE, f + 1)
                            summed(dve, W0 + expert_at["w3", f, 1], it)
                            a = F_H + 512 * (f % 2)
                            TT(W[:, a:a + 512], W[:, a:a + 512], bank(2 * (f % 2) + 1), ALU.mult).then_inc(Q["e_hid"], 1)
                        summed(dve, W0 + PER_EXPERT - 1, it)
                        v.tensor_copy(W[:, F_Y + 512:F_Y + 1024], bank(5)).then_inc(Q["y_d"], 1)
                        wait_it("acc_done", 4, 1)
                        for i in range(4):
                            wait_it("scat_mm", 4, i + 1)
                            acc = W[:, F_ACC + 512 * i:F_ACC + 512 * i + 512]
                            TT(acc, acc, bank(i), ALU.add).then_inc(Q["acc_done"], 1)
                    v.tensor_scalar(K("iota"), K("iota"), float(TOK), None, ALU.add).then_inc(Q["places_moved"], 1)
                    dve.wait_ge(Q["places_moved"], p + 1)
                for s in range(2):
                    for n in range(2):
                        a = F_ACC + 1024 * s + 512 * n
                        residual(1, 1, s, n, W[:, a:a + 512], W[:, 0:512])

            for l in range(DEPTH):
                modulation(l)
                norm(l, 0, 0)
                norm(l, 0, 1)
                norm_out(l, 0, 0)
                norm_out(l, 0, 1)
                both(group_A, l)
                both(group_B, l)
                both(group_C, l)
                out_proj(l)
                norm(l, 1, 0)
                norm(l, 1, 1)
                norm_out(l, 1, 0)
                norm_out(l, 1, 1)
                if l == 0:
                    dense_ffn()
                else:
                    routing()
                    experts()


INPUTS = ['x_prompt', 'x_sample', 'c', 'cache_swa_k', 'cache_swa_v', 'cache_mla_ckv', 'cache_mla_krope',
          'state_mlstm_C', 'state_mlstm_n', 'state_mlstm_m', 'c_ctx', 'ada_w', 'ada_b', 'norm1_g', 'norm2_g', 'w_in',
          'a_qn_g', 'a_kn_g', 'a_sink', 'b_gate_b', 'b_hn_g', 'c_qa_g', 'c_kva_g', 'c_wuq', 'c_wukv', 'c_qn_g',
          'c_kn_g', 'w_out', 'ffn_w1', 'ffn_w3', 'ffn_w2', 'moe_router', 'moe_w1', 'moe_w3', 'moe_w2']
OUTPUTS = [("y_prompt", (1, TOK, D)), ("y_sample", (1, TOK, D)),
           ("new_swa_k", (1, DEPTH, TOK, A_KV, HD)), ("new_swa_v", (1, DEPTH, TOK, A_KV, HD)),
           ("new_mla_ckv", (1, DEPTH, TOK, C_KVR)), ("new_mla_krope", (1, DEPTH, TOK, C_ROPE)),
           ("new_mlstm_C", (1, DEPTH, 2, B_H, HD, HD)), ("new_mlstm_n", (1, DEPTH, 2, B_H, HD)),
           ("new_mlstm_m", (1, DEPTH, 2, B_H))]


def kernel(**inputs):
    import concourse.bacc as bacc
    from concourse.bass_utils import run_bass_kernel_spmd

    nc = bacc.Bacc("TRN2", target_bir_lowering=False, num_devices=1)
    arrays = {f"in_{n}": np.ascontiguousarray(inputs[n]) for n in INPUTS}
    arrays["in_consts"] = constants()
    ins = {n[3:]: nc.dram_tensor(n, a.shape, mybir.dt.from_np(a.dtype), kind="ExternalInput").ap()
           for n, a in arrays.items()}
    outs = {n: nc.dram_tensor(f"out_{n}", shape, mybir.dt.float32, kind="ExternalOutput").ap() for n, shape in OUTPUTS}
    build_program(nc, ins, outs)
    r = run_bass_kernel_spmd(nc, [arrays], core_ids=[0])
    return tuple(r.results[0][f"out_{n}"] for n, _ in OUTPUTS)
```

```python
import concourse.bass as bass
from concourse import mybir
from contextlib import ExitStack
import numpy as np

D = 1024
TOK = 128
DEPTH = 2
KD = D // 128
HD = 64
A_H, A_KV, A_G = 6, 2, 3
B_H = 4
C_H, C_NOPE, C_ROPE, C_V = 6, 64, 32, 64
C_QK = C_NOPE + C_ROPE
C_QR, C_KVR = 256, 128
SIZES = (A_H * HD, A_KV * HD, A_KV * HD, 256, 256, 256, 256, 4 * B_H, C_QR, C_KVR, C_ROPE)
(AQ, AK, AV, BQ, BK, BV, BO, BG, CQ, CKV, CKR), D_IN = [sum(SIZES[:i]) for i in range(11)], sum(SIZES)
D_FF, N_EXP, D_FFE = 2816, 8, 3584
EPS = 1e-6
GRID_W, THETA, BIG = 64, 10000.0, 1e30

IN_CUTS = [0, 420, 840, 1260, 1680, D_IN]
FF = 256
N_FF = D_FF // FF
FE = 512
N_FE = D_FFE // FE
SLOT, N_SLOT = 2048, 7
PER_EXPERT = 6 * N_FE

CONST = {}
_at = 0
for _n, _w in (("ident", 128), ("s_le_t", 128), ("s_ge_t", 128), ("s_lt_t", 128), ("ones", 128), ("row_last", 128),
               ("row_first", 128), ("iota", 128), ("mask", 256), ("pick", 1024), ("cosA", 32), ("sinA", 32),
               ("cosC", 16), ("sinC", 16), ("iota8", 8)):
    CONST[_n] = (_at, _at + _w)
    _at += _w
N_CONST = _at

GAIN = {}
_at = 0
for _n, _w in (("a_qn_g", 64), ("a_kn_g", 64), ("c_qa_g", 256), ("c_kva_g", 128), ("c_qn_g", 96), ("c_kn_g", 96),
               ("b_hn_g", 64), ("b_gate_b", 16), ("a_sink", 6), ("m0", 8)):
    GAIN[_n] = (_at, _at + _w)
    _at += _w
N_GAIN = _at


def constants():
    t = np.zeros((128, N_CONST), np.float32)
    i = np.arange(128)

    def put(name, what):
        t[:what.shape[0], CONST[name][0]:CONST[name][1]] = what

    put("ident", np.eye(128))
    put("s_le_t", i[:, None] <= i[None, :])
    put("s_ge_t", i[:, None] >= i[None, :])
    put("s_lt_t", i[:, None] < i[None, :])
    put("ones", np.ones((128, 128)))
    put("row_last", np.repeat((i == 127)[:, None], 128, 1))
    put("row_first", np.repeat((i == 0)[:, None], 128, 1))
    put("iota", np.repeat(i[None, :], 128, 0))
    put("mask", BIG * np.concatenate([i[:, None] > i[None, :], i[:, None] < i[None, :]], 1))
    put("pick", np.repeat(np.eye(8)[:, :, None], 128, 2).reshape(8, 1024))
    put("iota8", np.repeat(np.arange(8)[None, :], 128, 0))
    for name, dim in (("A", HD), ("C", C_ROPE)):
        n = dim // 4
        freq = (np.float32(THETA) ** (-np.arange(n, dtype=np.float32) / np.float32(n))).astype(np.float32)
        row, col = (i // GRID_W).astype(np.float32), (i % GRID_W).astype(np.float32)
        ang = np.concatenate([row[:, None] * freq, col[:, None] * freq], 1).astype(np.float32)
        put("cos" + name, np.cos(ang))
        put("sin" + name, np.sin(ang))
    return t


def build_program(nc, I, O):
    f32, i32, u32, f32r = mybir.dt.float32, mybir.dt.int32, mybir.dt.uint32, mybir.dt.float32r
    ALU, ACT, AX = mybir.AluOpType, mybir.ActivationFunctionType, mybir.AxisListType
    ctx = ExitStack()
    with ctx:
        def sb(name, shape, dt=f32):
            return ctx.enter_context(nc.sbuf_tensor(name, shape, dt))

        def sem(name):
            return ctx.enter_context(nc.semaphore(name))

        ring = sb("ring", [128, N_SLOT, SLOT])
        x = sb("x", [128, 2, D])
        xr = sb("xr", [128, 2, D])
        xnT = sb("xnT", [128, KD, 2 * TOK])
        o = sb("o", [128, 2, D])
        cst = sb("cst", [128, N_CONST])
        gain = sb("gain", [128, DEPTH, N_GAIN])
        ctx_k = sb("ctx_k", [128, DEPTH, 128])
        ctx_v = sb("ctx_v", [128, DEPTH, 128])
        ctx_ckv = sb("ctx_ckv", [128, DEPTH, 128])
        ctx_kr = sb("ctx_kr", [128, DEPTH, C_ROPE])
        C0n0 = sb("C0n0", [128, DEPTH, 2, 2, HD + 1])
        m0row = sb("m0row", [8, 1 + DEPTH])
        gate = sb("gate", [128, 2, 2, D])
        modT = sb("modT", [128, 4, KD, 2])
        modS = sb("modS", [128, 2, KD, 2])
        modrow = sb("modrow", [2, 2, 512])
        crow = sb("crow", [2 * KD, 128])
        cT = sb("cT", [128, 2 * KD])
        ngrow = sb("ngrow", [4 * KD, 128])
        ngT = sb("ngT", [128, 4 * KD])
        router = sb("router", [128, KD, N_EXP])
        SCR = 6912
        arena = sb("arena", [128, 2 * D_IN + 2 * SCR])
        h = arena[:, 0:2 * D_IN].rearrange("p (s c) -> p s c", s=2)
        scr = arena[:, 2 * D_IN:2 * D_IN + 2 * SCR].rearrange("p (s c) -> p s c", s=2)
        N_HI, N_PARTS = 3, 8 * SLOT
        parts = nc.alloc_sbuf_tensor_at("parts", [128, N_PARTS], f32r, offset=nc.lookup_mloc(arena).addr)
        places = arena[:, N_PARTS:N_PARTS + 6 * TOK].rearrange("p (a s t) -> p a s t", a=3, s=2)
        small = sb("small", [128, 2, 320])
        ka_out = sb("ka_out", [128, 128])
        ckv_out = sb("ckv_out", [128, 128])
        n_pass = sb("n_pass", [128, 1], i32)
        PS = ctx.enter_context(nc.psum_tensor("PS", [128, 8, 512], f32))

        def K(name, rows=128):
            return cst[0:rows, CONST[name][0]:CONST[name][1]]

        def G(l, name):
            return gain[:, l, GAIN[name][0]:GAIN[name][1]]

        def R(s, a, n, parts=128):
            return scr[0:parts, s, a:a + n]

        def SM(s, a, n, parts=128):
            return small[0:parts, s, a:a + n]

        def bank(b, n=512, parts=128, a=0):
            return PS[0:parts, b, a:a + n]

        def banks(b, n, parts=128):
            return PS[0:parts, :, :].rearrange("p b n -> p (b n)")[:, b * 512:b * 512 + n]

        ident = K("ident")
        PICK = K("pick", 8).rearrange("p (c t) -> p c t", c=8)

        SQ, QK, QKT, VC = 0, 1728, 3456, 5760
        V1, KW, KS, NUM, H8 = QKT + 512, QKT + 772, QKT + 1284, QKT + 1540, VC
        SIG, BSQ = QK + 1024, QK + 1280
        ST = 1024
        xn_flat = xnT[:, :, :].rearrange("p k t -> p (k t)")
        hid = [xn_flat[:, 0:512], xn_flat[:, 512:1024]]
        y_e = xn_flat[:, 1024:2048]
        acc = o[:, :, :].rearrange("p s (n c) -> p (s n) c", c=512)
        P, PG, PGT = places[:, 0], places[:, 1], places[:, 2]

        def w_hi(i):
            return parts[:, SLOT * (i % N_HI):SLOT * (i % N_HI) + SLOT]

        def w_lo(i, n_lo):
            a = SLOT * (N_HI + i % n_lo)
            return parts[:, a:a + SLOT]

        a_hi = parts[:, 5 * SLOT:6 * SLOT].rearrange("p (k t) -> p k t", k=KD)
        a_lo = parts[:, 6 * SLOT:7 * SLOT].rearrange("p (k t) -> p k t", k=KD)
        xe_hi = parts[:, 6 * SLOT:6 * SLOT + 1024].rearrange("p (k t) -> p k t", k=KD)
        xe_lo = parts[:, 6 * SLOT + 1024:7 * SLOT].rearrange("p (k t) -> p k t", k=KD)
        t_hi = parts[:, 7 * SLOT:7 * SLOT + 1024].rearrange("p (b c) -> p b c", b=2)
        t_lo = parts[:, 7 * SLOT + 1024:8 * SLOT].rearrange("p (b c) -> p b c", b=2)

        cols = {}
        at = 0
        for name, w in (("var", 18), ("rs", 18), ("tmp", 18), ("bits", 18), ("mx", 6), ("nm", 6), ("ls", 6), ("es", 6),
                        ("g16", 16), ("absf", 8), ("expl", 8), ("lf", 8), ("m16", 16), ("u", 8), ("em", 8), ("a", 8),
                        ("mo", 8), ("ws", 8), ("lg", 8), ("v8", 8), ("i8", 8), ("if", 2), ("sel", 8), ("gt", 8),
                        ("eq", 8), ("posm", 8), ("ssq", 1), ("e2", 1), ("w1", 1), ("w2", 1), ("cnt", 1), ("rinv", 6)):
            cols[name] = (at, w)
            at += w
        assert at <= 320
        MFB = sb("MFB", [8, 2, 3, 128])

        def c_(s, name, n=None):
            a, w = cols[name]
            return SM(s, a, n or w)

        def slot(n, words=SLOT):
            return ring[:, n % N_SLOT, 0:words]

        loads = []

        def add(words, src, **dims):
            n = len(loads)
            loads.append((slot(n, words).rearrange("p (a c) -> p a c", **dims), src))
            return n

        def rows(w, k0, k1, c0, c1):
            return w[128 * k0:128 * k1, c0:c1].rearrange("(k p) c -> p k c", p=128)

        first = {}
        for l in range(DEPTH):
            first["ada", l] = len(loads)
            for n in range(12):
                for k in (0, 4):
                    add(2048, rows(I["ada_w"][l], k, k + 4, 512 * n, 512 * n + 512), a=4)
            first["in", l] = len(loads)
            for n in range(5):
                c0, c1 = IN_CUTS[n:n + 2]
                for k in (0, 4):
                    add(4 * (c1 - c0), rows(I["w_in"][l], k, k + 4, c0, c1), a=4)
            first["uq", l] = add(2 * C_H * C_QK, rows(I["c_wuq"][l], 0, 2, 0, C_H * C_QK), a=2)
            first["ukv", l] = add(C_H * 128, rows(I["c_wukv"][l], 0, 1, 0, C_H * 128), a=1)
            first["out", l] = len(loads)
            for n in range(2):
                for k in (0, 4):
                    add(2048, rows(I["w_out"][l], k, k + 4, 512 * n, 512 * n + 512), a=4)
            if l == 0:
                def w2_load(f):
                    first["w2", f] = add(2048, rows(I["ffn_w2"][0], 2 * f, 2 * f + 2, 0, D), a=2)

                for f in range(N_FF):
                    first["w1", f] = add(2048, rows(I["ffn_w1"][0], 0, KD, FF * f, FF * f + FF), a=KD)
                    first["w3", f] = add(2048, rows(I["ffn_w3"][0], 0, KD, FF * f, FF * f + FF), a=KD)
                    if f:
                        w2_load(f - 1)
                w2_load(N_FF - 1)
        W0 = len(loads)
        S0 = first["w1", 0]
        N_SPLIT = 3 * N_FF
        assert N_SPLIT % N_HI == 0 and PER_EXPERT % N_HI == 0

        def is_split(n):
            return S0 <= n < S0 + N_SPLIT
        expert_order = []
        for f in range(N_FE):
            expert_order += [("w1", f, 0), ("w1", f, 1), ("w3", f, 0), ("w3", f, 1)]
            if f:
                expert_order += [("w2", f - 1, 0), ("w2", f - 1, 1)]
        expert_order += [("w2", N_FE - 1, 0), ("w2", N_FE - 1, 1)]
        expert_at = {key: j for j, key in enumerate(expert_order)}
        assert len(expert_order) == PER_EXPERT and PER_EXPERT % N_SLOT == 0
        FULL_PER_EXPERT = 16 * PER_EXPERT // N_SLOT

        slot_full = [sem(f"slot_full{i}") for i in range(N_SLOT)]
        slot_used = sem("slot_used")
        hi_ready = sem("hi_ready")
        split_done = sem("split_done")
        first_in, x_in, small_in, adab_in = sem("first_in"), sem("x_in"), sem("small_in"), [sem("adab_in0"), sem("adab_in1")]
        out_sem = [sem("out_sem0"), sem("out_sem1")]
        state_out = [sem("state_out0"), sem("state_out1")]
        y_out = sem("y_out")
        dve_chain, act_chain = sem("dve_chain"), sem("act_chain")
        setup_T, c_ready, ng_ready, zeros_ready = sem("setup_T"), sem("c_ready"), sem("ng_ready"), sem("zeros_ready")
        names = ["modrow_ready", "mod_T", "mod_ready", "gate_bc", "gate_copied",
                 "ssq_ready", "xr_ready", "xr_T", "xnT_a", "xnT_d", "x_done",
                 "in_mm", "h_ready",
                 "qkA_ready", "TA", "TA_ready", "SA", "nmA", "PA", "PTA", "PTA_a", "PTA_d", "OA", "oA",
                 "cn_ready", "TC", "TC_ready", "C_mm", "C_heads", "C_headsx", "qkC_ready", "TC1", "TC1_a",
                 "TC1_d", "TC2", "TC2_a", "SC", "nmC", "PC", "PTC", "PTC_a", "PTC_d", "OC", "oC",
                 "absf_ready", "log_ready", "lf_ready", "bc_T", "u_ready", "qkB_T", "uT_S", "run_ready", "M_mm",
                 "Earg_ready", "E_ready", "last_mm", "WT_ready", "ws_arg", "ws_ready", "kw_ready", "num_mm",
                 "state_copied", "oB", "o_T", "oT_a", "oT_d", "out_mm",
                 "up_mm", "silu_ready", "hid_ready", "hid_T", "hT_hi", "hT_ready", "xs_hi", "xs_ready",
                 "xn_T", "xn_a", "xn_d", "logits_mm", "gap_ready", "gap_exp", "sel_ready", "pos_mm", "pass_ready",
                 "P_ready", "gather_mm", "Pg_T", "xe_hi", "xe_ready", "Pg_a", "e_silu", "e_hid", "e_T", "e_hT_hi", "e_hT",
                 "y_a", "y_d", "scat_mm", "acc_done", "places_moved"]
        Q = {n: sem(n) for n in names}

        def summed(eng, n, it=None):
            eng.wait_ge(slot_used, n + 1 if it is None else it * PER_EXPERT + (n + 1))

        block = ctx.enter_context(nc.Block())

        @block.sync
        def _(sp):
            for n, (dst, src) in enumerate(loads):
                m = n - N_SLOT
                if is_split(m):
                    sp.wait_ge(split_done, m - S0 + 1)
                elif m >= 0:
                    sp.wait_ge(slot_used, m + 1)
                sp.dma_start(dst, src).then_inc(slot_full[n % N_SLOT], 16)
            sp.wait_ge(Q["pass_ready"], 1)
            passes = sp.value_load(n_pass[0:1, 0:1], min_val=1, max_val=2)
            with sp.Fori(0, passes) as p:
                with sp.Fori(0, N_EXP) as e:
                    it = p * N_EXP + e
                    for j, (kind, f, half) in enumerate(expert_order):
                        n = W0 + j
                        dst = slot(n)
                        if kind == "w2":
                            r0 = FE * f + 256 * half
                            src = I["moe_w2"][0][bass.ds(e, 1), r0:r0 + 256, :]
                            src = src.rearrange("e (k p) c -> p (e k) c", p=128)
                            dst = dst.rearrange("p (a c) -> p a c", a=2)
                        else:
                            w = I["moe_" + kind][0]
                            src = w[bass.ds(e, 1), 512 * half:512 * half + 512, FE * f:FE * f + FE]
                            src = src.rearrange("e (k p) c -> p (e k) c", p=128)
                            dst = dst.rearrange("p (a c) -> p a c", a=4)
                        if j < N_SLOT:
                            sp.wait_ge(slot_used, n - N_SLOT + 1)
                        sp.wait_ge(split_done, it * PER_EXPERT + (N_SPLIT + j - N_SLOT + 1))
                        sp.dma_start(dst, src).then_inc(slot_full[n % N_SLOT], 16)
            sp.wait_ge(y_out, 32)
            for l in range(DEPTH):
                sp.wait_ge(out_sem[l], 16 * 4)
                sp.wait_ge(state_out[l], 16 * 3)

        N_FIRST = 5
        N_SMALL = DEPTH * (len(GAIN) + 4 + 2 * 2 * 2 + 1) + 1

        @block.gpsimd
        def _(pool):
            def load(dst, src, s=small_in, **how):
                pool.dma_start(dst, src, **how).then_inc(s, 16)

            load(R(0, 0, 6144, 2), I["ada_b"][0:1, :].broadcast_to([2, 6144]), adab_in[0])
            for l in range(DEPTH):
                for name in GAIN:
                    if name == "m0":
                        src = I["state_mlstm_m"][0:1, l, :, :].rearrange("a d h -> a (d h)")
                    else:
                        src = I[name][l:l + 1, :]
                    load(G(l, name), src.broadcast_to([128, src.shape[1]]))
                load(ctx_k[:, l, :], I["cache_swa_k"][0, l].rearrange("t g d -> t (g d)"))
                load(ctx_v[:, l, :], I["cache_swa_v"][0, l].rearrange("t g d -> t (g d)"))
                load(ctx_ckv[:, l, :], I["cache_mla_ckv"][0, l])
                load(ctx_kr[:, l, :], I["cache_mla_krope"][0, l])
                for par in range(2):
                    for d in range(2):
                        dst = C0n0[64 * par:64 * par + 64, l, d, :, :]
                        load(dst[:, :, 0:HD], I["state_mlstm_C"][0, l, d, par:B_H:2].rearrange("h k v -> k h v"))
                        load(dst[:, :, HD:HD + 1],
                             I["state_mlstm_n"][0, l, d, par:B_H:2].rearrange("h (k o) -> k h o", o=1),
                             allow_slow_non_contiguous=True)
                load(m0row[:, 1 + l:2 + l], I["state_mlstm_m"][0, l].rearrange("d (h o) -> (d h) o", o=1))
            load(router[:, :, :], I["moe_router"][0].rearrange("(k p) e -> p k e", p=128))
            for l in range(DEPTH):
                u = 2 * l

                def store(dst, src, s=out_sem[l], **how):
                    pool.dma_start(dst, src, **how).then_inc(s, 16)

                pool.wait_ge(Q["h_ready"], 10 * l + 9)
                store(O["new_swa_v"][0, l].rearrange("t g d -> t (g d)"), h[:, 0, AV:AV + 128])
                store(O["new_mla_krope"][0, l], h[:, 0, CKR:CKR + C_ROPE])
                pool.wait_ge(Q["qkA_ready"], u + 1)
                store(O["new_swa_k"][0, l].rearrange("t g d -> t (g d)"), ka_out[:, :])
                pool.wait_ge(Q["state_copied"], l + 1)
                st = R(0, ST, 8 * (HD + 1), 64).rearrange("p (c n) -> p c n", c=8)
                store(O["new_mlstm_C"][0, l].rearrange("d h k v -> k (d h) v"), st[:, :, 0:HD], state_out[l])
                store(O["new_mlstm_n"][0, l].rearrange("d h (k o) -> k (d h) o", o=1), st[:, :, HD:HD + 1], state_out[l],
                      allow_slow_non_contiguous=True)
                store(O["new_mlstm_m"][0:1, l].rearrange("a d h -> a (d h)"), c_(0, "mo")[0:1, :], state_out[l])
                pool.wait_ge(Q["cn_ready"], u + 1)
                store(O["new_mla_ckv"][0, l], ckv_out[:, :])
                if l == 0:
                    pool.wait_ge(Q["x_done"], 4)
                    load(R(0, 0, 6144, 2), I["ada_b"][1:2, :].broadcast_to([2, 6144]), adab_in[1])
            for s, name in ((0, "y_prompt"), (1, "y_sample")):
                pool.wait_ge(Q["x_done"], 7 + s)
                pool.dma_start(O[name][0], x[:, s, :]).then_inc(y_out, 16)

        @block.tensor
        def _(pe):
            mm, tr = nc.tensor.matmul, nc.tensor.transpose

            def wait(name, v):
                pe.wait_ge(Q[name], v)

            def weights(n):
                pe.wait_ge(slot_full[n % N_SLOT], 16 * (n // N_SLOT + 1))
                return loads[n][0]

            def split_weights(n, n_lo):
                i = n - S0
                pe.wait_ge(split_done, i + 1)
                k = loads[n][0].shape[1]
                return [w.rearrange("p (a c) -> p a c", a=k) for w in (w_hi(i), w_lo(i, n_lo))]

            def mm3(out, s_hi, s_lo, m_hi, m_lo, start, stop):
                mm(out, s_hi, m_hi, start=start, stop=False)
                mm(out, s_hi, m_lo, start=False, stop=False)
                return mm(out, s_lo, m_hi, start=False, stop=stop)

            def T(out, src):
                k = src.shape[0]
                return tr(out, src, ident[0:k, 0:k])

            pe.wait_ge(first_in, 16 * N_FIRST)
            T(bank(0, 2 * KD), crow[:, :])
            T(bank(1, 4 * KD), ngrow[:, :]).then_inc(setup_T, 1)
            pe.wait_ge(c_ready, 1)
            pe.wait_ge(ng_ready, 1)

            def modulation(l):
                n_gate = [0]

                def rows_of(n):
                    if n >= 2:
                        wait("modrow_ready", 12 * l + n - 1)
                    for k in range(KD):
                        w = weights(first["ada", l] + 2 * n + k // 4)
                        last = mm(bank(n % 2, parts=2), cT[:, k:2 * KD:KD], w[:, k % 4, :], start=(k == 0), stop=(k == KD - 1))
                        if k % 4 == 3 and k < 7:
                            last.then_inc(slot_used, 1)
                    last.then_inc(slot_used, 1)

                def spread(n):
                    wait("modrow_ready", 12 * l + n + 1)
                    j, half = n // 2, n % 2
                    row = modrow[:, n % 2, :]
                    if j in (2, 5):
                        for s in range(2):
                            b = n_gate[0]
                            if b >= 2:
                                wait("gate_copied", 8 * l + b - 1)
                            mm(bank(3 + b % 2), PICK[0:2, s, :], row, start=True, stop=True).then_inc(Q["gate_bc"], 1)
                            n_gate[0] += 1
                    else:
                        jj = j if j < 2 else j - 1
                        for c in range(4):
                            a = 16 * jj + 2 * (4 * half + c)
                            last = T(bank(2, 2, a=a), row[:, 128 * c:128 * c + 128])
                        last.then_inc(Q["mod_T"], 1)

                for n in range(12):
                    rows_of(n)
                    if n:
                        spread(n - 1)
                spread(11)

            def norm_T(l, j, s):
                nu = 4 * l + 2 * j + s
                wait("xr_ready", nu + 1)
                for k in range(KD):
                    last = T(bank(4 * s + k // 4, 128, a=128 * (k % 4)), xr[:, s, 128 * k:128 * k + 128])
                last.then_inc(Q["xr_T"], 1)
                wait("xnT_a", nu + 1)
                wait("xnT_d", nu + 1)

            def in_proj(l):
                for n in range(5):
                    c = IN_CUTS[n + 1] - IN_CUTS[n]
                    for s in range(2):
                        i = 2 * n + s
                        if i >= 8:
                            wait("h_ready", 10 * l + i - 7)
                        for k in range(KD):
                            w = weights(first["in", l] + 2 * n + k // 4)
                            last = mm(bank(i % 8, c), xnT[:, k, 128 * s:128 * s + 128], w[:, k % 4, :],
                                      start=(k == 0), stop=(k == KD - 1))
                            if s == 1 and k == 3:
                                last.then_inc(slot_used, 1)
                        last.then_inc(Q["in_mm"] if s == 0 else slot_used, 1)

            def scores_softmax_out(l, s, X, qT, kT, v, n_kt):
                u = 2 * l + s
                b0 = 4 * s
                for hi in range(6):
                    for kt in range(n_kt):
                        a = (hi % 3 * n_kt + kt) * 128
                        last = mm(bank(b0 + hi // 3 * 2 + a // 512, 128, a=a % 512), qT(hi), kT(hi, kt),
                                  start=True, stop=True)
                last.then_inc(Q["S" + X], 1)
                yield
                wait("P" + X, u + 1)
                p = R(s, SQ, 6 * n_kt * 128)
                for i in range(6 * n_kt):
                    last = T(bank(b0 + i // 4, 128, a=128 * (i % 4)), p[:, 128 * i:128 * i + 128])
                last.then_inc(Q["PT" + X], 1)
                yield
                wait("PT" + X + "_a", u + 1)
                wait("PT" + X + "_d", u + 1)
                pT = R(s, QK, 6 * n_kt * 128)
                for hi in range(6):
                    for kt in range(n_kt):
                        i = hi * n_kt + kt
                        last = mm(bank(b0 + 3, HD, a=HD * hi), pT[:, 128 * i:128 * i + 128], v(hi, kt),
                                  start=(kt == 0), stop=(kt == n_kt - 1))
                last.then_inc(Q["O" + X], 1)
                yield

            def group_A(l, s):
                u = 2 * l + s
                wait("qkA_ready", u + 1)
                wait("h_ready", 10 * l + 10)
                qk = R(s, QK + 512 * s, 512)
                b0 = 4 * s
                for r in range(3):
                    T(bank(b0, 128, a=128 * r), qk[:, 128 * r:128 * r + 128])
                if s == 0:
                    last = T(bank(b0, 128, a=384), ka_out[:, :])
                else:
                    T(bank(b0, 128, a=384), qk[:, 384:512])
                    last = T(bank(b0 + 1, 128), ctx_k[:, l, :])
                last.then_inc(Q["TA"], 1)
                yield
                wait("TA_ready", u + 1)
                t = R(s, QKT, 640)

                def qT(hi):
                    g, r = hi // 3, hi % 3
                    return t[64 * g:64 * g + 64, 128 * r:128 * r + 128]

                def kT(hi, kt):
                    g = hi // 3
                    a = 384 if kt == 0 else 512
                    return t[64 * g:64 * g + 64, a:a + 128]

                def v(hi, kt):
                    g = hi // 3
                    return h[:, s, AV + 64 * g:AV + 64 * g + 64] if kt == 0 else ctx_v[:, l, 64 * g:64 * g + 64]

                yield from scores_softmax_out(l, s, "A", qT, kT, v, 1 + s)

            def group_B(l, s):
                u = 2 * l + s
                b0 = 4 * s
                wait("lf_ready", u + 1)
                wait("oA", u + 1)
                lf = c_(s, "lf")
                mm(bank(b0, 4), K("s_le_t"), lf[:, 0:4], start=True, stop=True)
                mm(bank(b0, 4, a=4), K("s_ge_t"), lf[:, 4:8], start=True, stop=True)
                for i in range(2):
                    T(bank(b0 + 1, 128, a=128 * i), h[:, s, BQ + 128 * i:BQ + 128 * i + 128])
                for i in range(2):
                    last = T(bank(b0 + 1, 128, a=256 + 128 * i), R(s, KS, 256)[:, 128 * i:128 * i + 128])
                last.then_inc(Q["bc_T"], 1)
                yield
                wait("u_ready", u + 1)
                T(bank(b0 + 2, 128, parts=8), c_(s, "u"))
                wait("qkB_T", u + 1)
                t = R(s, QKT, 512)

                def head(a, hh):
                    return t[64 * (hh % 2):64 * (hh % 2) + 64, a + 128 * (hh // 2):a + 128 * (hh // 2) + 128]

                for hh in range(B_H):
                    last = mm(bank(b0 + 3 * (hh % 2), 128, a=128 * (hh // 2)), head(256, hh), head(0, hh),
                              start=True, stop=True)
                last.then_inc(Q["uT_S"], 1)
                yield
                wait("run_ready", u + 1)
                run = MFB[:, s, :, :]
                for d in range(2):
                    mm(bank(b0, 4, a=256 + 4 * d), run[:, 1 + d, :], ident[0:8, 4 * d:4 * d + 4], start=True, stop=True)
                for c in range(8):
                    last = mm(bank(b0 + 1 + c // 4, 128, a=128 * (c % 4)), PICK[:, c, :], run[:, 1 + c // 4, :],
                              start=True, stop=True)
                last.then_inc(Q["M_mm"], 1)
                yield
                if s == 0:
                    wait("Earg_ready", u + 1)
                    m16 = c_(s, "m16").rearrange("p (a c) -> p a c", a=2)
                    out = bank(b0, 16, a=288).rearrange("p (a c) -> p a c", a=2)
                    mm(out[:, :, 0:4], K("row_last"), m16[:, :, 0:4], start=True, stop=True)
                    mm(out[:, :, 4:8], K("row_first"), m16[:, :, 4:8], start=True, stop=True).then_inc(Q["last_mm"], 1)
                yield
                wait("WT_ready", u + 1)
                v1 = R(s, V1, 4 * 65).rearrange("p (h n) -> p h n", h=4)
                wT = R(s, QK, 1024)
                for c in range(8):
                    last = mm(bank(b0 + 1 + c // 4, 65, a=65 * (c % 4)), wT[:, 128 * c:128 * c + 128], v1[:, c % 4, :],
                              start=True, stop=True)
                if s == 1:
                    for c in range(8):
                        hh, d = c % 4, c // 4
                        p0 = 64 * (hh % 2)
                        last = mm(bank(b0 + 3 * (hh % 2), 65, a=65 * (2 * d + hh // 2)), head(0, hh),
                                  C0n0[p0:p0 + 64, l, d, hh // 2, :], start=True, stop=True)
                else:
                    wait("kw_ready", l + 1)
                    kw = R(0, KW, 512)
                    for c in range(8):
                        last = mm(bank(b0 if c >= 4 else b0 + 3, 65, parts=64, a=65 * (c % 4)),
                                  kw[:, 64 * c:64 * c + 64], v1[:, c % 4, :], start=True, stop=True)
                last.then_inc(Q["num_mm"], 1)
                yield

            def group_C(l, s):
                u = 2 * l + s
                b0 = 4 * s
                wait("cn_ready", u + 1)
                wait("oB", u + 1)
                if s == 0:
                    wait("state_copied", l + 1)
                cn = R(s, VC, 384)
                T(bank(b0 + 3, 128), cn[:, 0:128])
                T(bank(b0 + 3, 128, a=128), cn[:, 128:256])
                if s == 0:
                    last = T(bank(b0 + 3, 128, a=256), ckv_out[:, :])
                else:
                    T(bank(b0 + 3, 128, a=256), cn[:, 256:384])
                    last = T(bank(b0 + 3, 128, a=384), ctx_ckv[:, l, :])
                last.then_inc(Q["TC"], 1)
                yield
                wait("TC_ready", u + 1)
                t = R(s, QKT, 512)
                uq, ukv = weights(first["uq", l]), weights(first["ukv", l])
                for n in range(2):
                    for k in range(2):
                        last = mm(bank(b0 + n, 288), t[:, 128 * k:128 * k + 128], uq[:, k, 288 * n:288 * n + 288],
                                  start=(k == 0), stop=(k == 1))
                if s == 1:
                    last.then_inc(slot_used, 1)
                for n in range(2):
                    last = mm(bank(b0 + 2 + n, 384), t[:, 256:384], ukv[:, 0, 384 * n:384 * n + 384], start=True, stop=True)
                last.then_inc(Q["C_mm"], 1)
                yield
                if s == 1:
                    wait("C_heads", u + 1)
                    for n in range(2):
                        last = mm(bank(b0 + 2 + n, 384), t[:, 384:512], ukv[:, 0, 384 * n:384 * n + 384],
                                  start=True, stop=True)
                    last.then_inc(slot_used, 1)
                yield
                wait("qkC_ready", u + 1)
                nh = 12 + 6 * s
                qk = R(s, QK, nh * 96).rearrange("p (h d) -> p h d", h=nh)
                for i in range(min(nh, 16)):
                    last = T(bank(b0 + i // 4, 128, 96, 128 * (i % 4)), qk[:, i, :])
                last.then_inc(Q["TC1"], 1)
                yield
                wait("TC1_a", u + 1)
                wait("TC1_d", u + 1)
                if s == 1:
                    for i in range(16, nh):
                        last = T(bank(b0, 128, 96, 128 * (i % 4)), qk[:, i, :])
                    last.then_inc(Q["TC2"], 1)
                    wait("TC2_a", l + 1)
                qkT = R(s, QKT, nh * 128, 96)

                def qT(hi):
                    return qkT[:, 128 * hi:128 * hi + 128]

                def kT(hi, kt):
                    return qkT[:, 128 * (6 + 6 * kt + hi):128 * (7 + 6 * kt + hi)]

                def v(hi, kt):
                    return R(s, VC + 384 * kt + 64 * hi, 64)

                yield from scores_softmax_out(l, s, "C", qT, kT, v, 1 + s)

            def both(group, l):
                a, b = group(l, 0), group(l, 1)
                for _ in a:
                    next(b)

            def out_proj(l):
                for s in range(2):
                    wait("oC", 2 * l + s + 1)
                    for k in range(KD):
                        last = T(bank(4 * s + k // 4, 128, a=128 * (k % 4)), o[:, s, 128 * k:128 * k + 128])
                    last.then_inc(Q["o_T"], 1)
                for n in range(2):
                    for s in range(2):
                        if n == 0:
                            wait("oT_a", 2 * l + s + 1)
                            wait("oT_d", 2 * l + s + 1)
                        t = R(s, QKT, 1024)
                        for k in range(KD):
                            w = weights(first["out", l] + 2 * n + k // 4)
                            last = mm(bank(4 * s + 2 + n), t[:, 128 * k:128 * k + 128], w[:, k % 4, :],
                                      start=(k == 0), stop=(k == KD - 1))
                            if s == 1 and k == 3:
                                last.then_inc(slot_used, 1)
                        last.then_inc(Q["out_mm"] if s == 0 else slot_used, 1)

            def dense_ffn():
                def up(kind, f):
                    hi, lo = split_weights(first[kind, f], 2)
                    for s in range(2):
                        if kind == "w1" and f == 0:
                            wait("xs_ready", s + 1)
                        if kind == "w1" and f >= 2:
                            wait("hT_ready", 2 * (f - 2) + s + 1)
                        for k in range(KD):
                            t = slice(128 * s, 128 * s + 128)
                            last = mm3(bank(2 * (f % 2) + s, FF, a=FF * (kind == "w3")), a_hi[:, k, t], a_lo[:, k, t],
                                       hi[:, k, :], lo[:, k, :], k == 0, k == KD - 1)
                        if s == 0 and kind == "w3":
                            last.then_inc(Q["up_mm"], 1)
                    last.then_inc(slot_used, 1)

                def turn(f):
                    for s in range(2):
                        wait("hid_ready", 2 * f + s + 1)
                        for c in range(2):
                            last = T(bank(2 * (f % 2) + s, 128, a=128 * c), hid[s][:, 128 * c:128 * c + 128])
                        last.then_inc(Q["hid_T"], 1)

                def down(f):
                    hi, lo = split_weights(first["w2", f], 2)
                    for s in range(2):
                        wait("hT_ready", 2 * f + s + 1)
                        for n in range(2):
                            for c in range(2):
                                a = 256 * (f % 2) + 128 * c
                                cols = slice(512 * n, 512 * n + 512)
                                last = mm3(bank(4 + 2 * s + n), t_hi[:, s, a:a + 128], t_lo[:, s, a:a + 128],
                                           hi[:, c, cols], lo[:, c, cols], f == 0 and c == 0, f == N_FF - 1 and c == 1)
                    last.then_inc(slot_used, 1)

                for f in range(N_FF):
                    up("w1", f)
                    if f:
                        turn(f - 1)
                    up("w3", f)
                    if f:
                        down(f - 1)
                turn(N_FF - 1)
                down(N_FF - 1)

            def routing():
                for s in range(2):
                    for k in range(KD):
                        last = T(bank(4 * s + k // 4, 128, a=128 * (k % 4)), xnT[:, k, 128 * s:128 * s + 128])
                    last.then_inc(Q["xn_T"], 1)
                    for k in range(KD):
                        last = mm(bank(4 * s + 2, N_EXP), xnT[:, k, 128 * s:128 * s + 128], router[:, k, :],
                                  start=(k == 0), stop=(k == KD - 1))
                    last.then_inc(Q["logits_mm"], 1)
                wait("sel_ready", 2)
                sel = [c_(0, "sel"), c_(1, "sel")]
                mm(bank(3, 8), K("s_lt_t"), sel[0], start=True, stop=True)
                mm(bank(3, 8, a=8), K("s_lt_t"), sel[1], start=True, stop=False)
                mm(bank(3, 8, a=8), K("ones"), sel[0], start=False, stop=True)
                mm(bank(3, 8, a=16), K("ones"), sel[0], start=True, stop=False)
                mm(bank(3, 8, a=16), K("ones"), sel[1], start=False, stop=True).then_inc(Q["pos_mm"], 1)

            def experts():
                wait("pass_ready", 1)
                wait("xn_a", 2)
                wait("xn_d", 2)
                passes = pe.value_load(n_pass[0:1, 0:1], min_val=1, max_val=2)
                with pe.Fori(0, passes) as p:
                    with pe.Fori(0, N_EXP) as e:
                        it = p * N_EXP + e

                        def wait_it(name, per, v):
                            pe.wait_ge(Q[name], it * per + v)

                        def expert_weights(key, a):
                            j = expert_at[key]
                            pe.wait_ge(split_done, it * PER_EXPERT + (N_SPLIT + j + 1))
                            return [w.rearrange("p (a c) -> p a c", a=a) for w in (w_hi(j), w_lo(j, 3))]

                        wait_it("P_ready", 1, 1)
                        for half in range(2):
                            for k in range(4):
                                for s in range(2):
                                    last = mm(bank(6 + half, 128, a=128 * k), xr[:, s, 512 * half + 128 * k:512 * half + 128 * k + 128],
                                              P[:, s, :], start=(s == 0), stop=(s == 1))
                            last.then_inc(Q["gather_mm"], 1)
                        wait_it("acc_done", 4, 1)
                        for s in range(2):
                            last = T(bank(1, 128, a=128 * s), PG[:, s, :])
                        last.then_inc(Q["Pg_T"], 1)
                        def up(kind, f):
                            b = 2 * (f % 2) + (kind == "w3")
                            if f >= 2:
                                wait_it("e_hid", N_FE, f - 1)
                            elif kind == "w3" and f == 0:
                                wait_it("Pg_a", 1, 1)
                            for half in range(2):
                                if f == 0 and kind == "w1":
                                    wait_it("xe_ready", 2, half + 1)
                                hi, lo = expert_weights((kind, f, half), 4)
                                for k in range(4):
                                    last = mm3(bank(b), xe_hi[:, 4 * half + k, :], xe_lo[:, 4 * half + k, :],
                                               hi[:, k, :], lo[:, k, :], half == 0 and k == 0, half == 1 and k == 3)
                                last.then_inc(slot_used, 1)

                        def turn(f):
                            wait_it("e_hid", N_FE, f + 1)
                            if f >= 2:
                                wait_it("e_hT", N_FE, f - 1)
                            for c in range(4):
                                last = T(bank(6 + f % 2, 128, a=128 * c), hid[f % 2][:, 128 * c:128 * c + 128])
                            last.then_inc(Q["e_T"], 1)

                        def down(f):
                            wait_it("e_hT", N_FE, f + 1)
                            for half in range(2):
                                hi, lo = expert_weights(("w2", f, half), 2)
                                for n in range(2):
                                    for c in range(2):
                                        a = 128 * (2 * half + c)
                                        cols = slice(512 * n, 512 * n + 512)
                                        last = mm3(bank(4 + n), t_hi[:, f % 2, a:a + 128], t_lo[:, f % 2, a:a + 128],
                                                   hi[:, c, cols], lo[:, c, cols], f == 0 and half == 0 and c == 0,
                                                   f == N_FE - 1 and half == 1 and c == 1)
                                last.then_inc(slot_used, 1)

                        for f in range(N_FE):
                            up("w1", f)
                            if f:
                                turn(f - 1)
                            up("w3", f)
                            if f:
                                down(f - 1)
                        turn(N_FE - 1)
                        down(N_FE - 1)
                        wait_it("y_a", 1, 1)
                        wait_it("y_d", 1, 1)
                        for s in range(2):
                            for n in range(2):
                                mm(bank(2 * s + n), PGT[:, s, :], y_e[:, 512 * n:512 * n + 512], start=True, stop=True).then_inc(Q["scat_mm"], 1)

            for l in range(DEPTH):
                modulation(l)
                wait("mod_ready", l + 1)
                norm_T(l, 0, 0)
                norm_T(l, 0, 1)
                in_proj(l)
                both(group_A, l)
                both(group_B, l)
                both(group_C, l)
                out_proj(l)
                norm_T(l, 1, 0)
                norm_T(l, 1, 1)
                if l == 0:
                    dense_ffn()
                else:
                    routing()
                    experts()

        @block.scalar
        def _(act):
            A = nc.scalar.activation
            chain = [0]

            def wait(name, v):
                act.wait_ge(Q[name], v)

            def link(ins):
                chain[0] += 1
                ins.then_inc(act_chain, 1)
                act.wait_ge(act_chain, chain[0])

            for dst, src, s in ((crow[0:KD, :], I["c_ctx"].rearrange("(k p) -> k p", p=128), first_in),
                                (crow[KD:2 * KD, :], I["c"].rearrange("a (k p) -> (a k) p", p=128), first_in),
                                (cst[:, :], I["consts"], first_in),
                                (ngrow[0:2 * KD, :], I["norm1_g"].rearrange("l (k p) -> (l k) p", p=128), first_in),
                                (ngrow[2 * KD:4 * KD, :], I["norm2_g"].rearrange("l (k p) -> (l k) p", p=128), first_in),
                                (x[:, 0, :], I["x_prompt"][0], x_in), (x[:, 1, :], I["x_sample"][0], x_in)):
                act.dma_start(dst, src).then_inc(s, 16)
            act.wait_ge(setup_T, 1)
            A(cT[:, :], bank(0, 2 * KD), ACT.Silu).then_inc(c_ready, 1)

            def split_hi(n):
                i = n - S0
                act.wait_ge(slot_full[n % N_SLOT], 16 * (n // N_SLOT + 1))
                act.wait_ge(slot_used, n - N_HI + 1)
                A(w_hi(i), slot(n), ACT.Copy).then_inc(hi_ready, 1)

            def norm(l, j, s):
                nu = 4 * l + 2 * j + s
                if nu >= 2:
                    wait("x_done", nu - 1)
                elif nu == 0:
                    act.wait_ge(x_in, 32)
                A(xr[:, s, :], x[:, s, :], ACT.Square, accum_out=c_(s, "ssq")).then_inc(Q["ssq_ready"], 1)

            def norm_out(l, j, s):
                nu = 4 * l + 2 * j + s
                wait("xr_T", nu + 1)
                wait("mod_ready", l + 1)
                for k in range(4):
                    last = A(xnT[:, k, 128 * s:128 * s + 128], bank(4 * s, 128, a=128 * k), ACT.Identity,
                             scale=modS[:, j, k, s:s + 1], bias=modT[:, 2 * j, k, s:s + 1])
                last.then_inc(Q["xnT_a"], 1)
                if nu in (2, 3):
                    wait("xnT_a", nu + 1)
                    A(a_hi[:, 0:4, 128 * s:128 * s + 128], xnT[:, 0:4, 128 * s:128 * s + 128], ACT.Copy)\
                        .then_inc(Q["xs_hi"], 1)

            def in_proj(l):
                for n in range(5):
                    for s in range(2):
                        i = 2 * n + s
                        if s == 0:
                            wait("in_mm", 5 * l + n + 1)
                        else:
                            summed(act, first["in", l] + 2 * n + 1)
                        c0, c1 = IN_CUTS[n:n + 2]
                        A(h[:, s, c0:c1], bank(i % 8, c1 - c0), ACT.Copy).then_inc(Q["h_ready"], 1)

            def softmax(l, s, X, scale, n_kt):
                u = 2 * l + s
                wait("nm" + X, u + 1)
                p = R(s, SQ, 6 * n_kt * 128)
                w = 128 * n_kt
                for hi in range(6):
                    last = A(p[:, w * hi:w * hi + w], banks(4 * s + hi // 3 * 2, 3 * w)[:, w * (hi % 3):w * (hi % 3) + w], ACT.Exp,
                             bias=c_(s, "nm")[:, hi:hi + 1], scale=scale, accum_out=c_(s, "ls")[:, hi:hi + 1])
                if X == "A":
                    last = A(c_(s, "es"), c_(s, "es"), ACT.Exp)
                last.then_inc(Q["P" + X], 1)
                yield
                wait("PT" + X, u + 1)
                n = 512 * n_kt
                A(R(s, QK, n), banks(4 * s, n), ACT.Copy).then_inc(Q["PT" + X + "_a"], 1)
                yield

            def group_A(l, s):
                u = 2 * l + s
                wait("TA", u + 1)
                n = 512 + 128 * s
                A(R(s, QKT, n), banks(4 * s, n), ACT.Copy).then_inc(Q["TA_ready"], 1)
                yield
                yield from softmax(l, s, "A", HD ** -0.5, 1 + s)

            def group_B(l, s):
                u = 2 * l + s
                wait("absf_ready", u + 1)
                link(A(c_(s, "expl"), c_(s, "absf"), ACT.Exp, scale=-1.0))
                A(c_(s, "expl"), c_(s, "expl"), ACT.Ln, bias=1.0).then_inc(Q["log_ready"], 1)
                yield
                wait("bc_T", u + 1)
                A(R(s, QKT, 512), bank(4 * s + 1), ACT.Copy).then_inc(Q["qkB_T"], 1)
                yield
                wait("Earg_ready", u + 1)
                A(R(s, SQ, 1024), R(s, SQ, 1024), ACT.Exp, scale=-1.0)
                A(c_(s, "em"), c_(s, "em"), ACT.Exp, scale=-1.0)
                if s == 1:
                    A(c_(s, "a"), c_(s, "a"), ACT.Exp)
                A(R(s, SIG, 256), h[:, s, BO:BO + 256], ACT.Exp, scale=-1.0).then_inc(Q["E_ready"], 1)
                yield
                if s == 0:
                    wait("ws_arg", l + 1)
                    A(c_(0, "ws"), c_(0, "ws"), ACT.Exp).then_inc(Q["ws_ready"], 1)
                    wait("num_mm", u + 1)
                    st = R(0, ST, 520, 64)
                    A(st[:, 0:260], bank(3, 260, 64), ACT.Copy)
                    A(st[:, 260:520], bank(0, 260, 64), ACT.Copy).then_inc(Q["state_copied"], 1)
                yield

            def group_C(l, s):
                u = 2 * l + s
                b0 = 4 * s
                wait("TC", u + 1)
                A(R(s, QKT, 384 + 128 * s), bank(b0 + 3, 384 + 128 * s), ACT.Copy).then_inc(Q["TC_ready"], 1)
                yield
                wait("C_mm", u + 1)
                heads = R(s, QK, 18 * 96).rearrange("p (h d) -> p h d", h=18)

                def halves(b, n):
                    return PS[:, b:b + 2, 0:n]

                A(R(s, QK, 576).rearrange("p (a n) -> p a n", a=2), halves(b0, 288), ACT.Copy)

                def kv(set_):
                    src = halves(b0 + 2, 384).rearrange("p a (h d) -> p a h d", h=3)
                    dst = heads[:, 6 + 6 * set_:12 + 6 * set_, 0:C_NOPE].rearrange("p (a h) d -> p a h d", a=2)
                    A(dst, src[:, :, :, 0:C_NOPE], ACT.Copy)
                    dst = R(s, VC + 384 * set_, 384).rearrange("p (a h d) -> p a h d", a=2, h=3)
                    kr = h[:, s, CKR:CKR + C_ROPE] if set_ == 0 else ctx_kr[:, l, :]
                    A(heads[:, 6 + 6 * set_:12 + 6 * set_, C_NOPE:C_QK],
                      kr.unsqueeze(1).broadcast_to([128, 6, C_ROPE]), ACT.Copy)
                    return A(dst, src[:, :, :, C_NOPE:128], ACT.Copy)

                kv(0).then_inc(Q["C_heads"], 1)
                yield
                if s == 1:
                    summed(act, first["ukv", l])
                    kv(1).then_inc(Q["C_headsx"], 1)
                yield
                wait("TC1", u + 1)
                A(R(s, QKT, 1024, 96), banks(b0, 1024, 96), ACT.Copy).then_inc(Q["TC1_a"], 1)
                if s == 1:
                    wait("TC2", l + 1)
                    A(R(s, QKT + 2048, 256, 96), bank(b0, 256, 96), ACT.Copy).then_inc(Q["TC2_a"], 1)
                yield
                yield from softmax(l, s, "C", C_QK ** -0.5, 1 + s)

            def both(group, l):
                a, b = group(l, 0), group(l, 1)
                for _ in a:
                    next(b)

            def out_proj(l):
                for s in range(2):
                    wait("o_T", 2 * l + s + 1)
                    A(R(s, QKT, 512), bank(4 * s), ACT.Copy).then_inc(Q["oT_a"], 1)

            def dense_start():
                act.wait_ge(out_sem[0], 16 * 4)
                for n in (first["w1", 0], first["w3", 0], first["w1", 1]):
                    split_hi(n)

            def dense_ffn():
                for f in range(N_FF):
                    for s in range(2):
                        if s == 0:
                            wait("up_mm", f + 1)
                        else:
                            summed(act, first["w3", f])
                        A(hid[s][:, 0:FF], bank(2 * (f % 2) + s, FF), ACT.Silu).then_inc(Q["silu_ready"], 1)
                    if f + 1 < N_FF:
                        split_hi(first["w3", f + 1])
                    split_hi(first["w2", f])
                    for s in range(2):
                        wait("hid_T", 2 * f + s + 1)
                        if f >= 2:
                            summed(act, first["w2", f - 2])
                        A(t_hi[:, s, 256 * (f % 2):256 * (f % 2) + 256], bank(2 * (f % 2) + s, 256), ACT.Copy)\
                            .then_inc(Q["hT_hi"], 1)
                    if f + 2 < N_FF:
                        split_hi(first["w1", f + 2])

            def routing():
                for s in range(2):
                    wait("xn_T", s + 1)
                    A(xr[:, s, 0:512], bank(4 * s), ACT.Copy).then_inc(Q["xn_a"], 1)
                    wait("gap_ready", s + 1)
                    A(c_(s, "e2"), c_(s, "e2"), ACT.Exp).then_inc(Q["gap_exp"], 1)

            def experts():
                act.wait_ge(Q["pass_ready"], 1)
                passes = act.value_load(n_pass[0:1, 0:1], min_val=1, max_val=2)
                with act.Fori(0, passes) as p:
                    with act.Fori(0, N_EXP) as e:
                        it = p * N_EXP + e

                        def wait_it(name, per, v):
                            act.wait_ge(Q[name], it * per + v)

                        def hi(kind, f, half):
                            j = expert_at[kind, f, half]
                            n = W0 + j
                            act.wait_ge(slot_full[n % N_SLOT], it * FULL_PER_EXPERT + 16 * (n // N_SLOT + 1))
                            act.wait_ge(slot_used, it * PER_EXPERT + (n - N_HI + 1))
                            A(w_hi(j), slot(n), ACT.Copy).then_inc(hi_ready, 1)

                        def turned(f):
                            wait_it("e_T", N_FE, f + 1)
                            if f >= 2:
                                summed(act, W0 + expert_at["w2", f - 2, 1], it)
                            A(t_hi[:, f % 2, :], bank(6 + f % 2), ACT.Copy).then_inc(Q["e_hT_hi"], 1)

                        hi("w1", 0, 0)
                        hi("w1", 0, 1)
                        for half in range(2):
                            wait_it("gather_mm", 2, half + 1)
                            A(xe_hi[:, 4 * half:4 * half + 4, :].rearrange("p k t -> p (k t)"), bank(6 + half), ACT.Copy)\
                                .then_inc(Q["xe_hi"], 1)
                        wait_it("Pg_T", 1, 1)
                        A(PGT.rearrange("p s t -> p (s t)"), bank(1, 256), ACT.Copy).then_inc(Q["Pg_a"], 1)
                        hi("w3", 0, 0)
                        for f in range(N_FE):
                            hi("w3", f, 1)
                            if f:
                                turned(f - 1)
                            summed(act, W0 + expert_at["w1", f, 1], it)
                            if f >= 2:
                                wait_it("e_T", N_FE, f - 1)
                            A(hid[f % 2], bank(2 * (f % 2)), ACT.Silu).then_inc(Q["e_silu"], 1)
                            if f:
                                hi("w2", f - 1, 0)
                                hi("w2", f - 1, 1)
                            if f + 1 < N_FE:
                                hi("w1", f + 1, 0)
                                hi("w1", f + 1, 1)
                                hi("w3", f + 1, 0)
                        hi("w2", N_FE - 1, 0)
                        hi("w2", N_FE - 1, 1)
                        turned(N_FE - 1)
                        summed(act, W0 + PER_EXPERT - 1, it)
                        A(y_e[:, 0:512], bank(4), ACT.Copy).then_inc(Q["y_a"], 1)

            for l in range(DEPTH):
                norm(l, 0, 0)
                norm(l, 0, 1)
                norm_out(l, 0, 0)
                norm_out(l, 0, 1)
                in_proj(l)
                if l == 0:
                    act.wait_ge(small_in, 16 * N_SMALL)
                both(group_A, l)
                both(group_B, l)
                both(group_C, l)
                out_proj(l)
                norm(l, 1, 0)
                norm(l, 1, 1)
                if l == 0:
                    dense_start()
                norm_out(l, 1, 0)
                norm_out(l, 1, 1)
                if l == 0:
                    dense_ffn()
                else:
                    routing()
                    experts()

        @block.vector
        def _(dve):
            v = nc.vector
            TT, TS, STT, RED = v.tensor_tensor, v.tensor_scalar, v.scalar_tensor_tensor, v.tensor_reduce
            chain = [0]

            def wait(name, n):
                dve.wait_ge(Q[name], n)

            def link(ins):
                chain[0] += 1
                ins.then_inc(dve_chain, 1)
                dve.wait_ge(dve_chain, chain[0])

            def rsqrt(s, n):
                y, t, w, bits = c_(s, "rs", n), c_(s, "tmp", n), c_(s, "var", n), c_(s, "bits", n).bitcast(i32)
                link(v.tensor_single_scalar(bits, w.bitcast(i32), 1, op=ALU.logical_shift_right))
                link(TS(y.bitcast(i32), bits, -1.0, float(0x5F3759DF), ALU.mult, ALU.add))
                for _ in range(3):
                    link(TT(t, y, y, ALU.mult))
                    link(STT(t, t, -0.5, w, ALU.mult, ALU.mult))
                    link(STT(y, t, 1.5, y, ALU.add, ALU.mult))
                return y

            v.memset(m0row[:, 0:1], 0.0).then_inc(zeros_ready, 1)
            dve.wait_ge(zeros_ready, 1)
            dve.wait_ge(setup_T, 1)
            v.tensor_copy(ngT[:, :], bank(1, 4 * KD)).then_inc(ng_ready, 1)
            dve.wait_ge(ng_ready, 1)

            def split_lo(n, n_lo=2):
                i = n - S0
                dve.wait_ge(hi_ready, i + 1)
                dve.wait_ge(slot_used, n - n_lo + 1)
                TT(w_lo(i, n_lo), slot(n), w_hi(i).bitcast(f32), ALU.subtract).then_inc(split_done, 1)

            def modulation(l):
                dve.wait_ge(adab_in[l], 16)
                b_ = [0]

                def copies(n):
                    j, half = n // 2, n % 2
                    if j not in (2, 5):
                        return
                    for s in range(2):
                        b = b_[0]
                        wait("gate_bc", 8 * l + b + 1)
                        v.tensor_copy(gate[:, s, j // 5, 512 * half:512 * half + 512], bank(3 + b % 2))\
                            .then_inc(Q["gate_copied"], 1)
                        b_[0] += 1

                def spread_done(n):
                    j = n // 2
                    if j in (2, 5):
                        return "gate_bc", 8 * l + 4 * (j // 5) + 2 * (n % 2) + 2
                    return "mod_T", 8 * l + [0, 2, None, 4, 6][j] + n % 2 + 1

                for n in range(12):
                    summed(dve, first["ada", l] + 2 * n + 1)
                    if n >= 2:
                        wait(*spread_done(n - 2))
                    TT(modrow[:, n % 2, :], bank(n % 2, parts=2), R(0, 512 * n, 512, 2), ALU.add)\
                        .then_inc(Q["modrow_ready"], 1)
                    if n:
                        copies(n - 1)
                copies(11)
                wait("mod_T", 8 * l + 8)
                link(v.tensor_copy(modT[:, :, :, :].rearrange("p j k s -> p (j k s)"), bank(2, 64)))
                for j in range(2):
                    g = ngT[:, 2 * KD * j + KD * l:2 * KD * j + KD * l + KD].unsqueeze(2).broadcast_to([128, KD, 2])
                    last = STT(modS[:, j, :, :], modT[:, 2 * j + 1, :, :], 1.0, g, ALU.add, ALU.mult)
                last.then_inc(Q["mod_ready"], 1)
                wait("mod_ready", l + 1)

            def norm(l, j, s):
                nu = 4 * l + 2 * j + s
                wait("ssq_ready", nu + 1)
                link(TS(c_(s, "var", 1), c_(s, "ssq"), 1.0 / D, EPS, ALU.mult, ALU.add))
                r = rsqrt(s, 1)
                TS(xr[:, s, :], x[:, s, :], r, None, ALU.mult).then_inc(Q["xr_ready"], 1)

            def norm_out(l, j, s):
                nu = 4 * l + 2 * j + s
                wait("xr_T", nu + 1)
                for k in range(4, KD):
                    last = TS(xnT[:, k, 128 * s:128 * s + 128], bank(4 * s + 1, 128, a=128 * (k - 4)),
                              modS[:, j, k, s:s + 1], modT[:, 2 * j, k, s:s + 1], ALU.mult, ALU.add)
                last.then_inc(Q["xnT_d"], 1)
                if nu in (2, 3):
                    wait("xnT_d", nu + 1)
                    t = slice(128 * s, 128 * s + 128)
                    link(v.tensor_copy(a_hi[:, 4:8, t], xnT[:, 4:8, t]))
                    wait("xs_hi", s + 1)
                    TT(a_lo[:, :, t], xnT[:, :, t], a_hi[:, :, t].bitcast(f32), ALU.subtract).then_inc(Q["xs_ready"], 1)

            def rope(x_, out, cos, sin, n, half, tmp):
                x1, x2 = x_[:, :, 0:half], x_[:, :, half:2 * half]
                c = cos.unsqueeze(1).broadcast_to([128, n, half])
                s_ = sin.unsqueeze(1).broadcast_to([128, n, half])
                TT(tmp[0], x1, c, ALU.mult)
                TT(tmp[1], x2, s_, ALU.mult)
                TT(tmp[2], x1, s_, ALU.mult)
                link(TT(tmp[3], x2, c, ALU.mult))
                TT(out[:, :, 0:half], tmp[0], tmp[1], ALU.subtract)
                return TT(out[:, :, half:2 * half], tmp[2], tmp[3], ALU.add)

            def softmax(l, s, X, scale, n_kt):
                u = 2 * l + s
                w = 128 * n_kt
                wait("S" + X, u + 1)
                lots = banks(4 * s, 2048).rearrange("p (a n) -> p a n", a=2)[:, :, 0:3 * w]
                link(RED(c_(s, "mx").rearrange("p (a h) -> p a h", a=2), lots.rearrange("p a (h n) -> p a h n", h=3),
                         AX.X, ALU.max))
                if X == "A":
                    sink, mx = G(l, "a_sink"), c_(s, "mx")
                    link(STT(mx, mx, scale, sink, ALU.mult, ALU.max))
                    TT(c_(s, "es"), sink, mx, ALU.subtract)
                    TS(c_(s, "nm"), c_(s, "mx"), -1.0, None, ALU.mult).then_inc(Q["nm" + X], 1)
                else:
                    TS(c_(s, "nm"), c_(s, "mx"), -scale, None, ALU.mult).then_inc(Q["nm" + X], 1)
                yield
                wait("P" + X, u + 1)
                if X == "A":
                    link(TT(c_(s, "ls"), c_(s, "ls"), c_(s, "es"), ALU.add))
                link(v.reciprocal(c_(s, "rinv"), c_(s, "ls")))
                wait("PT" + X, u + 1)
                n, all_ = 512 * n_kt, 768 * n_kt
                v.tensor_copy(R(s, QK + n, all_ - n), banks(4 * s, all_)[:, n:all_]).then_inc(Q["PT" + X + "_d"], 1)
                yield
                wait("O" + X, u + 1)
                a = 0 if X == "A" else 640
                TT(o[:, s, a:a + 384].rearrange("p (h d) -> p h d", d=HD), bank(4 * s + 3, 384).rearrange("p (h d) -> p h d", d=HD),
                   c_(s, "rinv").unsqueeze(2).broadcast_to([128, 6, HD]), ALU.mult).then_inc(Q["o" + X], 1)
                yield

            def group_A(l, s):
                u = 2 * l + s
                wait("h_ready", 10 * l + 2 + s + 1)
                a8 = h[:, s, 0:512]
                link(TT(R(s, SQ, 512), a8, a8, ALU.mult))
                link(RED(c_(s, "tmp", 8), R(s, SQ, 512).rearrange("p (h d) -> p h d", h=8), AX.X, ALU.add))
                link(TS(c_(s, "var", 8), c_(s, "tmp", 8), 1.0 / HD, EPS, ALU.mult, ALU.add))
                r = rsqrt(s, 8)
                link(TT(R(s, SQ, 512).rearrange("p (h d) -> p h d", h=8), a8.rearrange("p (h d) -> p h d", h=8),
                        r.unsqueeze(2).broadcast_to([128, 8, HD]), ALU.mult))
                qg = G(l, "a_qn_g").unsqueeze(1).broadcast_to([128, 3, HD])
                kg = G(l, "a_kn_g").unsqueeze(1).broadcast_to([128, 2, HD])
                for g in range(2):
                    TT(R(s, QK, 384).rearrange("p (r g d) -> p r g d", g=2, d=HD)[:, :, g, :],
                       R(s, SQ + 192 * g, 192).rearrange("p (r d) -> p r d", d=HD), qg, ALU.mult)
                if s == 0 and l == 1:
                    dve.wait_ge(out_sem[0], 16 * 4)
                kdst = ka_out[:, :] if s == 0 else R(s, QK + 384, 128)
                last = TT(kdst.rearrange("p (g d) -> p g d", d=HD),
                          R(s, SQ + 384, 128).rearrange("p (g d) -> p g d", d=HD), kg, ALU.mult)
                if s == 1:
                    link(last)
                    last = rope(R(s, QK, 512).rearrange("p (h d) -> p h d", h=8),
                                R(s, QK + 512, 512).rearrange("p (h d) -> p h d", h=8), K("cosA"), K("sinA"), 8, 32,
                                [R(s, SQ + 256 * i, 256).rearrange("p (h d) -> p h d", h=8) for i in range(4)])
                last.then_inc(Q["qkA_ready"], 1)
                yield
                yield from softmax(l, s, "A", HD ** -0.5, 1 + s)

            def group_B(l, s):
                u = 2 * l + s
                g16 = c_(s, "g16")
                wait("h_ready", 10 * l + 6 + s + 1)
                wait("oA", u + 1)
                link(TT(g16, h[:, s, BG:BG + 16], G(l, "b_gate_b"), ALU.add))
                gates = g16.rearrange("p (d k h) -> p d k h", d=2, k=2)
                li, fg = gates[:, :, 0, :], gates[:, :, 1, :]

                def two(name):
                    return c_(s, name).rearrange("p (d h) -> p d h", d=2)

                STT(two("absf"), fg, -1.0, fg, ALU.mult, ALU.max).then_inc(Q["absf_ready"], 1)
                TS(R(s, KS, 256), h[:, s, BK:BK + 256], HD ** -0.5, None, ALU.mult)
                v1 = R(s, V1, 4 * 65).rearrange("p (h n) -> p h n", h=4)
                v.memset(v1[:, :, HD:HD + 1], 1.0)
                v.tensor_copy(v1[:, :, 0:HD], h[:, s, BV:BV + 256].rearrange("p (h d) -> p h d", h=4))
                wait("log_ready", u + 1)
                STT(two("lf"), fg, 0.0, two("expl"), ALU.min, ALU.subtract).then_inc(Q["lf_ready"], 1)
                yield
                wait("bc_T", u + 1)
                m16 = c_(s, "m16")
                v.tensor_copy(m16[:, 8:16], bank(4 * s, 8))
                TT(two("u"), li, bank(4 * s, 8).rearrange("p (d h) -> p d h", d=2), ALU.subtract).then_inc(Q["u_ready"], 1)
                yield
                wait("uT_S", u + 1)
                run = MFB[:, s, :, :]
                link(v.tensor_copy(run[:, 0, :], bank(4 * s + 2, 128, 8)))
                m0 = m0row[:, (1 + l) * s:(1 + l) * s + 1]
                v.tensor_tensor_scan(run[:, 1, :], run[:, 0, :], run[:, 0, :], m0, ALU.max, ALU.max)
                v.tensor_tensor_scan(run[:, 2, ::-1], run[:, 0, ::-1], run[:, 0, ::-1], m0, ALU.max, ALU.max)\
                    .then_inc(Q["run_ready"], 1)
                yield
                wait("M_mm", u + 1)
                link(v.tensor_copy(m16[:, 0:8], bank(4 * s, 8, a=256)))
                if s == 1:
                    TT(c_(s, "a"), G(l, "m0"), m16[:, 0:8], ALU.subtract)
                TT(c_(s, "em"), m16[:, 0:8], m16[:, 8:16], ALU.add)
                mask = K("mask").rearrange("p (d t) -> p d t", d=2)
                for c in range(8):
                    last = STT(R(s, SQ + 128 * c, 128), bank(4 * s + 1 + c // 4, 128, a=128 * (c % 4)),
                               c_(s, "u")[:, c:c + 1], mask[:, c // 4, :], ALU.subtract, ALU.add)
                last.then_inc(Q["Earg_ready"], 1)
                if s == 0:
                    wait("last_mm", l + 1)
                    TT(c_(0, "ws"), c_(0, "u"), bank(0, 8, a=288), ALU.subtract).then_inc(Q["ws_arg"], 1)
                    tot = c_(0, "mo")
                    link(v.tensor_copy(tot, bank(0, 8, a=296)))
                    TT(tot, tot, bank(0, 8, a=288), ALU.add)
                yield
                wait("E_ready", u + 1)
                for par in range(2):
                    def heads_of(a):
                        return R(s, a, 1024).rearrange("p (d a b t) -> p d a b t", d=2, a=2, b=2)[:, :, :, par, :]

                    sT = bank(4 * s + 3 * par, 256).rearrange("p (a t) -> p a t", a=2)
                    last = TT(heads_of(QK), heads_of(SQ), sT.unsqueeze(1).broadcast_to([128, 2, 2, 128]), ALU.mult)
                last.then_inc(Q["WT_ready"], 1)
                if s == 0:
                    wait("ws_ready", l + 1)
                    for d in range(2):
                        last = TT(R(0, KW + 256 * d, 256).rearrange("p (h d) -> p h d", h=4),
                                  R(0, KS, 256).rearrange("p (h d) -> p h d", h=4),
                                  c_(0, "ws")[:, 4 * d:4 * d + 4].unsqueeze(2).broadcast_to([128, 4, HD]), ALU.mult)
                    last.then_inc(Q["kw_ready"], 1)
                yield
                wait("num_mm", u + 1)
                num = R(s, NUM, 520).rearrange("p (c n) -> p c n", c=8)

                def four(b):
                    return bank(b, 260).rearrange("p (c n) -> p c n", c=4)

                for d in range(2):
                    if s == 0:
                        last = v.tensor_copy(num[:, 4 * d:4 * d + 4, :], four(4 * s + 1 + d))
                    else:
                        if d == 0:
                            for par in range(2):
                                last = TT(num.rearrange("p (a b) n -> p a b n", b=2)[:, :, par, :], four(4 * s + 3 * par),
                                          c_(s, "a").rearrange("p (a b) -> p a b", b=2)[:, :, par].unsqueeze(2)
                                          .broadcast_to([128, 4, HD + 1]), ALU.mult)
                            link(last)
                        last = TT(num[:, 4 * d:4 * d + 4, :], num[:, 4 * d:4 * d + 4, :], four(4 * s + 1 + d), ALU.add)
                link(last)
                den, t8, r8 = num[:, :, HD], c_(s, "tmp", 8), c_(s, "rs", 8)
                link(STT(t8, den, -1.0, den, ALU.mult, ALU.max))
                link(TT(t8, t8, c_(s, "em"), ALU.max))
                link(v.reciprocal(r8, t8))
                h8 = R(s, H8, 512)
                link(TT(h8.rearrange("p (c d) -> p c d", c=8), num[:, :, 0:HD],
                        r8.unsqueeze(2).broadcast_to([128, 8, HD]), ALU.mult))
                hs = R(s, H8 + 512, 256)
                link(TT(hs, h8[:, 0:256], h8[:, 256:512], ALU.add))
                link(TT(R(s, BSQ, 256), hs, hs, ALU.mult))
                link(RED(t8[:, 0:4], R(s, BSQ, 256).rearrange("p (h d) -> p h d", h=4), AX.X, ALU.add))
                link(TS(c_(s, "var", 4), t8[:, 0:4], 1.0 / HD, EPS, ALU.mult, ALU.add))
                r4 = rsqrt(s, 4)
                sig = R(s, SIG, 256)
                link(TS(sig, sig, 1.0, None, ALU.add))
                link(v.reciprocal(sig, sig))
                hs4 = hs.rearrange("p (h d) -> p h d", h=4)
                link(TT(hs4, hs4, r4.unsqueeze(2).broadcast_to([128, 4, HD]), ALU.mult))
                link(TT(hs4, hs4, G(l, "b_hn_g").unsqueeze(1).broadcast_to([128, 4, HD]), ALU.mult))
                TT(o[:, s, 384:640], hs, sig, ALU.mult).then_inc(Q["oB"], 1)
                yield

            def group_C(l, s):
                u = 2 * l + s
                wait("h_ready", 10 * l + 8 + s + 1)
                wait("oB", u + 1)
                lat = h[:, s, CQ:CQ + 384]
                link(TT(R(s, SQ, 384), lat, lat, ALU.mult))
                RED(c_(s, "tmp")[:, 0:1], R(s, SQ, 256), AX.X, ALU.add)
                link(RED(c_(s, "tmp")[:, 1:2], R(s, SQ + 256, 128), AX.X, ALU.add))
                TS(c_(s, "var")[:, 0:1], c_(s, "tmp")[:, 0:1], 1.0 / C_QR, EPS, ALU.mult, ALU.add)
                link(TS(c_(s, "var")[:, 1:2], c_(s, "tmp")[:, 1:2], 1.0 / C_KVR, EPS, ALU.mult, ALU.add))
                r = rsqrt(s, 2)
                STT(R(s, VC, 256), lat[:, 0:256], r[:, 0:1], G(l, "c_qa_g"), ALU.mult, ALU.mult)
                STT(ckv_out[:, :] if s == 0 else R(s, VC + 256, 128), lat[:, 256:384], r[:, 1:2], G(l, "c_kva_g"),
                    ALU.mult, ALU.mult).then_inc(Q["cn_ready"], 1)
                yield
                yield
                wait("C_heads", u + 1)
                if s == 1:
                    wait("C_headsx", l + 1)
                if s == 0:
                    dve.wait_ge(state_out[l], 16 * 3)
                nh = 12 + 6 * s
                qk = R(s, QK, nh * 96).rearrange("p (h d) -> p h d", h=nh)
                sq = R(s, SQ, nh * 96).rearrange("p (h d) -> p h d", h=nh)
                link(TT(sq, qk, qk, ALU.mult))
                link(RED(c_(s, "tmp", nh), sq, AX.X, ALU.add))
                link(TS(c_(s, "var", nh), c_(s, "tmp", nh), 1.0 / C_QK, EPS, ALU.mult, ALU.add))
                r = rsqrt(s, nh)
                link(TT(qk, qk, r.unsqueeze(2).broadcast_to([128, nh, C_QK]), ALU.mult))
                TT(qk[:, 0:6, :], qk[:, 0:6, :], G(l, "c_qn_g").unsqueeze(1).broadcast_to([128, 6, C_QK]), ALU.mult)
                last = TT(qk[:, 6:nh, :], qk[:, 6:nh, :], G(l, "c_kn_g").unsqueeze(1).broadcast_to([128, nh - 6, C_QK]),
                          ALU.mult)
                if s == 1:
                    link(last)
                    tail = qk[:, 0:12, C_NOPE:C_QK]
                    last = rope(tail, tail, K("cosC"), K("sinC"), 12, 16,
                                [R(s, SQ + 192 * i, 192).rearrange("p (h d) -> p h d", h=12) for i in range(4)])
                last.then_inc(Q["qkC_ready"], 1)
                yield
                wait("TC1", u + 1)
                n = 128 * min(nh, 16)
                v.tensor_copy(R(s, QKT + 1024, n - 1024, 96), banks(4 * s, n, 96)[:, 1024:n]).then_inc(Q["TC1_d"], 1)
                yield
                yield from softmax(l, s, "C", C_QK ** -0.5, 1 + s)

            def both(group, l):
                a, b = group(l, 0), group(l, 1)
                for _ in a:
                    next(b)

            def residual(l, j, s, n, src, tmp):
                xs = x[:, s, 512 * n:512 * n + 512]
                link(TT(tmp, src, gate[:, s, j, 512 * n:512 * n + 512], ALU.mult))
                last = TT(xs, xs, tmp, ALU.add)
                if n == 1:
                    last.then_inc(Q["x_done"], 1)
                    wait("x_done", 4 * l + 2 * j + s + 1)
                else:
                    link(last)

            def out_proj(l):
                for s in range(2):
                    wait("o_T", 2 * l + s + 1)
                    v.tensor_copy(R(s, QKT + 512, 512), bank(4 * s + 1)).then_inc(Q["oT_d"], 1)
                for n in range(2):
                    for s in range(2):
                        if s == 0:
                            wait("out_mm", 2 * l + n + 1)
                        else:
                            summed(dve, first["out", l] + 2 * n + 1)
                        residual(l, 0, s, n, bank(4 * s + 2 + n), R(s, SQ, 512))

            def dense_ffn():
                split_lo(first["w3", 0])
                for f in range(N_FF):
                    if f + 1 < N_FF:
                        split_lo(first["w1", f + 1])
                    for s in range(2):
                        wait("silu_ready", 2 * f + s + 1)
                        TT(hid[s][:, 0:FF], hid[s][:, 0:FF], bank(2 * (f % 2) + s, FF, a=FF), ALU.mult)\
                            .then_inc(Q["hid_ready"], 1)
                    if f + 1 < N_FF:
                        split_lo(first["w3", f + 1])
                    for s in range(2):
                        wait("hT_hi", 2 * f + s + 1)
                        a = slice(256 * (f % 2), 256 * (f % 2) + 256)
                        TT(t_lo[:, s, a], bank(2 * (f % 2) + s, 256), t_hi[:, s, a].bitcast(f32), ALU.subtract)\
                            .then_inc(Q["hT_ready"], 1)
                    split_lo(first["w2", f])
                summed(dve, first["w2", N_FF - 1])
                for s in range(2):
                    for n in range(2):
                        residual(0, 1, s, n, bank(4 + 2 * s + n), hid[0])

            def routing():
                for s in range(2):
                    wait("xn_T", s + 1)
                    v.tensor_copy(xr[:, s, 512:1024], bank(4 * s + 1)).then_inc(Q["xn_d"], 1)
                    wait("logits_mm", s + 1)
                    lg, v8, i8, idx = c_(s, "lg"), c_(s, "v8"), c_(s, "i8").bitcast(u32), c_(s, "if")
                    link(v.tensor_copy(lg, bank(4 * s + 2, 8)))
                    link(v.max(v8, lg))
                    link(v.max_index(i8, v8, lg))
                    v.tensor_copy(idx, i8[:, 0:2])
                    TT(c_(s, "e2"), v8[:, 1:2], v8[:, 0:1], ALU.subtract).then_inc(Q["gap_ready"], 1)
                    wait("gap_exp", s + 1)
                    link(TS(c_(s, "w1"), c_(s, "e2"), 1.0, None, ALU.add))
                    link(v.reciprocal(c_(s, "w1"), c_(s, "w1")))
                    link(TT(c_(s, "w2"), c_(s, "w1"), c_(s, "e2"), ALU.mult))
                    i1, i2 = idx[:, 0:1], idx[:, 1:2]
                    TS(c_(s, "eq"), K("iota8"), i2, None, ALU.is_equal)
                    TS(c_(s, "gt"), K("iota8"), i1, c_(s, "w1"), ALU.is_equal, ALU.mult)
                    link(TS(c_(s, "sel"), K("iota8"), i1, None, ALU.is_equal))
                    STT(c_(s, "gt"), c_(s, "eq"), c_(s, "w2"), c_(s, "gt"), ALU.mult, ALU.add)
                    TT(c_(s, "sel"), c_(s, "sel"), c_(s, "eq"), ALU.add).then_inc(Q["sel_ready"], 1)
                wait("sel_ready", 2)
                wait("pos_mm", 1)
                for s in range(2):
                    link(STT(c_(s, "posm"), bank(3, 8, a=8 * s), 1.0, c_(s, "sel"), ALU.add, ALU.mult))
                    link(TS(c_(s, "posm"), c_(s, "posm"), -1.0, None, ALU.add))
                link(RED(c_(0, "cnt"), bank(3, 8, a=16), AX.X, ALU.max))
                link(TS(c_(0, "cnt"), c_(0, "cnt"), float(TOK), 1.0, ALU.is_gt, ALU.add))
                v.tensor_copy(n_pass[:, :], c_(0, "cnt")).then_inc(Q["pass_ready"], 1)

            def experts():
                v.memset(acc, 0.0).then_inc(Q["acc_done"], 1)
                wait("pass_ready", 1)
                passes = dve.value_load(n_pass[0:1, 0:1], min_val=1, max_val=2)
                with dve.Fori(0, passes) as p:
                    with dve.Fori(0, N_EXP) as e:
                        it = p * N_EXP + e

                        def wait_it(name, per, n):
                            dve.wait_ge(Q[name], it * per + n)

                        for s in range(2):
                            pos = c_(s, "posm")[:, bass.ds(e, 1)]
                            TS(P[:, s, :], K("iota"), pos, None, ALU.is_equal)
                            last = TS(PG[:, s, :], K("iota"), pos, c_(s, "gt")[:, bass.ds(e, 1)], ALU.is_equal, ALU.mult)
                        last.then_inc(Q["P_ready"], 1)

                        def lo(kind, f, half):
                            j = expert_at[kind, f, half]
                            dve.wait_ge(hi_ready, it * PER_EXPERT + (N_SPLIT + j + 1))
                            dve.wait_ge(slot_used, it * PER_EXPERT + (W0 + j - 3 + 1))
                            TT(w_lo(j, 3), slot(W0 + j), w_hi(j).bitcast(f32), ALU.subtract).then_inc(split_done, 1)

                        def turned(f):
                            wait_it("e_hT_hi", N_FE, f + 1)
                            TT(t_lo[:, f % 2, :], bank(6 + f % 2), t_hi[:, f % 2, :].bitcast(f32), ALU.subtract)\
                                .then_inc(Q["e_hT"], 1)

                        lo("w1", 0, 0)
                        lo("w1", 0, 1)
                        for half in range(2):
                            wait_it("xe_hi", 2, half + 1)
                            k = slice(4 * half, 4 * half + 4)
                            TT(xe_lo[:, k, :].rearrange("p k t -> p (k t)"), bank(6 + half),
                               xe_hi[:, k, :].rearrange("p k t -> p (k t)").bitcast(f32), ALU.subtract)\
                                .then_inc(Q["xe_ready"], 1)
                        lo("w3", 0, 0)
                        for f in range(N_FE):
                            lo("w3", f, 1)
                            if f:
                                turned(f - 1)
                                lo("w2", f - 1, 0)
                                lo("w2", f - 1, 1)
                            wait_it("e_silu", N_FE, f + 1)
                            summed(dve, W0 + expert_at["w3", f, 1], it)
                            TT(hid[f % 2], hid[f % 2], bank(2 * (f % 2) + 1), ALU.mult).then_inc(Q["e_hid"], 1)
                            if f + 1 < N_FE:
                                lo("w1", f + 1, 0)
                                lo("w1", f + 1, 1)
                                lo("w3", f + 1, 0)
                        lo("w2", N_FE - 1, 0)
                        lo("w2", N_FE - 1, 1)
                        turned(N_FE - 1)
                        summed(dve, W0 + PER_EXPERT - 1, it)
                        v.tensor_copy(y_e[:, 512:1024], bank(5)).then_inc(Q["y_d"], 1)
                        wait_it("acc_done", 4, 1)
                        for i in range(4):
                            wait_it("scat_mm", 4, i + 1)
                            TT(acc[:, i, :], acc[:, i, :], bank(i), ALU.add).then_inc(Q["acc_done"], 1)
                    v.tensor_scalar(K("iota"), K("iota"), float(TOK), None, ALU.add).then_inc(Q["places_moved"], 1)
                    dve.wait_ge(Q["places_moved"], p + 1)
                for s in range(2):
                    for n in range(2):
                        residual(1, 1, s, n, acc[:, 2 * s + n, :], hid[0])

            for l in range(DEPTH):
                norm(l, 0, 0)
                norm(l, 0, 1)
                modulation(l)
                norm_out(l, 0, 0)
                norm_out(l, 0, 1)
                if l == 0:
                    dve.wait_ge(small_in, 16 * N_SMALL)
                both(group_A, l)
                both(group_B, l)
                both(group_C, l)
                out_proj(l)
                norm(l, 1, 0)
                norm(l, 1, 1)
                if l == 0:
                    split_lo(first["w1", 0])
                norm_out(l, 1, 0)
                norm_out(l, 1, 1)
                if l == 0:
                    dense_ffn()
                else:
                    routing()
                    experts()


INPUTS = ['x_prompt', 'x_sample', 'c', 'cache_swa_k', 'cache_swa_v', 'cache_mla_ckv', 'cache_mla_krope',
          'state_mlstm_C', 'state_mlstm_n', 'state_mlstm_m', 'c_ctx', 'ada_w', 'ada_b', 'norm1_g', 'norm2_g', 'w_in',
          'a_qn_g', 'a_kn_g', 'a_sink', 'b_gate_b', 'b_hn_g', 'c_qa_g', 'c_kva_g', 'c_wuq', 'c_wukv', 'c_qn_g',
          'c_kn_g', 'w_out', 'ffn_w1', 'ffn_w3', 'ffn_w2', 'moe_router', 'moe_w1', 'moe_w3', 'moe_w2']
OUTPUTS = [("y_prompt", (1, TOK, D)), ("y_sample", (1, TOK, D)),
           ("new_swa_k", (1, DEPTH, TOK, A_KV, HD)), ("new_swa_v", (1, DEPTH, TOK, A_KV, HD)),
           ("new_mla_ckv", (1, DEPTH, TOK, C_KVR)), ("new_mla_krope", (1, DEPTH, TOK, C_ROPE)),
           ("new_mlstm_C", (1, DEPTH, 2, B_H, HD, HD)), ("new_mlstm_n", (1, DEPTH, 2, B_H, HD)),
           ("new_mlstm_m", (1, DEPTH, 2, B_H))]


def kernel(**inputs):
    import concourse.bacc as bacc
    from concourse.bass_utils import run_bass_kernel_spmd

    nc = bacc.Bacc("TRN2", target_bir_lowering=False, num_devices=1)
    arrays = {f"in_{n}": np.ascontiguousarray(inputs[n]) for n in INPUTS}
    arrays["in_consts"] = constants()
    ins = {n[3:]: nc.dram_tensor(n, a.shape, mybir.dt.from_np(a.dtype), kind="ExternalInput").ap()
           for n, a in arrays.items()}
    outs = {n: nc.dram_tensor(f"out_{n}", shape, mybir.dt.float32, kind="ExternalOutput").ap() for n, shape in OUTPUTS}
    build_program(nc, ins, outs)
    r = run_bass_kernel_spmd(nc, [arrays], core_ids=[0])
    return tuple(r.results[0][f"out_{n}"] for n, _ in OUTPUTS)
```

```python
import concourse.bass as bass
from concourse import mybir
from contextlib import ExitStack
import numpy as np

D = 1024
TOK = 128
DEPTH = 2
KD = D // 128
HD = 64
A_H, A_KV, A_G = 6, 2, 3
B_H = 4
C_H, C_NOPE, C_ROPE, C_V = 6, 64, 32, 64
C_QK = C_NOPE + C_ROPE
C_QR, C_KVR = 256, 128
SIZES = (A_H * HD, A_KV * HD, A_KV * HD, 256, 256, 256, 256, 4 * B_H, C_QR, C_KVR, C_ROPE)
(AQ, AK, AV, BQ, BK, BV, BO, BG, CQ, CKV, CKR), D_IN = [sum(SIZES[:i]) for i in range(11)], sum(SIZES)
D_FF, N_EXP, D_FFE = 2816, 8, 3584
EPS = 1e-6
GRID_W, THETA, BIG = 64, 10000.0, 1e30

IN_CUTS = [0, 420, 840, 1260, 1680, D_IN]
FF = 256
N_FF = D_FF // FF
FE = 512
N_FE = D_FFE // FE
SLOT, N_SLOT = 2048, 7
PER_EXPERT = 6 * N_FE

CONST = {}
_at = 0
for _n, _w in (("ident", 128), ("s_le_t", 128), ("s_ge_t", 128), ("s_lt_t", 128), ("iota", 128),
               ("mask", 256), ("sum5", 2), ("cosA", 32), ("sinA", 32), ("cosC", 16), ("sinC", 16), ("iota8", 8)):
    CONST[_n] = (_at, _at + _w)
    _at += _w
N_CONST = _at

GAIN = {}
_at = 0
for _n, _w in (("a_qn_g", 64), ("a_kn_g", 64), ("c_qa_g", 256), ("c_kva_g", 128), ("c_qn_g", 96), ("c_kn_g", 96),
               ("b_hn_g", 64), ("b_gate_b", 16), ("a_sink", 6), ("m0", 8)):
    GAIN[_n] = (_at, _at + _w)
    _at += _w
N_GAIN = _at


def constants():
    t = np.zeros((128, N_CONST), np.float32)
    i = np.arange(128)

    def put(name, what):
        t[:what.shape[0], CONST[name][0]:CONST[name][1]] = what

    put("ident", np.eye(128))
    put("s_le_t", i[:, None] <= i[None, :])
    put("s_ge_t", i[:, None] >= i[None, :])
    put("s_lt_t", i[:, None] < i[None, :])
    put("iota", np.repeat(i[None, :], 128, 0))
    put("mask", BIG * np.concatenate([i[:, None] > i[None, :], i[:, None] < i[None, :]], 1))
    put("sum5", np.array([[1, 0], [0, 1], [1, 0], [0, 1], [1, 1]]))
    put("iota8", np.repeat(np.arange(8)[None, :], 128, 0))
    for name, dim in (("A", HD), ("C", C_ROPE)):
        n = dim // 4
        freq = (np.float32(THETA) ** (-np.arange(n, dtype=np.float32) / np.float32(n))).astype(np.float32)
        row, col = (i // GRID_W).astype(np.float32), (i % GRID_W).astype(np.float32)
        ang = np.concatenate([row[:, None] * freq, col[:, None] * freq], 1).astype(np.float32)
        put("cos" + name, np.cos(ang))
        put("sin" + name, np.sin(ang))
    return t


def build_program(nc, I, O):
    f32, i32, u32, f32r = mybir.dt.float32, mybir.dt.int32, mybir.dt.uint32, mybir.dt.float32r
    ALU, ACT, AX = mybir.AluOpType, mybir.ActivationFunctionType, mybir.AxisListType
    ctx = ExitStack()
    with ctx:
        def sb(name, shape, dt=f32):
            return ctx.enter_context(nc.sbuf_tensor(name, shape, dt))

        def sem(name):
            return ctx.enter_context(nc.semaphore(name))

        ring = sb("ring", [128, N_SLOT, SLOT])
        x = sb("x", [128, 2, D])
        xr = sb("xr", [128, 2, D])
        xnT = sb("xnT", [128, KD, 2 * TOK])
        o = sb("o", [128, 2, D])
        crow, ngrow = o[0:2 * KD, 0, 0:128], o[0:4 * KD, 0, 128:256]
        cst = sb("cst", [128, N_CONST])
        gain = sb("gain", [128, DEPTH, N_GAIN])
        ctx_k = sb("ctx_k", [128, DEPTH, 128])
        ctx_v = sb("ctx_v", [128, DEPTH, 128])
        ctx_ckv = sb("ctx_ckv", [128, DEPTH, 128])
        ctx_kr = sb("ctx_kr", [128, DEPTH, C_ROPE])
        C0n0 = sb("C0n0", [128, DEPTH, 2, 2, HD + 1])
        m0row = sb("m0row", [8, 1 + DEPTH])
        gate = sb("gate", [128, 2, 2, D])
        modT = sb("modT", [128, 4, KD, 2])
        modS = sb("modS", [128, 2, KD, 2])
        cT = sb("cT", [128, 2 * KD])
        cT4 = sb("cT4", [128, KD, 4], f32r)
        ngT = sb("ngT", [128, 4 * KD])
        router = sb("router", [128, KD, N_EXP])
        SCR = 6912
        arena = sb("arena", [128, 2 * D_IN + 2 * SCR])
        h = arena[:, 0:2 * D_IN].rearrange("p (s c) -> p s c", s=2)
        scr = arena[:, 2 * D_IN:2 * D_IN + 2 * SCR].rearrange("p (s c) -> p s c", s=2)
        N_HI, N_PARTS = 3, 8 * SLOT
        parts = nc.alloc_sbuf_tensor_at("parts", [128, 2 * D_IN + 2 * SCR], f32r, offset=nc.lookup_mloc(arena).addr)
        places = arena[:, N_PARTS:N_PARTS + 6 * TOK].rearrange("p (a s t) -> p a s t", a=3, s=2)
        mod5 = sb("mod5", [5, 4, 512])
        small = sb("small", [128, 2, 288])
        ka_out = sb("ka_out", [128, 128])
        ckv_out = sb("ckv_out", [128, 128])
        c_lat = sb("c_lat", [128, 640])
        n_pass = sb("n_pass", [128, 1], i32)
        PS = ctx.enter_context(nc.psum_tensor("PS", [128, 8, 512], f32))

        def K(name, rows=128):
            return cst[0:rows, CONST[name][0]:CONST[name][1]]

        def G(l, name):
            return gain[:, l, GAIN[name][0]:GAIN[name][1]]

        def R(s, a, n, parts=128):
            return scr[0:parts, s, a:a + n]

        def SM(s, a, n, parts=128):
            return small[0:parts, s, a:a + n]

        def bank(b, n=512, parts=128, a=0):
            return PS[0:parts, b, a:a + n]

        def banks(b, n, parts=128):
            return PS[0:parts, :, :].rearrange("p b n -> p (b n)")[:, b * 512:b * 512 + n]

        ident = K("ident")

        def to_all(column):
            return column.broadcast_to([column.shape[0], 128])

        ones = to_all(K("s_le_t")[:, 127:128])

        SQ, QK, QKT, VC = 0, 1728, 3456, 5760
        V1, KW, KS, CSQ = QKT + 640, QKT + 900, QKT + 1412, QKT + 900
        ST = VC + 384
        xn_flat = xnT[:, :, :].rearrange("p k t -> p (k t)")
        hid = [xn_flat[:, 0:512], xn_flat[:, 512:1024]]
        y_e = xn_flat[:, 1024:2048]
        acc = o[:, :, :].rearrange("p s (n c) -> p (s n) c", c=512)
        SCAT_BANKS = (2, 3, 6, 7)
        P, PG, PGT = places[:, 0], places[:, 1], places[:, 2]

        def num_(s):
            return xr[:, s, 0:520]

        def sig_(s):
            return xr[:, s, 520:776]

        def h8_(s):
            return xn_flat[:, 1024 * s:1024 * s + 768]

        def cq_(s):
            return c_lat[:, 256 * s:256 * s + 256]

        def w_hi(i):
            return parts[:, SLOT * (i % N_HI):SLOT * (i % N_HI) + SLOT]

        def w_lo(i, n_lo):
            a = SLOT * (N_HI + i % n_lo)
            return parts[:, a:a + SLOT]

        a_hi = parts[:, 5 * SLOT:6 * SLOT].rearrange("p (k t) -> p k t", k=KD)
        a_lo = parts[:, 6 * SLOT:7 * SLOT].rearrange("p (k t) -> p k t", k=KD)
        xe_hi = parts[:, 6 * SLOT:6 * SLOT + 1024].rearrange("p (k t) -> p k t", k=KD)
        xe_lo = parts[:, 6 * SLOT + 1024:7 * SLOT].rearrange("p (k t) -> p k t", k=KD)
        t_hi = parts[:, 7 * SLOT:7 * SLOT + 1024].rearrange("p (b c) -> p b c", b=2)
        t_lo = parts[:, 7 * SLOT + 1024:8 * SLOT].rearrange("p (b c) -> p b c", b=2)

        cols = {}
        at = 0
        for name, w in (("var", 18), ("rs", 18), ("tmp", 18), ("bits", 18), ("mx", 6), ("nm", 6), ("ls", 6), ("es", 6),
                        ("g16", 16), ("absf", 8), ("expl", 8), ("lf", 8), ("m16", 16), ("u", 8), ("em", 8), ("a", 8),
                        ("mo", 8), ("ws", 8), ("lg", 8), ("v8", 8), ("i8", 8), ("if", 2), ("sel", 8),
                        ("gt", 2 * N_EXP + 1), ("eq", 8), ("posm", 2 * N_EXP + 1),
                        ("ssq", 1), ("e2", 1), ("w1", 1), ("w2", 1), ("cnt", 1), ("rinv", 6)):
            cols[name] = (at, w)
            at += w
        assert at <= 288
        MFB = sb("MFB", [8, 2, 3, 128])

        def c_(s, name, n=None):
            a, w = cols[name]
            return SM(s, a, n or w)

        def slot(n, words=SLOT):
            return ring[:, n % N_SLOT, 0:words]

        loads = []

        def add(words, src, **dims):
            n = len(loads)
            loads.append((slot(n, words).rearrange("p (a c) -> p a c", **dims), src))
            return n

        def rows(w, k0, k1, c0, c1):
            return w[128 * k0:128 * k1, c0:c1].rearrange("(k p) c -> p k c", p=128)

        EARLY = 4
        IN_STEPS = [("in", 0, 0), ("in", 0, 1), ("ada", 4)]
        for i in range(8):
            IN_STEPS += [("in", 1 + i // 2, i % 2)] + ([("ada", 5 + i)] if i < 7 else [])
        IN_ORDER = [step[:2] for step in IN_STEPS if step[0] == "ada" or step[2] == 1]
        ADA_STEP = N_FF - 1 - EARLY
        first = {}

        def two_loads(kind, l, n):
            first[kind, l, n] = len(loads)
            w, (c0, c1) = (I["ada_w"][l], (512 * n, 512 * n + 512)) if kind == "ada" else (I["w_in"][l], IN_CUTS[n:n + 2])
            for k in (0, 4):
                add(4 * (c1 - c0), rows(w, k, k + 4, c0, c1), a=4)

        def ada_of(f):
            return f - ADA_STEP if 0 <= f - ADA_STEP < EARLY else None

        def row_bank(l, n):
            if n >= EARLY:
                return 4 + n % 2
            return 6 + n % 2 if l == 0 else 2 * ((ADA_STEP + n - 1) % 2) + 1

        for l in range(DEPTH):
            for kind, n in [("ada", n) for n in range(EARLY) if l == 0] + IN_ORDER:
                two_loads(kind, l, n)
            first["uq", l] = add(2 * C_H * C_QK, rows(I["c_wuq"][l], 0, 2, 0, C_H * C_QK), a=2)
            first["ukv", l] = add(C_H * 128, rows(I["c_wukv"][l], 0, 1, 0, C_H * 128), a=1)
            first["out", l] = len(loads)
            for n in range(2):
                for k in (0, 4):
                    add(2048, rows(I["w_out"][l], k, k + 4, 512 * n, 512 * n + 512), a=4)
            if l == 0:
                def w2_load(f):
                    first["w2", f] = add(2048, rows(I["ffn_w2"][0], 2 * f, 2 * f + 2, 0, D), a=2)

                for f in range(N_FF):
                    first["w1", f] = add(2048, rows(I["ffn_w1"][0], 0, KD, FF * f, FF * f + FF), a=KD)
                    first["w3", f] = add(2048, rows(I["ffn_w3"][0], 0, KD, FF * f, FF * f + FF), a=KD)
                    if ada_of(f) is not None:
                        two_loads("ada", 1, ada_of(f))
                    if f:
                        w2_load(f - 1)
                w2_load(N_FF - 1)
        W0 = len(loads)
        early = [[first["ada", l, n] + half for n in range(EARLY) for half in range(2)] for l in range(DEPTH)]
        late = [[first["ada", l, n] + half for n in range(EARLY, 12) for half in range(2)] for l in range(DEPTH)]
        common = early[0] + list(range(first["w1", 0], first["w2", N_FF - 1] + 1))
        split_loads = sorted(common + late[0] + late[1])
        split_at = {n: i for i, n in enumerate(split_loads)}
        N_SPLIT = len(split_loads)
        assert N_SPLIT % N_HI == 0 and PER_EXPERT % N_HI == 0
        hi_part, lo_part, hi_after, lo_after = {}, {}, {}, {}
        for i, n in enumerate(common):
            hi_part[n], lo_part[n] = w_hi(i), w_lo(i, 2)
            hi_after[n] = common[i - N_HI] if i >= N_HI else None
            lo_after[n] = common[i - 2] if i >= 2 else None
        for l in range(DEPTH):
            for i, n in enumerate(late[l]):
                a = 2 * D_IN + QK + 1024 + SLOT * (i % 2)
                hi_part[n], lo_part[n] = parts[:, a:a + SLOT], parts[:, SCR + a:SCR + a + SLOT]
                hi_after[n] = lo_after[n] = late[l][i - 2] if i >= 2 else early[l][-1]

        expert_order = []
        for f in range(N_FE):
            expert_order += [("w1", f, 0), ("w1", f, 1), ("w3", f, 0), ("w3", f, 1)]
            if f:
                expert_order += [("w2", f - 1, 0), ("w2", f - 1, 1)]
        expert_order += [("w2", N_FE - 1, 0), ("w2", N_FE - 1, 1)]
        expert_at = {key: j for j, key in enumerate(expert_order)}
        assert len(expert_order) == PER_EXPERT and PER_EXPERT % N_SLOT == 0
        FULL_PER_EXPERT = 16 * PER_EXPERT // N_SLOT

        slot_full = [sem(f"slot_full{i}") for i in range(N_SLOT)]
        slot_used = sem("slot_used")
        hi_ready = sem("hi_ready")
        split_done = sem("split_done")
        first_in, x_in = sem("first_in"), sem("x_in")
        small_in = [sem(f"small_in{l}") for l in range(DEPTH)]
        adab_in = [sem(f"adab_in{i}") for i in range(4)]
        out_sem = [sem("out_sem0"), sem("out_sem1")]
        state_out = [sem("state_out0"), sem("state_out1")]
        y_out = sem("y_out")
        dve_chain, act_chain = sem("dve_chain"), sem("act_chain")
        c_hi_ready, c_lo_ready = sem("c_hi_ready"), sem("c_lo_ready")
        setup_T, c_ready, ng_ready, zeros_ready = sem("setup_T"), sem("c_ready"), sem("ng_ready"), sem("zeros_ready")
        names = ["modrow_ready", "spread", "mod_ready", "gate_copied",
                 "ssq_ready", "xr_ready", "xr_T", "xnT_a", "xnT_d", "x_done",
                 "in_mm", "h_ready",
                 "qkA_ready", "TA", "TA_ready", "SA", "nmA", "PA", "PTA", "PTA_a", "PTA_d", "OA", "oA",
                 "cn_ready", "TC", "TC_ready", "C_mm", "C_heads", "C_headsx", "C_sq", "qkC_ready", "TC1", "TC1_a",
                 "TC1_d", "TC2", "TC2_a", "SC", "nmC", "PC", "PTC", "PTC_a", "PTC_d", "OC", "oC",
                 "absf_ready", "log_ready", "lf_ready", "bc_T", "u_ready", "qkB_T", "uT_S", "run_ready", "M_mm",
                 "Earg_ready", "E_ready", "last_mm", "WT_ready", "ws_arg", "ws_ready", "kw_ready", "num_mm",
                 "state_copied", "num_read", "o_T", "oT_a", "oT_d", "out_mm",
                 "up_mm", "silu_ready", "hid_ready", "hid_T", "hT_hi", "hT_ready", "xs_hi", "xs_ready",
                 "xn_T", "xn_a", "xn_d", "logits_mm", "gap_ready", "gap_exp", "sel_ready", "pos_mm", "pass_ready",
                 "P_ready", "gather_mm", "Pg_T", "xe_hi", "xe_ready", "Pg_a", "e_silu", "e_hid", "e_T", "e_hT_hi", "e_hT",
                 "y_a", "y_d", "scat_mm", "zeroed", "acc_done"]
        Q = {n: sem(n) for n in names}

        def summed(eng, n, it=None):
            eng.wait_ge(slot_used, n + 1 if it is None else it * PER_EXPERT + (n + 1))

        block = ctx.enter_context(nc.Block())

        @block.sync
        def _(sp):
            for n, (dst, src) in enumerate(loads):
                m = n - N_SLOT
                if m in split_at:
                    sp.wait_ge(split_done, split_at[m] + 1)
                elif m >= 0:
                    sp.wait_ge(slot_used, m + 1)
                sp.dma_start(dst, src).then_inc(slot_full[n % N_SLOT], 16)

            def expert_loads(e, it):
                for j, (kind, f, half) in enumerate(expert_order):
                    n = W0 + j
                    dst = slot(n)
                    if kind == "w2":
                        r0 = FE * f + 256 * half
                        src = I["moe_w2"][0][bass.ds(e, 1), r0:r0 + 256, :]
                        src = src.rearrange("e (k p) c -> p (e k) c", p=128)
                        dst = dst.rearrange("p (a c) -> p a c", a=2)
                    else:
                        w = I["moe_" + kind][0]
                        src = w[bass.ds(e, 1), 512 * half:512 * half + 512, FE * f:FE * f + FE]
                        src = src.rearrange("e (k p) c -> p (e k) c", p=128)
                        dst = dst.rearrange("p (a c) -> p a c", a=4)
                    if j < N_SLOT:
                        sp.wait_ge(slot_used, n - N_SLOT + 1)
                    sp.wait_ge(split_done, it * PER_EXPERT + (N_SPLIT + j - N_SLOT + 1))
                    sp.dma_start(dst, src).then_inc(slot_full[n % N_SLOT], 16)

            expert_loads(0, 0)
            sp.wait_ge(Q["pass_ready"], 1)
            passes = sp.value_load(n_pass[0:1, 0:1], min_val=1, max_val=2)
            with sp.Fori(1, passes * N_EXP) as it:
                expert_loads(it % N_EXP, it)
            sp.wait_ge(y_out, 32)
            for l in range(DEPTH):
                sp.wait_ge(out_sem[l], 16 * 4)
                sp.wait_ge(state_out[l], 16 * 3)

        N_FIRST = 5
        N_SMALL = len(GAIN) + 4 + 2 * 2 * 2 + 1

        @block.gpsimd
        def _(pool):
            pool.wait_ge(slot_full[2], 16)
            for l in range(DEPTH):
                def load(dst, src, **how):
                    pool.dma_start(dst, src, **how).then_inc(small_in[l], 16)

                for name in GAIN:
                    if name == "m0":
                        src = I["state_mlstm_m"][0:1, l, :, :].rearrange("a d h -> a (d h)")
                    else:
                        src = I[name][l:l + 1, :]
                    load(G(l, name), src.broadcast_to([128, src.shape[1]]))
                load(ctx_k[:, l, :], I["cache_swa_k"][0, l].rearrange("t g d -> t (g d)"))
                load(ctx_v[:, l, :], I["cache_swa_v"][0, l].rearrange("t g d -> t (g d)"))
                load(ctx_ckv[:, l, :], I["cache_mla_ckv"][0, l])
                load(ctx_kr[:, l, :], I["cache_mla_krope"][0, l])
                for par in range(2):
                    for d in range(2):
                        dst = C0n0[64 * par:64 * par + 64, l, d, :, :]
                        load(dst[:, :, 0:HD], I["state_mlstm_C"][0, l, d, par:B_H:2].rearrange("h k v -> k h v"))
                        load(dst[:, :, HD:HD + 1],
                             I["state_mlstm_n"][0, l, d, par:B_H:2].rearrange("h (k o) -> k h o", o=1),
                             allow_slow_non_contiguous=True)
                load(m0row[:, 1 + l:2 + l], I["state_mlstm_m"][0, l].rearrange("d (h o) -> (d h) o", o=1))
            load(router[:, :, :], I["moe_router"][0].rearrange("(k p) e -> p k e", p=128))
            for l in range(DEPTH):
                u = 2 * l

                def store(dst, src, s=out_sem[l], **how):
                    pool.dma_start(dst, src, **how).then_inc(s, 16)

                pool.wait_ge(Q["h_ready"], 10 * l + 9)
                store(O["new_swa_v"][0, l].rearrange("t g d -> t (g d)"), h[:, 0, AV:AV + 128])
                store(O["new_mla_krope"][0, l], h[:, 0, CKR:CKR + C_ROPE])
                pool.wait_ge(Q["qkA_ready"], u + 1)
                store(O["new_swa_k"][0, l].rearrange("t g d -> t (g d)"), ka_out[:, :])
                pool.wait_ge(Q["state_copied"], l + 1)
                st = R(0, ST, 8 * (HD + 1), 64).rearrange("p (c n) -> p c n", c=8)
                store(O["new_mlstm_C"][0, l].rearrange("d h k v -> k (d h) v"), st[:, :, 0:HD], state_out[l])
                store(O["new_mlstm_n"][0, l].rearrange("d h (k o) -> k (d h) o", o=1), st[:, :, HD:HD + 1], state_out[l],
                      allow_slow_non_contiguous=True)
                store(O["new_mlstm_m"][0:1, l].rearrange("a d h -> a (d h)"), c_(0, "mo")[0:1, :], state_out[l])
                pool.wait_ge(Q["cn_ready"], u + 1)
                store(O["new_mla_ckv"][0, l], ckv_out[:, :])
            for s, name in ((0, "y_prompt"), (1, "y_sample")):
                pool.wait_ge(Q["x_done"], 7 + s)
                pool.dma_start(O[name][0], x[:, s, :]).then_inc(y_out, 16)

        @block.tensor
        def _(pe):
            mm, tr = nc.tensor.matmul, nc.tensor.transpose

            def wait(name, v):
                pe.wait_ge(Q[name], v)

            def weights(n):
                pe.wait_ge(slot_full[n % N_SLOT], 16 * (n // N_SLOT + 1))
                return loads[n][0]

            def split_weights(n):
                pe.wait_ge(split_done, split_at[n] + 1)
                k = loads[n][0].shape[1]
                return [w.rearrange("p (a c) -> p a c", a=k) for w in (hi_part[n], lo_part[n])]

            def mm3(out, s_hi, s_lo, m_hi, m_lo, start, stop):
                mm(out, s_hi, m_hi, start=start, stop=False)
                mm(out, s_hi, m_lo, start=False, stop=False)
                return mm(out, s_lo, m_hi, start=False, stop=stop)

            def T(out, src):
                k = src.shape[0]
                return tr(out, src, ident[0:k, 0:k])

            pe.wait_ge(first_in, 16 * N_FIRST)
            T(bank(0, 2 * KD), crow[:, :])
            T(bank(1, 4 * KD), ngrow[:, :]).then_inc(setup_T, 1)
            pe.wait_ge(c_lo_ready, 1)

            def rows_of(l, n):
                b = row_bank(l, n)
                if n >= EARLY + 2 or l == 0 and 2 <= n < EARLY:
                    wait("modrow_ready", 12 * l + n - 1)
                for half in range(2):
                    hi, lo = split_weights(first["ada", l, n] + half)
                    for k in range(4):
                        c4 = cT4[:, 4 * half + k, :]
                        mm(bank(b, parts=4), c4, hi[:, k, :], start=(half == 0 and k == 0), stop=False)
                        last = mm(bank(b, parts=4), c4, lo[:, k, :], start=False, stop=(half == 1 and k == 3))
                    last.then_inc(slot_used, 1)

            def spread(l, n):
                g = 12 * l + n
                wait("modrow_ready", g + 1)
                pe.wait_ge(adab_in[g % 4], 16 * (g // 4 + 1))
                j, half = n // 2, n % 2
                rows5 = mod5[:, g % 4, :]
                if j in (2, 5):
                    if n == 10:
                        wait("mod_ready", 2 * l + 2)
                    else:
                        wait("gate_copied", 8 * l + 4 * (j // 5) + 2 * half)
                    for s in range(2):
                        last = mm(bank(6 + s), to_all(K("sum5", 5)[:, s:s + 1]), rows5, start=True, stop=True)
                else:
                    if n == 6:
                        wait("gate_copied", 8 * l + 4)
                    jj = j if j < 2 else j - 3
                    for c in range(4):
                        a = 16 * jj + 2 * (4 * half + c)
                        last = mm(bank(2 if n < EARLY else 6, 2, a=a), rows5[:, 128 * c:128 * c + 128], K("sum5", 5),
                                  start=True, stop=True)
                last.then_inc(Q["spread"], 1)

            def modulation(l):
                for n in range(EARLY):
                    if l == 0:
                        rows_of(l, n)
                        if n:
                            spread(l, n - 1)
                    else:
                        spread(l, n)
                norm_T(l, 0, 0)
                norm_T(l, 0, 1)
                if l == 0:
                    spread(l, EARLY - 1)
                wait("mod_ready", 2 * l + 1)

            def norm_T(l, j, s):
                wait("xr_ready", 4 * l + 2 * j + s + 1)
                for k in range(KD):
                    last = T(bank(4 * s + k // 4, 128, a=128 * (k % 4)), xr[:, s, 128 * k:128 * k + 128])
                last.then_inc(Q["xr_T"], 1)

            def norm_done(l, j):
                wait("xnT_a", 4 * l + 2 * j + 2)
                wait("xnT_d", 4 * l + 2 * j + 2)

            def in_proj(l):
                def unit(n, s):
                    c = IN_CUTS[n + 1] - IN_CUTS[n]
                    i = 2 * n + s
                    if i >= 4:
                        wait("h_ready", 10 * l + i - 3)
                    for k in range(KD):
                        w = weights(first["in", l, n] + k // 4)
                        last = mm(bank(i % 4, c), xnT[:, k, 128 * s:128 * s + 128], w[:, k % 4, :],
                                  start=(k == 0), stop=(k == KD - 1))
                        if s == 1 and k == 3:
                            last.then_inc(slot_used, 1)
                    last.then_inc(Q["in_mm"] if s == 0 else slot_used, 1)

                behind = None
                for kind, n, *s in IN_STEPS:
                    if kind == "in":
                        unit(n, *s)
                        if behind:
                            spread(l, behind)
                            behind = None
                    else:
                        rows_of(l, n)
                        behind = n

            def scores_softmax_out(l, s, X, qT, kT, v, n_kt):
                u = 2 * l + s
                b0 = 4 * s
                for hi in range(6):
                    for kt in range(n_kt):
                        a = (hi % 3 * n_kt + kt) * 128
                        last = mm(bank(b0 + hi // 3 * 2 + a // 512, 128, a=a % 512), qT(hi), kT(hi, kt),
                                  start=True, stop=True)
                last.then_inc(Q["S" + X], 1)
                yield
                wait("P" + X, u + 1)
                p = R(s, SQ, 6 * n_kt * 128)
                for i in range(6 * n_kt):
                    last = T(bank(b0 + i // 4, 128, a=128 * (i % 4)), p[:, 128 * i:128 * i + 128])
                last.then_inc(Q["PT" + X], 1)
                yield
                wait("PT" + X + "_a", u + 1)
                wait("PT" + X + "_d", u + 1)
                pT = R(s, QK, 6 * n_kt * 128)
                for hi in range(6):
                    for kt in range(n_kt):
                        i = hi * n_kt + kt
                        last = mm(bank(b0 + 3, HD, a=HD * hi), pT[:, 128 * i:128 * i + 128], v(hi, kt),
                                  start=(kt == 0), stop=(kt == n_kt - 1))
                last.then_inc(Q["O" + X], 1)
                yield

            def group_A(l, s):
                u = 2 * l + s
                wait("qkA_ready", u + 1)
                wait("h_ready", 10 * l + 10)
                wait("gate_copied", 8 * l + 8)
                qk = R(s, QK + 512 * s, 512)
                b0 = 4 * s
                for r in range(3):
                    T(bank(b0, 128, a=128 * r), qk[:, 128 * r:128 * r + 128])
                if s == 0:
                    last = T(bank(b0, 128, a=384), ka_out[:, :])
                else:
                    T(bank(b0, 128, a=384), qk[:, 384:512])
                    last = T(bank(b0 + 1, 128), ctx_k[:, l, :])
                last.then_inc(Q["TA"], 1)
                yield
                wait("TA_ready", u + 1)
                t = R(s, QKT, 640)

                def qT(hi):
                    g, r = hi // 3, hi % 3
                    return t[64 * g:64 * g + 64, 128 * r:128 * r + 128]

                def kT(hi, kt):
                    g = hi // 3
                    a = 384 if kt == 0 else 512
                    return t[64 * g:64 * g + 64, a:a + 128]

                def v(hi, kt):
                    g = hi // 3
                    return h[:, s, AV + 64 * g:AV + 64 * g + 64] if kt == 0 else ctx_v[:, l, 64 * g:64 * g + 64]

                yield from scores_softmax_out(l, s, "A", qT, kT, v, 1 + s)

            def group_B(l, s):
                u = 2 * l + s
                b0 = 4 * s
                wait("lf_ready", l + 1)
                lf = c_(s, "lf")
                mm(bank(b0, 4), K("s_le_t"), lf[:, 0:4], start=True, stop=True)
                mm(bank(b0, 4, a=4), K("s_ge_t"), lf[:, 4:8], start=True, stop=True)
                for i in range(2):
                    T(bank(b0 + 1, 128, a=128 * i), h[:, s, BQ + 128 * i:BQ + 128 * i + 128])
                for i in range(2):
                    last = T(bank(b0 + 1, 128, a=256 + 128 * i), R(s, KS, 256)[:, 128 * i:128 * i + 128])
                last.then_inc(Q["bc_T"], 1)
                yield
                wait("u_ready", u + 1)
                wait("oA", u + 1)
                T(bank(b0 + 2, 128, parts=8), c_(s, "u"))
                wait("qkB_T", u + 1)
                t = R(s, QKT, 512)

                def head(a, hh):
                    return t[64 * (hh % 2):64 * (hh % 2) + 64, a + 128 * (hh // 2):a + 128 * (hh // 2) + 128]

                for hh in range(B_H):
                    last = mm(bank(b0 + 3 * (hh % 2), 128, a=128 * (hh // 2)), head(256, hh), head(0, hh),
                              start=True, stop=True)
                last.then_inc(Q["uT_S"], 1)
                yield
                wait("run_ready", u + 1)
                run = MFB[:, s, :, :]
                for d in range(2):
                    mm(bank(b0, 4, a=256 + 4 * d), run[:, 1 + d, :], ident[0:8, 4 * d:4 * d + 4], start=True, stop=True)
                for c in range(8):
                    last = mm(bank(b0 + 1 + c // 4, 128, a=128 * (c % 4)), to_all(ident[0:8, c:c + 1]), run[:, 1 + c // 4, :],
                              start=True, stop=True)
                last.then_inc(Q["M_mm"], 1)
                yield
                if s == 0:
                    wait("Earg_ready", u + 1)
                    m16 = c_(s, "m16").rearrange("p (a c) -> p a c", a=2)
                    out = bank(b0, 16, a=288).rearrange("p (a c) -> p a c", a=2)
                    mm(out[:, :, 0:4], to_all(ident[:, 127:128]), m16[:, :, 0:4], start=True, stop=True)
                    mm(out[:, :, 4:8], to_all(ident[:, 0:1]), m16[:, :, 4:8], start=True, stop=True).then_inc(Q["last_mm"], 1)
                yield
                wait("WT_ready", u + 1)
                v1 = R(s, V1, 4 * 65).rearrange("p (h n) -> p h n", h=4)
                wT = R(s, QK, 1024)
                for c in range(8):
                    last = mm(bank(b0 + 1 + c // 4, 65, a=65 * (c % 4)), wT[:, 128 * c:128 * c + 128], v1[:, c % 4, :],
                              start=True, stop=True)
                if s == 1:
                    for c in range(8):
                        hh, d = c % 4, c // 4
                        p0 = 64 * (hh % 2)
                        last = mm(bank(b0 + 3 * (hh % 2), 65, a=65 * (2 * d + hh // 2)), head(0, hh),
                                  C0n0[p0:p0 + 64, l, d, hh // 2, :], start=True, stop=True)
                else:
                    wait("kw_ready", l + 1)
                    kw = R(0, KW, 512)
                    for c in range(8):
                        last = mm(bank(b0 if c >= 4 else b0 + 3, 65, parts=64, a=65 * (c % 4)),
                                  kw[:, 64 * c:64 * c + 64], v1[:, c % 4, :], start=True, stop=True)
                last.then_inc(Q["num_mm"], 1)
                yield

            def group_C(l, s):
                u = 2 * l + s
                b0 = 4 * s
                wait("cn_ready", u + 1)
                wait("num_read", u + 1)
                if s == 0:
                    wait("state_copied", l + 1)
                cn = cq_(s)
                T(bank(b0 + 3, 128), cn[:, 0:128])
                T(bank(b0 + 3, 128, a=128), cn[:, 128:256])
                if s == 0:
                    last = T(bank(b0 + 3, 128, a=256), ckv_out[:, :])
                else:
                    T(bank(b0 + 3, 128, a=256), c_lat[:, 512:640])
                    last = T(bank(b0 + 3, 128, a=384), ctx_ckv[:, l, :])
                last.then_inc(Q["TC"], 1)
                yield
                wait("TC_ready", u + 1)
                t = R(s, QKT, 512)
                uq, ukv = weights(first["uq", l]), weights(first["ukv", l])
                for n in range(2):
                    for k in range(2):
                        last = mm(bank(b0 + n, 288), t[:, 128 * k:128 * k + 128], uq[:, k, 288 * n:288 * n + 288],
                                  start=(k == 0), stop=(k == 1))
                if s == 1:
                    last.then_inc(slot_used, 1)
                for n in range(2):
                    last = mm(bank(b0 + 2 + n, 384), t[:, 256:384], ukv[:, 0, 384 * n:384 * n + 384], start=True, stop=True)
                last.then_inc(Q["C_mm"], 1)
                yield
                if s == 1:
                    wait("C_heads", u + 1)
                    for n in range(2):
                        last = mm(bank(b0 + 2 + n, 384), t[:, 384:512], ukv[:, 0, 384 * n:384 * n + 384],
                                  start=True, stop=True)
                    last.then_inc(slot_used, 1)
                yield
                wait("qkC_ready", u + 1)
                nh = 12 + 6 * s
                qk = R(s, QK, nh * 96).rearrange("p (h d) -> p h d", h=nh)
                for i in range(min(nh, 16)):
                    last = T(bank(b0 + i // 4, 128, 96, 128 * (i % 4)), qk[:, i, :])
                last.then_inc(Q["TC1"], 1)
                yield
                wait("TC1_a", u + 1)
                wait("TC1_d", u + 1)
                if s == 1:
                    for i in range(16, nh):
                        last = T(bank(b0, 128, 96, 128 * (i % 4)), qk[:, i, :])
                    last.then_inc(Q["TC2"], 1)
                    wait("TC2_a", l + 1)
                qkT = R(s, QKT, nh * 128, 96)

                def qT(hi):
                    return qkT[:, 128 * hi:128 * hi + 128]

                def kT(hi, kt):
                    return qkT[:, 128 * (6 + 6 * kt + hi):128 * (7 + 6 * kt + hi)]

                def v(hi, kt):
                    return R(s, VC + 384 * kt + 64 * hi, 64)

                yield from scores_softmax_out(l, s, "C", qT, kT, v, 1 + s)

            def both(group, l):
                a, b = group(l, 0), group(l, 1)
                for _ in a:
                    next(b)

            def out_proj(l):
                for s in range(2):
                    wait("oC", 2 * l + s + 1)
                    for k in range(KD):
                        last = T(bank(4 * s + k // 4, 128, a=128 * (k % 4)), o[:, s, 128 * k:128 * k + 128])
                    last.then_inc(Q["o_T"], 1)
                for n in range(2):
                    for s in range(2):
                        if n == 0:
                            wait("oT_a", 2 * l + s + 1)
                            wait("oT_d", 2 * l + s + 1)
                        t = R(s, QKT, 1024)
                        for k in range(KD):
                            w = weights(first["out", l] + 2 * n + k // 4)
                            last = mm(bank(4 * s + 2 + n), t[:, 128 * k:128 * k + 128], w[:, k % 4, :],
                                      start=(k == 0), stop=(k == KD - 1))
                            if s == 1 and k == 3:
                                last.then_inc(slot_used, 1)
                        last.then_inc(Q["out_mm"] if s == 0 else slot_used, 1)

            def dense_ffn():
                def up(kind, f):
                    hi, lo = split_weights(first[kind, f])
                    for s in range(2):
                        if kind == "w1" and f == 0:
                            wait("xs_ready", s + 1)
                        if kind == "w1" and f >= 2:
                            wait("hT_ready", 2 * (f - 2) + s + 1)
                        if kind == "w1" and s == 1 and ada_of(f - 1) is not None:
                            wait("modrow_ready", 12 + ada_of(f - 1) + 1)
                        for k in range(KD):
                            t = slice(128 * s, 128 * s + 128)
                            last = mm3(bank(2 * (f % 2) + s, FF, a=FF * (kind == "w3")), a_hi[:, k, t], a_lo[:, k, t],
                                       hi[:, k, :], lo[:, k, :], k == 0, k == KD - 1)
                        if s == 0 and kind == "w3":
                            last.then_inc(Q["up_mm"], 1)
                    last.then_inc(slot_used, 1)

                def turn(f):
                    for s in range(2):
                        wait("hid_ready", 2 * f + s + 1)
                        for c in range(2):
                            last = T(bank(2 * (f % 2) + s, 128, a=128 * c), hid[s][:, 128 * c:128 * c + 128])
                        last.then_inc(Q["hid_T"], 1)

                def down(f):
                    hi, lo = split_weights(first["w2", f])
                    for s in range(2):
                        wait("hT_ready", 2 * f + s + 1)
                        for n in range(2):
                            for c in range(2):
                                a = 256 * (f % 2) + 128 * c
                                cols = slice(512 * n, 512 * n + 512)
                                last = mm3(bank(4 + 2 * s + n), t_hi[:, s, a:a + 128], t_lo[:, s, a:a + 128],
                                           hi[:, c, cols], lo[:, c, cols], f == 0 and c == 0, f == N_FF - 1 and c == 1)
                    last.then_inc(slot_used, 1)

                for f in range(N_FF):
                    up("w1", f)
                    if f:
                        turn(f - 1)
                    up("w3", f)
                    if ada_of(f) is not None:
                        wait("hT_ready", 2 * f)
                        rows_of(1, ada_of(f))
                    if f:
                        down(f - 1)
                turn(N_FF - 1)
                down(N_FF - 1)

            def routing():
                for s in range(2):
                    for k in range(KD):
                        last = mm(bank(4 * s + 2, N_EXP), xnT[:, k, 128 * s:128 * s + 128], router[:, k, :],
                                  start=(k == 0), stop=(k == KD - 1))
                last.then_inc(Q["logits_mm"], 1)
                for s in range(2):
                    for k in range(KD):
                        last = T(bank(4 * s + k // 4, 128, a=128 * (k % 4)), xnT[:, k, 128 * s:128 * s + 128])
                    last.then_inc(Q["xn_T"], 1)
                wait("sel_ready", 1)
                sel = [c_(0, "sel"), c_(1, "sel")]
                mm(bank(3, 8), K("s_lt_t"), sel[0], start=True, stop=True)
                mm(bank(3, 8, a=8), K("s_lt_t"), sel[1], start=True, stop=False)
                mm(bank(3, 8, a=8), ones, sel[0], start=False, stop=True)
                mm(bank(3, 8, a=16), ones, sel[0], start=True, stop=False)
                mm(bank(3, 8, a=16), ones, sel[1], start=False, stop=True).then_inc(Q["pos_mm"], 1)

            def experts():

                def gather():
                    for half in range(2):
                        for k in range(4):
                            for s in range(2):
                                a = 512 * half + 128 * k
                                last = mm(bank(2 + half, 128, a=128 * k), xr[:, s, a:a + 128], P[:, s, :],
                                          start=(s == 0), stop=(s == 1))
                        last.then_inc(Q["gather_mm"], 1)

                def scatter():
                    for s in range(2):
                        for n in range(2):
                            mm(bank(SCAT_BANKS[2 * s + n]), PGT[:, s, :], y_e[:, 512 * n:512 * n + 512], start=True, stop=True)\
                                .then_inc(Q["scat_mm"], 1)

                wait("xn_a", 2)
                wait("xn_d", 2)
                wait("P_ready", 1)
                gather()
                wait("pass_ready", 1)
                passes = pe.value_load(n_pass[0:1, 0:1], min_val=1, max_val=2)
                with pe.Fori(0, passes) as p:
                    with pe.Fori(0, N_EXP) as e:
                        it = p * N_EXP + e

                        def wait_it(name, per, v):
                            pe.wait_ge(Q[name], it * per + v)

                        def expert_weights(key, a):
                            j = expert_at[key]
                            pe.wait_ge(split_done, it * PER_EXPERT + (N_SPLIT + j + 1))
                            return [w.rearrange("p (a c) -> p a c", a=a) for w in (w_hi(j), w_lo(j, 3))]

                        def up(kind, f):
                            b = 2 * (f % 2) + (kind == "w3")
                            if f >= 2:
                                wait_it("e_hid", N_FE, f - 1)
                            elif f == 1:
                                wait_it("acc_done", 4, 1 + (kind == "w3"))
                            for half in range(2):
                                if f == 0 and kind == "w1":
                                    wait_it("xe_ready", 2, half + 1)
                                hi, lo = expert_weights((kind, f, half), 4)
                                for k in range(4):
                                    last = mm3(bank(b), xe_hi[:, 4 * half + k, :], xe_lo[:, 4 * half + k, :],
                                               hi[:, k, :], lo[:, k, :], half == 0 and k == 0, half == 1 and k == 3)
                                last.then_inc(slot_used, 1)

                        def turn(f):
                            wait_it("e_hid", N_FE, f + 1)
                            if f >= 2:
                                wait_it("e_hT", N_FE, f - 1)
                            if f == 0:
                                wait_it("acc_done", 4, 3)
                            if f == 1:
                                wait_it("Pg_a", 1, 1)
                            for c in range(4):
                                last = T(bank(6 + f % 2, 128, a=128 * c), hid[f % 2][:, 128 * c:128 * c + 128])
                            last.then_inc(Q["e_T"], 1)

                        def down(f):
                            wait_it("e_hT", N_FE, f + 1)
                            for half in range(2):
                                hi, lo = expert_weights(("w2", f, half), 2)
                                for n in range(2):
                                    for c in range(2):
                                        a = 128 * (2 * half + c)
                                        cols = slice(512 * n, 512 * n + 512)
                                        last = mm3(bank(4 + n), t_hi[:, f % 2, a:a + 128], t_lo[:, f % 2, a:a + 128],
                                                   hi[:, c, cols], lo[:, c, cols], f == 0 and half == 0 and c == 0,
                                                   f == N_FE - 1 and half == 1 and c == 1)
                                last.then_inc(slot_used, 1)

                        up("w1", 0)
                        wait_it("y_a", 1, 1)
                        wait_it("y_d", 1, 1)
                        scatter()
                        up("w3", 0)
                        for f in range(1, N_FE):
                            up("w1", f)
                            turn(f - 1)
                            if f == 1:
                                wait_it("acc_done", 4, 4)
                                for s in range(2):
                                    last = T(bank(7, 128, a=128 * s), PG[:, s, :])
                                last.then_inc(Q["Pg_T"], 1)
                            up("w3", f)
                            if f == N_FE - 1:
                                wait_it("P_ready", 1, 2)
                                gather()
                                turn(f)
                            down(f - 1)
                        down(N_FE - 1)
                pe.wait_ge(Q["y_a"], passes * N_EXP + 1)
                pe.wait_ge(Q["y_d"], passes * N_EXP + 1)
                scatter()

            for l in range(DEPTH):
                modulation(l)
                norm_done(l, 0)
                in_proj(l)
                both(group_A, l)
                both(group_B, l)
                both(group_C, l)
                out_proj(l)
                norm_T(l, 1, 0)
                norm_T(l, 1, 1)
                norm_done(l, 1)
                if l == 0:
                    dense_ffn()
                else:
                    routing()
                    experts()

        @block.scalar
        def _(act):
            A = nc.scalar.activation
            chain = [0]

            def wait(name, v):
                act.wait_ge(Q[name], v)

            def link(ins):
                chain[0] += 1
                ins.then_inc(act_chain, 1)
                act.wait_ge(act_chain, chain[0])

            for dst, src, s in ((crow[0:KD, :], I["c_ctx"].rearrange("(k p) -> k p", p=128), first_in),
                                (crow[KD:2 * KD, :], I["c"].rearrange("a (k p) -> (a k) p", p=128), first_in),
                                (cst[:, :], I["consts"], first_in),
                                (ngrow[0:2 * KD, :], I["norm1_g"].rearrange("l (k p) -> (l k) p", p=128), first_in),
                                (ngrow[2 * KD:4 * KD, :], I["norm2_g"].rearrange("l (k p) -> (l k) p", p=128), first_in),
                                *[(mod5[4:5, n, :], I["ada_b"][0:1, 512 * n:512 * n + 512], adab_in[n]) for n in range(EARLY)],
                                (x[:, 0, :], I["x_prompt"][0], x_in), (x[:, 1, :], I["x_sample"][0], x_in)):
                act.dma_start(dst, src).then_inc(s, 16)

            def c_parts():
                act.wait_ge(setup_T, 1)
                A(cT[:, :], bank(0, 2 * KD), ACT.Silu).then_inc(c_ready, 1)
                act.wait_ge(c_ready, 1)
                A(cT4[:, :, 0:2], cT[:, :].rearrange("p (s k) -> p k s", s=2), ACT.Copy).then_inc(c_hi_ready, 1)

            def split_hi(n):
                act.wait_ge(slot_full[n % N_SLOT], 16 * (n // N_SLOT + 1))
                if hi_after[n] is not None:
                    act.wait_ge(slot_used, hi_after[n] + 1)
                A(hi_part[n], slot(n), ACT.Copy).then_inc(hi_ready, 1)

            def load_bias(l, n):
                g = 12 * l + n
                wait("spread", g - 3)
                act.dma_start(mod5[4:5, g % 4, :], I["ada_b"][l:l + 1, 512 * n:512 * n + 512]).then_inc(adab_in[g % 4], 16)

            def copy_rows(l, n):
                g = 12 * l + n
                summed(act, first["ada", l, n] + 1)
                if g >= 4:
                    wait("spread", g - 3)
                A(mod5[0:4, g % 4, :], bank(row_bank(l, n), parts=4), ACT.Copy).then_inc(Q["modrow_ready"], 1)

            def modulation(l):
                for n in range(EARLY if l == 0 else 0):
                    if n == 1:
                        c_parts()
                    for half in range(2):
                        split_hi(first["ada", l, n] + half)
                    if n:
                        copy_rows(l, n - 1)
                    if n == 2:
                        norm(l, 0, 0)
                        norm(l, 0, 1)
                if l == 0:
                    copy_rows(l, EARLY - 1)
                else:
                    norm(l, 0, 0)
                    norm(l, 0, 1)

            def norm(l, j, s):
                nu = 4 * l + 2 * j + s
                if nu >= 2:
                    wait("x_done", nu - 1)
                elif nu == 0:
                    act.wait_ge(x_in, 32)
                A(xr[:, s, :], x[:, s, :], ACT.Square, accum_out=c_(s, "ssq")).then_inc(Q["ssq_ready"], 1)

            def norm_out(l, j, s):
                nu = 4 * l + 2 * j + s
                wait("xr_T", nu + 1)
                wait("mod_ready", 2 * l + j + 1)
                for k in range(4):
                    last = A(xnT[:, k, 128 * s:128 * s + 128], bank(4 * s, 128, a=128 * k), ACT.Identity,
                             scale=modS[:, j, k, s:s + 1], bias=modT[:, 2 * j, k, s:s + 1])
                last.then_inc(Q["xnT_a"], 1)
                if nu in (2, 3):
                    wait("xnT_a", nu + 1)
                    A(a_hi[:, 0:4, 128 * s:128 * s + 128], xnT[:, 0:4, 128 * s:128 * s + 128], ACT.Copy)\
                        .then_inc(Q["xs_hi"], 1)

            def in_proj(l):
                def unit(n, s):
                    if s == 0:
                        wait("in_mm", 5 * l + n + 1)
                    else:
                        summed(act, first["in", l, n] + 1)
                    c0, c1 = IN_CUTS[n:n + 2]
                    A(h[:, s, c0:c1], bank((2 * n + s) % 4, c1 - c0), ACT.Copy).then_inc(Q["h_ready"], 1)

                def split_chunk(n):
                    for half in range(2):
                        split_hi(first["ada", l, n] + half)

                load_bias(l, EARLY)
                load_bias(l, EARLY + 1)
                split_chunk(EARLY)
                behind = None
                for kind, n, *s in IN_STEPS:
                    if kind == "in":
                        unit(n, *s)
                        if behind in (4, 5, 10, 11):
                            wait("spread", 12 * l + behind + 1)
                            for s_ in range(2):
                                half = behind % 2
                                A(gate[:, s_, behind // 10, 512 * half:512 * half + 512], bank(6 + s_), ACT.Copy)\
                                    .then_inc(Q["gate_copied"], 1)
                        behind = None
                    else:
                        copy_rows(l, n)
                        if n < 11:
                            split_chunk(n + 1)
                        if n < 10:
                            load_bias(l, n + 2)
                        behind = n
                if l == 0:
                    for n in range(EARLY):
                        load_bias(1, n)

            def softmax(l, s, X, scale, n_kt):
                u = 2 * l + s
                wait("nm" + X, u + 1)
                p = R(s, SQ, 6 * n_kt * 128)
                w = 128 * n_kt
                for hi in range(6):
                    last = A(p[:, w * hi:w * hi + w], banks(4 * s + hi // 3 * 2, 3 * w)[:, w * (hi % 3):w * (hi % 3) + w], ACT.Exp,
                             bias=c_(s, "nm")[:, hi:hi + 1], scale=scale, accum_out=c_(s, "ls")[:, hi:hi + 1])
                if X == "A":
                    last = A(c_(s, "es"), c_(s, "es"), ACT.Exp)
                last.then_inc(Q["P" + X], 1)
                yield
                wait("PT" + X, u + 1)
                n = 512 * n_kt
                A(R(s, QK, n), banks(4 * s, n), ACT.Copy).then_inc(Q["PT" + X + "_a"], 1)
                yield

            def group_A(l, s):
                u = 2 * l + s
                wait("TA", u + 1)
                n = 512 + 128 * s
                A(R(s, QKT, n), banks(4 * s, n), ACT.Copy).then_inc(Q["TA_ready"], 1)
                yield
                yield from softmax(l, s, "A", HD ** -0.5, 1 + s)

            def gates_B(l):
                wait("absf_ready", l + 1)
                absf, expl = cols["absf"][0], cols["expl"][0]
                absf, expl = small[:, :, absf:absf + 8], small[:, :, expl:expl + 8]
                link(A(expl, absf, ACT.Exp, scale=-1.0))
                A(expl, expl, ACT.Ln, bias=1.0).then_inc(Q["log_ready"], 1)

            def group_B(l, s):
                u = 2 * l + s
                wait("bc_T", u + 1)
                A(R(s, QKT, 512), bank(4 * s + 1), ACT.Copy).then_inc(Q["qkB_T"], 1)
                yield
                wait("Earg_ready", u + 1)
                A(R(s, SQ, 1024), R(s, SQ, 1024), ACT.Exp, scale=-1.0)
                A(c_(s, "em"), c_(s, "em"), ACT.Exp, scale=-1.0)
                if s == 1:
                    A(c_(s, "a"), c_(s, "a"), ACT.Exp)
                A(sig_(s), h[:, s, BO:BO + 256], ACT.Exp, scale=-1.0).then_inc(Q["E_ready"], 1)
                yield
                if s == 0:
                    wait("ws_arg", l + 1)
                    A(c_(0, "ws"), c_(0, "ws"), ACT.Exp).then_inc(Q["ws_ready"], 1)
                    wait("num_mm", u + 1)
                    st = R(0, ST, 520, 64)
                    A(st[:, 0:260], bank(3, 260, 64), ACT.Copy)
                    A(st[:, 260:520], bank(0, 260, 64), ACT.Copy).then_inc(Q["state_copied"], 1)
                yield

            def group_C(l, s):
                u = 2 * l + s
                b0 = 4 * s
                wait("TC", u + 1)
                A(R(s, QKT, 384 + 128 * s), bank(b0 + 3, 384 + 128 * s), ACT.Copy).then_inc(Q["TC_ready"], 1)
                yield
                wait("C_mm", u + 1)
                heads = R(s, QK, 18 * 96).rearrange("p (h d) -> p h d", h=18)

                def halves(b, n):
                    return PS[:, b:b + 2, 0:n]

                A(R(s, QK, 576).rearrange("p (a n) -> p a n", a=2), halves(b0, 288), ACT.Copy)

                def kv(set_):
                    src = halves(b0 + 2, 384).rearrange("p a (h d) -> p a h d", h=3)
                    dst = heads[:, 6 + 6 * set_:12 + 6 * set_, 0:C_NOPE].rearrange("p (a h) d -> p a h d", a=2)
                    A(dst, src[:, :, :, 0:C_NOPE], ACT.Copy)
                    dst = R(s, VC + 384 * set_, 384).rearrange("p (a h d) -> p a h d", a=2, h=3)
                    kr = h[:, s, CKR:CKR + C_ROPE] if set_ == 0 else ctx_kr[:, l, :]
                    A(heads[:, 6 + 6 * set_:12 + 6 * set_, C_NOPE:C_QK],
                      kr.unsqueeze(1).broadcast_to([128, 6, C_ROPE]), ACT.Copy)
                    return A(dst, src[:, :, :, C_NOPE:128], ACT.Copy)

                kv(0).then_inc(Q["C_heads"], 1)
                yield
                if s == 1:
                    summed(act, first["ukv", l])
                    kv(1).then_inc(Q["C_headsx"], 1)
                    wait("C_headsx", l + 1)
                wait("C_heads", u + 1)
                nh = 12 + 6 * s
                A(R(s, SQ, nh * 96), R(s, QK, nh * 96), ACT.Square).then_inc(Q["C_sq"], 1)
                yield
                wait("TC1", u + 1)
                A(R(s, QKT, 1024, 96), banks(b0, 1024, 96), ACT.Copy).then_inc(Q["TC1_a"], 1)
                if s == 1:
                    wait("TC2", l + 1)
                    A(R(s, QKT + 2048, 256, 96), bank(b0, 256, 96), ACT.Copy).then_inc(Q["TC2_a"], 1)
                yield
                yield from softmax(l, s, "C", C_QK ** -0.5, 1 + s)

            def both(group, l):
                a, b = group(l, 0), group(l, 1)
                for _ in a:
                    next(b)
                    yield

            def out_proj(l):
                for s in range(2):
                    wait("o_T", 2 * l + s + 1)
                    A(R(s, QKT, 512), bank(4 * s), ACT.Copy).then_inc(Q["oT_a"], 1)

            def dense_start():
                act.wait_ge(out_sem[0], 16 * 4)
                act.wait_ge(state_out[0], 16 * 3)
                for n in (first["w1", 0], first["w3", 0], first["w1", 1]):
                    split_hi(n)

            def dense_ffn():
                for f in range(N_FF):
                    for s in range(2):
                        if s == 0:
                            wait("up_mm", f + 1)
                        else:
                            summed(act, first["w3", f])
                        A(hid[s][:, 0:FF], bank(2 * (f % 2) + s, FF), ACT.Silu).then_inc(Q["silu_ready"], 1)
                    n = ada_of(f + 1)
                    if f + 1 < N_FF:
                        split_hi(first["w3", f + 1])
                    if n is None:
                        split_hi(first["w2", f])
                    else:
                        split_hi(first["ada", 1, n])
                        split_hi(first["ada", 1, n] + 1)
                    for s in range(2):
                        wait("hid_T", 2 * f + s + 1)
                        if f >= 2:
                            summed(act, first["w2", f - 2])
                        A(t_hi[:, s, 256 * (f % 2):256 * (f % 2) + 256], bank(2 * (f % 2) + s, 256), ACT.Copy)\
                            .then_inc(Q["hT_hi"], 1)
                    if n is not None:
                        split_hi(first["w2", f])
                        copy_rows(1, n)
                    if f + 2 < N_FF:
                        split_hi(first["w1", f + 2])

            def routing():
                wait("gap_ready", 1)
                a = cols["e2"][0]
                A(small[:, :, a:a + 1], small[:, :, a:a + 1], ACT.Exp).then_inc(Q["gap_exp"], 1)
                for s in range(2):
                    wait("xn_T", s + 1)
                    A(xr[:, s, 0:512], bank(4 * s), ACT.Copy).then_inc(Q["xn_a"], 1)

            def experts():
                act.wait_ge(Q["pass_ready"], 1)
                passes = act.value_load(n_pass[0:1, 0:1], min_val=1, max_val=2)

                act.wait_ge(out_sem[1], 16 * 4)
                act.wait_ge(Q["zeroed"], 1)
                with act.Fori(0, passes) as p:
                    with act.Fori(0, N_EXP) as e:
                        it = p * N_EXP + e

                        def wait_it(name, per, v):
                            act.wait_ge(Q[name], it * per + v)

                        def hi(kind, f, half):
                            j = expert_at[kind, f, half]
                            n = W0 + j
                            act.wait_ge(slot_full[n % N_SLOT], it * FULL_PER_EXPERT + 16 * (n // N_SLOT + 1))
                            act.wait_ge(slot_used, it * PER_EXPERT + (n - N_HI + 1))
                            A(w_hi(j), slot(n), ACT.Copy).then_inc(hi_ready, 1)

                        def turned(f):
                            wait_it("e_T", N_FE, f + 1)
                            if f >= 2:
                                summed(act, W0 + expert_at["w2", f - 2, 1], it)
                            A(t_hi[:, f % 2, :], bank(6 + f % 2), ACT.Copy).then_inc(Q["e_hT_hi"], 1)

                        hi("w1", 0, 0)
                        for half in range(2):
                            wait_it("gather_mm", 2, half + 1)
                            A(xe_hi[:, 4 * half:4 * half + 4, :].rearrange("p k t -> p (k t)"), bank(2 + half), ACT.Copy)\
                                .then_inc(Q["xe_hi"], 1)
                        hi("w1", 0, 1)
                        act.wait_ge(slot_used, it * PER_EXPERT + W0)
                        A(y_e[:, 0:512], bank(4), ACT.Copy).then_inc(Q["y_a"], 1)
                        hi("w3", 0, 0)
                        for f in range(N_FE):
                            hi("w3", f, 1)
                            if f:
                                turned(f - 1)
                            if f == 1:
                                wait_it("Pg_T", 1, 1)
                                A(PGT.rearrange("p s t -> p (s t)"), bank(7, 256), ACT.Copy).then_inc(Q["Pg_a"], 1)
                            summed(act, W0 + expert_at["w1", f, 1], it)
                            if f >= 2:
                                wait_it("e_T", N_FE, f - 1)
                            A(hid[f % 2], bank(2 * (f % 2)), ACT.Silu).then_inc(Q["e_silu"], 1)
                            if f:
                                hi("w2", f - 1, 0)
                                hi("w2", f - 1, 1)
                            if f + 1 < N_FE:
                                hi("w1", f + 1, 0)
                                hi("w1", f + 1, 1)
                                hi("w3", f + 1, 0)
                        hi("w2", N_FE - 1, 0)
                        turned(N_FE - 1)
                        hi("w2", N_FE - 1, 1)
                act.wait_ge(slot_used, passes * (N_EXP * PER_EXPERT) + W0)
                A(y_e[:, 0:512], bank(4), ACT.Copy).then_inc(Q["y_a"], 1)

            for l in range(DEPTH):
                modulation(l)
                norm_out(l, 0, 0)
                norm_out(l, 0, 1)
                in_proj(l)
                act.wait_ge(small_in[l], 16 * (N_SMALL + l))
                A_, B_, C_ = both(group_A, l), both(group_B, l), both(group_C, l)
                next(A_)
                next(A_)
                next(A_)
                gates_B(l)
                for group in (A_, B_, C_):
                    for _ in group:
                        pass
                out_proj(l)
                norm(l, 1, 0)
                norm(l, 1, 1)
                if l == 0:
                    dense_start()
                norm_out(l, 1, 0)
                norm_out(l, 1, 1)
                if l == 0:
                    dense_ffn()
                else:
                    routing()
                    experts()

        @block.vector
        def _(dve):
            v = nc.vector
            TT, TS, STT, RED = v.tensor_tensor, v.tensor_scalar, v.scalar_tensor_tensor, v.tensor_reduce
            chain = [0]

            def wait(name, n):
                dve.wait_ge(Q[name], n)

            def link(ins):
                chain[0] += 1
                ins.then_inc(dve_chain, 1)
                dve.wait_ge(dve_chain, chain[0])

            def rsqrt(s, n):
                def col(name):
                    a = cols[name][0]
                    return small[:, :, a:a + n] if s is None else c_(s, name, n)

                y, t, w, bits = col("rs"), col("tmp"), col("var"), col("bits").bitcast(i32)
                link(v.tensor_single_scalar(bits, w.bitcast(i32), 1, op=ALU.logical_shift_right))
                link(TS(y.bitcast(i32), bits, -1.0, float(0x5F3759DF), ALU.mult, ALU.add))
                for _ in range(3):
                    link(TT(t, y, y, ALU.mult))
                    link(STT(t, t, -0.5, w, ALU.mult, ALU.mult))
                    link(STT(y, t, 1.5, y, ALU.add, ALU.mult))
                return y

            v.memset(m0row[:, 0:1], 0.0).then_inc(zeros_ready, 1)
            dve.wait_ge(zeros_ready, 1)

            def c_parts():
                dve.wait_ge(setup_T, 1)
                v.tensor_copy(ngT[:, :], bank(1, 4 * KD)).then_inc(ng_ready, 1)
                dve.wait_ge(ng_ready, 1)
                dve.wait_ge(c_hi_ready, 1)
                TT(cT4[:, :, 2:4], cT[:, :].rearrange("p (s k) -> p k s", s=2), cT4[:, :, 0:2].bitcast(f32), ALU.subtract)\
                    .then_inc(c_lo_ready, 1)

            def split_lo(n):
                dve.wait_ge(hi_ready, split_at[n] + 1)
                if lo_after[n] is not None:
                    dve.wait_ge(slot_used, lo_after[n] + 1)
                TT(lo_part[n], slot(n), hi_part[n].bitcast(f32), ALU.subtract).then_inc(split_done, 1)

            def mod_columns(l, j):
                wait("spread", 12 * l + (EARLY if j == 0 else 10))
                cols4 = modT[:, 2 * j:2 * j + 2, :, :]
                link(v.tensor_copy(cols4.rearrange("p j k s -> p (j k s)"), bank(2 if j == 0 else 6, 32)))
                g = ngT[:, 2 * KD * j + KD * l:2 * KD * j + KD * l + KD].unsqueeze(2).broadcast_to([128, KD, 2])
                STT(modS[:, j, :, :], modT[:, 2 * j + 1, :, :], 1.0, g, ALU.add, ALU.mult).then_inc(Q["mod_ready"], 1)
                wait("mod_ready", 2 * l + j + 1)

            def modulation(l):
                for n in range(EARLY if l == 0 else 0):
                    if n == 1:
                        c_parts()
                    if n == 3:
                        norm(l, 0)
                    for half in range(2):
                        split_lo(first["ada", l, n] + half)
                mod_columns(l, 0)
                if l == 1:
                    norm(l, 0)

            def late_modulation(l, first_of_A):
                for n in range(EARLY, 12):
                    for half in range(2):
                        split_lo(first["ada", l, n] + half)
                    if n == 8:
                        dve.wait_ge(small_in[l], 16 * (N_SMALL + l))
                    if n in (8, 9):
                        next(first_of_A[n - 8])
                    if n == 10:
                        mod_columns(l, 1)

            def norm(l, j):
                nu = 4 * l + 2 * j
                wait("ssq_ready", nu + 2)
                a, b = cols["ssq"][0], cols["var"][0]
                link(TS(small[:, :, b:b + 1], small[:, :, a:a + 1], 1.0 / D, EPS, ALU.mult, ALU.add))
                r = rsqrt(None, 1)
                for s in range(2):
                    TS(xr[:, s, :], x[:, s, :], r[:, s, :], None, ALU.mult).then_inc(Q["xr_ready"], 1)

            def norm_out(l, j, s):
                nu = 4 * l + 2 * j + s
                wait("xr_T", nu + 1)
                for k in range(4, KD):
                    last = TS(xnT[:, k, 128 * s:128 * s + 128], bank(4 * s + 1, 128, a=128 * (k - 4)),
                              modS[:, j, k, s:s + 1], modT[:, 2 * j, k, s:s + 1], ALU.mult, ALU.add)
                last.then_inc(Q["xnT_d"], 1)
                if nu in (2, 3):
                    wait("xnT_d", nu + 1)
                    t = slice(128 * s, 128 * s + 128)
                    link(v.tensor_copy(a_hi[:, 4:8, t], xnT[:, 4:8, t]))
                    wait("xs_hi", s + 1)
                    TT(a_lo[:, :, t], xnT[:, :, t], a_hi[:, :, t].bitcast(f32), ALU.subtract).then_inc(Q["xs_ready"], 1)

            def rope(x_, out, cos, sin, n, half, tmp):
                x1, x2 = x_[:, :, 0:half], x_[:, :, half:2 * half]
                c = cos.unsqueeze(1).broadcast_to([128, n, half])
                s_ = sin.unsqueeze(1).broadcast_to([128, n, half])
                TT(tmp[0], x1, c, ALU.mult)
                TT(tmp[1], x2, s_, ALU.mult)
                TT(tmp[2], x1, s_, ALU.mult)
                link(TT(tmp[3], x2, c, ALU.mult))
                TT(out[:, :, 0:half], tmp[0], tmp[1], ALU.subtract)
                return TT(out[:, :, half:2 * half], tmp[2], tmp[3], ALU.add)

            def softmax(l, s, X, scale, n_kt):
                u = 2 * l + s
                w = 128 * n_kt
                wait("S" + X, u + 1)
                lots = banks(4 * s, 2048).rearrange("p (a n) -> p a n", a=2)[:, :, 0:3 * w]
                link(RED(c_(s, "mx").rearrange("p (a h) -> p a h", a=2), lots.rearrange("p a (h n) -> p a h n", h=3),
                         AX.X, ALU.max))
                if X == "A":
                    sink, mx = G(l, "a_sink"), c_(s, "mx")
                    link(STT(mx, mx, scale, sink, ALU.mult, ALU.max))
                    TT(c_(s, "es"), sink, mx, ALU.subtract)
                    TS(c_(s, "nm"), c_(s, "mx"), -1.0, None, ALU.mult).then_inc(Q["nm" + X], 1)
                else:
                    TS(c_(s, "nm"), c_(s, "mx"), -scale, None, ALU.mult).then_inc(Q["nm" + X], 1)
                yield
                wait("P" + X, u + 1)
                if X == "A":
                    link(TT(c_(s, "ls"), c_(s, "ls"), c_(s, "es"), ALU.add))
                link(v.reciprocal(c_(s, "rinv"), c_(s, "ls")))
                wait("PT" + X, u + 1)
                n, all_ = 512 * n_kt, 768 * n_kt
                v.tensor_copy(R(s, QK + n, all_ - n), banks(4 * s, all_)[:, n:all_]).then_inc(Q["PT" + X + "_d"], 1)
                yield
                wait("O" + X, u + 1)
                a = 0 if X == "A" else 640
                TT(o[:, s, a:a + 384].rearrange("p (h d) -> p h d", d=HD), bank(4 * s + 3, 384).rearrange("p (h d) -> p h d", d=HD),
                   c_(s, "rinv").unsqueeze(2).broadcast_to([128, 6, HD]), ALU.mult).then_inc(Q["o" + X], 1)
                yield

            def group_A(l, s):
                u = 2 * l + s
                wait("h_ready", 10 * l + 2 + s + 1)
                a8 = h[:, s, 0:512]
                link(TT(R(s, SQ, 512), a8, a8, ALU.mult))
                link(RED(c_(s, "tmp", 8), R(s, SQ, 512).rearrange("p (h d) -> p h d", h=8), AX.X, ALU.add))
                link(TS(c_(s, "var", 8), c_(s, "tmp", 8), 1.0 / HD, EPS, ALU.mult, ALU.add))
                r = rsqrt(s, 8)
                link(TT(R(s, SQ, 512).rearrange("p (h d) -> p h d", h=8), a8.rearrange("p (h d) -> p h d", h=8),
                        r.unsqueeze(2).broadcast_to([128, 8, HD]), ALU.mult))
                qg = G(l, "a_qn_g").unsqueeze(1).broadcast_to([128, 3, HD])
                kg = G(l, "a_kn_g").unsqueeze(1).broadcast_to([128, 2, HD])
                for g in range(2):
                    TT(R(s, QK, 384).rearrange("p (r g d) -> p r g d", g=2, d=HD)[:, :, g, :],
                       R(s, SQ + 192 * g, 192).rearrange("p (r d) -> p r d", d=HD), qg, ALU.mult)
                if s == 0 and l == 1:
                    dve.wait_ge(out_sem[0], 16 * 4)
                kdst = ka_out[:, :] if s == 0 else R(s, QK + 384, 128)
                last = TT(kdst.rearrange("p (g d) -> p g d", d=HD),
                          R(s, SQ + 384, 128).rearrange("p (g d) -> p g d", d=HD), kg, ALU.mult)
                if s == 1:
                    link(last)
                    last = rope(R(s, QK, 512).rearrange("p (h d) -> p h d", h=8),
                                R(s, QK + 512, 512).rearrange("p (h d) -> p h d", h=8), K("cosA"), K("sinA"), 8, 32,
                                [R(s, SQ + 256 * i, 256).rearrange("p (h d) -> p h d", h=8) for i in range(4)])
                last.then_inc(Q["qkA_ready"], 1)
                yield
                yield from softmax(l, s, "A", HD ** -0.5, 1 + s)

            def gates_of(s, which):
                return c_(s, "g16").rearrange("p (d k h) -> p d k h", d=2, k=2)[:, :, which, :]

            def two(s, name):
                return c_(s, name).rearrange("p (d h) -> p d h", d=2)

            def gates_B(l):
                wait("h_ready", 10 * l + 8)
                for s in range(2):
                    link(TT(c_(s, "g16"), h[:, s, BG:BG + 16], G(l, "b_gate_b"), ALU.add))
                    last = STT(two(s, "absf"), gates_of(s, 1), -1.0, gates_of(s, 1), ALU.mult, ALU.max)
                last.then_inc(Q["absf_ready"], 1)
                for s in range(2):
                    TS(R(s, KS, 256), h[:, s, BK:BK + 256], HD ** -0.5, None, ALU.mult)
                    v1 = R(s, V1, 4 * 65).rearrange("p (h n) -> p h n", h=4)
                    v.memset(v1[:, :, HD:HD + 1], 1.0)
                    v.tensor_copy(v1[:, :, 0:HD], h[:, s, BV:BV + 256].rearrange("p (h d) -> p h d", h=4))

            def log_gates_B(l):
                wait("log_ready", l + 1)
                for s in range(2):
                    last = STT(two(s, "lf"), gates_of(s, 1), 0.0, two(s, "expl"), ALU.min, ALU.subtract)
                last.then_inc(Q["lf_ready"], 1)

            def group_B(l, s):
                u = 2 * l + s
                wait("bc_T", u + 1)
                m16 = c_(s, "m16")
                v.tensor_copy(m16[:, 8:16], bank(4 * s, 8))
                TT(two(s, "u"), gates_of(s, 0), bank(4 * s, 8).rearrange("p (d h) -> p d h", d=2), ALU.subtract).then_inc(Q["u_ready"], 1)
                yield
                wait("uT_S", u + 1)
                run = MFB[:, s, :, :]
                link(v.tensor_copy(run[:, 0, :], bank(4 * s + 2, 128, 8)))
                m0 = m0row[:, (1 + l) * s:(1 + l) * s + 1]
                v.tensor_tensor_scan(run[:, 1, :], run[:, 0, :], run[:, 0, :], m0, ALU.max, ALU.max)
                v.tensor_tensor_scan(run[:, 2, ::-1], run[:, 0, ::-1], run[:, 0, ::-1], m0, ALU.max, ALU.max)\
                    .then_inc(Q["run_ready"], 1)
                yield
                wait("M_mm", u + 1)
                link(v.tensor_copy(m16[:, 0:8], bank(4 * s, 8, a=256)))
                if s == 1:
                    TT(c_(s, "a"), G(l, "m0"), m16[:, 0:8], ALU.subtract)
                TT(c_(s, "em"), m16[:, 0:8], m16[:, 8:16], ALU.add)
                mask = K("mask").rearrange("p (d t) -> p d t", d=2)
                for c in range(8):
                    last = STT(R(s, SQ + 128 * c, 128), bank(4 * s + 1 + c // 4, 128, a=128 * (c % 4)),
                               c_(s, "u")[:, c:c + 1], mask[:, c // 4, :], ALU.subtract, ALU.add)
                last.then_inc(Q["Earg_ready"], 1)
                if s == 0:
                    wait("last_mm", l + 1)
                    TT(c_(0, "ws"), c_(0, "u"), bank(0, 8, a=288), ALU.subtract).then_inc(Q["ws_arg"], 1)
                    tot = c_(0, "mo")
                    link(v.tensor_copy(tot, bank(0, 8, a=296)))
                    TT(tot, tot, bank(0, 8, a=288), ALU.add)
                yield
                wait("E_ready", u + 1)
                for par in range(2):
                    def heads_of(a):
                        return R(s, a, 1024).rearrange("p (d a b t) -> p d a b t", d=2, a=2, b=2)[:, :, :, par, :]

                    sT = bank(4 * s + 3 * par, 256).rearrange("p (a t) -> p a t", a=2)
                    last = TT(heads_of(QK), heads_of(SQ), sT.unsqueeze(1).broadcast_to([128, 2, 2, 128]), ALU.mult)
                last.then_inc(Q["WT_ready"], 1)
                if s == 0:
                    wait("ws_ready", l + 1)
                    for d in range(2):
                        last = TT(R(0, KW + 256 * d, 256).rearrange("p (h d) -> p h d", h=4),
                                  R(0, KS, 256).rearrange("p (h d) -> p h d", h=4),
                                  c_(0, "ws")[:, 4 * d:4 * d + 4].unsqueeze(2).broadcast_to([128, 4, HD]), ALU.mult)
                    last.then_inc(Q["kw_ready"], 1)
                yield
                wait("num_mm", u + 1)
                num = num_(s).rearrange("p (c n) -> p c n", c=8)

                def four(b):
                    return bank(b, 260).rearrange("p (c n) -> p c n", c=4)

                for d in range(2):
                    if s == 0:
                        last = v.tensor_copy(num[:, 4 * d:4 * d + 4, :], four(4 * s + 1 + d))
                    else:
                        if d == 0:
                            for par in range(2):
                                last = TT(num.rearrange("p (a b) n -> p a b n", b=2)[:, :, par, :], four(4 * s + 3 * par),
                                          c_(s, "a").rearrange("p (a b) -> p a b", b=2)[:, :, par].unsqueeze(2)
                                          .broadcast_to([128, 4, HD + 1]), ALU.mult)
                            link(last)
                        last = TT(num[:, 4 * d:4 * d + 4, :], num[:, 4 * d:4 * d + 4, :], four(4 * s + 1 + d), ALU.add)
                last.then_inc(Q["num_read"], 1)
                wait("num_read", u + 1)
                yield

            def tail_B(l, s):
                u = 2 * l + s
                num = num_(s).rearrange("p (c n) -> p c n", c=8)
                den, t8, r8 = num[:, :, HD], c_(s, "tmp", 8), c_(s, "rs", 8)
                link(STT(t8, den, -1.0, den, ALU.mult, ALU.max))
                link(TT(t8, t8, c_(s, "em"), ALU.max))
                link(v.reciprocal(r8, t8))
                h8 = h8_(s)[:, 0:512]
                link(TT(h8.rearrange("p (c d) -> p c d", c=8), num[:, :, 0:HD],
                        r8.unsqueeze(2).broadcast_to([128, 8, HD]), ALU.mult))
                hs = h8_(s)[:, 512:768]
                link(TT(hs, h8[:, 0:256], h8[:, 256:512], ALU.add))
                link(TT(h8[:, 0:256], hs, hs, ALU.mult))
                link(RED(t8[:, 0:4], h8[:, 0:256].rearrange("p (h d) -> p h d", h=4), AX.X, ALU.add))
                link(TS(c_(s, "var", 4), t8[:, 0:4], 1.0 / HD, EPS, ALU.mult, ALU.add))
                yield
                r4 = rsqrt(s, 4)
                yield
                sig = sig_(s)
                link(TS(sig, sig, 1.0, None, ALU.add))
                link(v.reciprocal(sig, sig))
                hs4 = hs.rearrange("p (h d) -> p h d", h=4)
                link(TT(hs4, hs4, r4.unsqueeze(2).broadcast_to([128, 4, HD]), ALU.mult))
                link(TT(hs4, hs4, G(l, "b_hn_g").unsqueeze(1).broadcast_to([128, 4, HD]), ALU.mult))
                link(TT(o[:, s, 384:640], hs, sig, ALU.mult))

            def norms_C(l, s):
                u = 2 * l + s
                wait("h_ready", 10 * l + 8 + s + 1)
                lat = h[:, s, CQ:CQ + 384]
                link(TT(R(s, CSQ, 384), lat, lat, ALU.mult))
                RED(c_(s, "tmp")[:, 0:1], R(s, CSQ, 256), AX.X, ALU.add)
                link(RED(c_(s, "tmp")[:, 1:2], R(s, CSQ + 256, 128), AX.X, ALU.add))
                TS(c_(s, "var")[:, 0:1], c_(s, "tmp")[:, 0:1], 1.0 / C_QR, EPS, ALU.mult, ALU.add)
                link(TS(c_(s, "var")[:, 1:2], c_(s, "tmp")[:, 1:2], 1.0 / C_KVR, EPS, ALU.mult, ALU.add))
                r = rsqrt(s, 2)
                STT(cq_(s), lat[:, 0:256], r[:, 0:1], G(l, "c_qa_g"), ALU.mult, ALU.mult)
                STT(ckv_out[:, :] if s == 0 else c_lat[:, 512:640], lat[:, 256:384], r[:, 1:2], G(l, "c_kva_g"),
                    ALU.mult, ALU.mult).then_inc(Q["cn_ready"], 1)

            def group_C(l, s):
                u = 2 * l + s
                wait("C_sq", u + 1)
                nh = 12 + 6 * s
                qk = R(s, QK, nh * 96).rearrange("p (h d) -> p h d", h=nh)
                sq = R(s, SQ, nh * 96).rearrange("p (h d) -> p h d", h=nh)
                link(RED(c_(s, "tmp", nh), sq, AX.X, ALU.add))
                link(TS(c_(s, "var", nh), c_(s, "tmp", nh), 1.0 / C_QK, EPS, ALU.mult, ALU.add))
                r = rsqrt(s, nh)
                link(TT(qk, qk, r.unsqueeze(2).broadcast_to([128, nh, C_QK]), ALU.mult))
                TT(qk[:, 0:6, :], qk[:, 0:6, :], G(l, "c_qn_g").unsqueeze(1).broadcast_to([128, 6, C_QK]), ALU.mult)
                last = TT(qk[:, 6:nh, :], qk[:, 6:nh, :], G(l, "c_kn_g").unsqueeze(1).broadcast_to([128, nh - 6, C_QK]),
                          ALU.mult)
                if s == 1:
                    link(last)
                    tail = qk[:, 0:12, C_NOPE:C_QK]
                    last = rope(tail, tail, K("cosC"), K("sinC"), 12, 16,
                                [R(s, SQ + 192 * i, 192).rearrange("p (h d) -> p h d", h=12) for i in range(4)])
                last.then_inc(Q["qkC_ready"], 1)
                yield
                wait("TC1", u + 1)
                n = 128 * min(nh, 16)
                v.tensor_copy(R(s, QKT + 1024, n - 1024, 96), banks(4 * s, n, 96)[:, 1024:n]).then_inc(Q["TC1_d"], 1)
                yield
                yield from softmax(l, s, "C", C_QK ** -0.5, 1 + s)

            def pair(a, b):
                for _ in a:
                    next(b)
                    yield

            def both(group, l):
                return pair(group(l, 0), group(l, 1))

            def residual(l, j, s, n, src, tmp):
                xs = x[:, s, 512 * n:512 * n + 512]
                link(TT(tmp, src, gate[:, s, j, 512 * n:512 * n + 512], ALU.mult))
                last = TT(xs, xs, tmp, ALU.add)
                if n == 1:
                    last.then_inc(Q["x_done"], 1)
                    wait("x_done", 4 * l + 2 * j + s + 1)
                else:
                    link(last)

            def out_proj(l):
                for s in range(2):
                    wait("o_T", 2 * l + s + 1)
                    v.tensor_copy(R(s, QKT + 512, 512), bank(4 * s + 1)).then_inc(Q["oT_d"], 1)
                if l == 1:
                    v.memset(acc, 0.0)
                    v.memset(PGT, 0.0)
                for n in range(2):
                    for s in range(2):
                        if s == 0:
                            wait("out_mm", 2 * l + n + 1)
                        else:
                            summed(dve, first["out", l] + 2 * n + 1)
                        residual(l, 0, s, n, bank(4 * s + 2 + n), R(s, SQ, 512))

            def dense_ffn():
                split_lo(first["w3", 0])
                for f in range(N_FF):
                    if f + 1 < N_FF:
                        split_lo(first["w1", f + 1])
                    for s in range(2):
                        wait("silu_ready", 2 * f + s + 1)
                        TT(hid[s][:, 0:FF], hid[s][:, 0:FF], bank(2 * (f % 2) + s, FF, a=FF), ALU.mult)\
                            .then_inc(Q["hid_ready"], 1)
                    if f + 1 < N_FF:
                        split_lo(first["w3", f + 1])
                    for s in range(2):
                        wait("hT_hi", 2 * f + s + 1)
                        a = slice(256 * (f % 2), 256 * (f % 2) + 256)
                        TT(t_lo[:, s, a], bank(2 * (f % 2) + s, 256), t_hi[:, s, a].bitcast(f32), ALU.subtract)\
                            .then_inc(Q["hT_ready"], 1)
                    if ada_of(f + 1) is not None:
                        for half in range(2):
                            split_lo(first["ada", 1, ada_of(f + 1)] + half)
                    split_lo(first["w2", f])
                summed(dve, first["w2", N_FF - 1])
                for s in range(2):
                    for n in range(2):
                        residual(0, 1, s, n, bank(4 + 2 * s + n), hid[0])

            def routing():
                def two(name, n):
                    a = cols[name][0]
                    return small[:, :, a:a + n]

                def each(name):
                    return two(name, 1).broadcast_to([128, 2, N_EXP])

                wait("logits_mm", 1)
                for s in range(2):
                    last = v.tensor_copy(c_(s, "lg"), bank(4 * s + 2, N_EXP))
                link(last)
                for s in range(2):
                    last = v.max(c_(s, "v8"), c_(s, "lg"))
                link(last)
                for s in range(2):
                    last = v.max_index(c_(s, "i8").bitcast(u32), c_(s, "v8"), c_(s, "lg"))
                v8 = two("v8", 2)
                TT(two("e2", 1), v8[:, :, 1:2], v8[:, :, 0:1], ALU.subtract).then_inc(Q["gap_ready"], 1)
                wait("gap_ready", 1)
                link(v.tensor_copy(two("if", 2), two("i8", 2).bitcast(u32)))
                iota8 = K("iota8").unsqueeze(1).broadcast_to([128, 2, N_EXP])
                i1, i2 = two("if", 1), two("if", 2)[:, :, 1:2]
                TT(two("eq", 8), iota8, i2.broadcast_to([128, 2, N_EXP]), ALU.is_equal)
                link(TT(two("sel", 8), iota8, i1.broadcast_to([128, 2, N_EXP]), ALU.is_equal))
                wait("gap_exp", 1)
                link(TS(two("w1", 1), two("e2", 1), 1.0, None, ALU.add))
                link(v.reciprocal(two("w1", 1), two("w1", 1)))
                link(TT(two("w2", 1), two("w1", 1), two("e2", 1), ALU.mult))
                gt = two("gt", 8)
                TT(gt, two("sel", 8), each("w1"), ALU.mult)
                link(TT(two("lg", 8), two("eq", 8), each("w2"), ALU.mult))
                TT(gt, gt, two("lg", 8), ALU.add)
                TT(two("sel", 8), two("sel", 8), two("eq", 8), ALU.add).then_inc(Q["sel_ready"], 1)
                for s in range(2):
                    wait("xn_T", s + 1)
                    v.tensor_copy(xr[:, s, 512:1024], bank(4 * s + 1)).then_inc(Q["xn_d"], 1)
                wait("sel_ready", 1)
                wait("pos_mm", 1)
                for s in range(2):
                    link(STT(c_(s, "posm", 8), bank(3, 8, a=8 * s), 1.0, c_(s, "sel"), ALU.add, ALU.mult))
                    link(TS(c_(s, "posm", 8), c_(s, "posm", 8), -1.0, None, ALU.add))
                    TS(c_(s, "posm")[:, 8:16], c_(s, "posm", 8), -float(TOK), None, ALU.add)
                    v.tensor_copy(c_(s, "gt")[:, 8:16], c_(s, "gt", 8))
                    v.memset(c_(s, "posm")[:, 16:17], -1.0)
                    link(v.memset(c_(s, "gt")[:, 16:17], 0.0))
                link(RED(c_(0, "cnt"), bank(3, 8, a=16), AX.X, ALU.max))
                link(TS(c_(0, "cnt"), c_(0, "cnt"), float(TOK), 1.0, ALU.is_gt, ALU.add))
                v.tensor_copy(n_pass[:, :], c_(0, "cnt")).then_inc(Q["pass_ready"], 1)

            def experts():
                def make_places(i):
                    for s in range(2):
                        pos = c_(s, "posm")[:, bass.ds(i, 1)]
                        TS(P[:, s, :], K("iota"), pos, None, ALU.is_equal)
                        last = TS(PG[:, s, :], K("iota"), pos, c_(s, "gt")[:, bass.ds(i, 1)], ALU.is_equal, ALU.mult)
                    last.then_inc(Q["P_ready"], 1)

                def add_scattered(it):
                    for i in range(4):
                        dve.wait_ge(Q["scat_mm"], it * 4 + (i + 1))
                        TT(acc[:, i, :], acc[:, i, :], bank(SCAT_BANKS[i]), ALU.add).then_inc(Q["acc_done"], 1)

                make_places(0)
                wait("xn_a", 2)
                v.memset(banks(4, 1024), 0.0).then_inc(Q["zeroed"], 1)
                wait("zeroed", 1)
                wait("pass_ready", 1)
                passes = dve.value_load(n_pass[0:1, 0:1], min_val=1, max_val=2)
                with dve.Fori(0, passes) as p:
                    with dve.Fori(0, N_EXP) as e:
                        it = p * N_EXP + e

                        def wait_it(name, per, n):
                            dve.wait_ge(Q[name], it * per + n)

                        def lo(kind, f, half):
                            j = expert_at[kind, f, half]
                            dve.wait_ge(hi_ready, it * PER_EXPERT + (N_SPLIT + j + 1))
                            dve.wait_ge(slot_used, it * PER_EXPERT + (W0 + j - 3 + 1))
                            TT(w_lo(j, 3), slot(W0 + j), w_hi(j).bitcast(f32), ALU.subtract).then_inc(split_done, 1)

                        def turned(f):
                            wait_it("e_hT_hi", N_FE, f + 1)
                            TT(t_lo[:, f % 2, :], bank(6 + f % 2), t_hi[:, f % 2, :].bitcast(f32), ALU.subtract)\
                                .then_inc(Q["e_hT"], 1)

                        lo("w1", 0, 0)
                        for half in range(2):
                            wait_it("xe_hi", 2, half + 1)
                            k = slice(4 * half, 4 * half + 4)
                            TT(xe_lo[:, k, :].rearrange("p k t -> p (k t)"), bank(2 + half),
                               xe_hi[:, k, :].rearrange("p k t -> p (k t)").bitcast(f32), ALU.subtract)\
                                .then_inc(Q["xe_ready"], 1)
                        lo("w1", 0, 1)
                        dve.wait_ge(slot_used, it * PER_EXPERT + W0)
                        v.tensor_copy(y_e[:, 512:1024], bank(5)).then_inc(Q["y_d"], 1)
                        lo("w3", 0, 0)
                        for f in range(N_FE):
                            lo("w3", f, 1)
                            if f:
                                turned(f - 1)
                                lo("w2", f - 1, 0)
                                lo("w2", f - 1, 1)
                            else:
                                add_scattered(it)
                                lo("w1", 1, 0)
                                lo("w1", 1, 1)
                            wait_it("e_silu", N_FE, f + 1)
                            summed(dve, W0 + expert_at["w3", f, 1], it)
                            TT(hid[f % 2], hid[f % 2], bank(2 * (f % 2) + 1), ALU.mult).then_inc(Q["e_hid"], 1)
                            if 1 <= f and f + 1 < N_FE:
                                lo("w1", f + 1, 0)
                                lo("w1", f + 1, 1)
                            if f + 1 < N_FE:
                                lo("w3", f + 1, 0)
                            if f == 2:
                                wait_it("Pg_T", 1, 1)
                                make_places(it + 1)
                        lo("w2", N_FE - 1, 0)
                        turned(N_FE - 1)
                        lo("w2", N_FE - 1, 1)
                dve.wait_ge(slot_used, passes * (N_EXP * PER_EXPERT) + W0)
                v.tensor_copy(y_e[:, 512:1024], bank(5)).then_inc(Q["y_d"], 1)
                add_scattered(passes * N_EXP)
                dve.wait_ge(Q["acc_done"], passes * (4 * N_EXP) + 4)
                for s in range(2):
                    for n in range(2):
                        residual(1, 1, s, n, acc[:, 2 * s + n, :], hid[0])

            for l in range(DEPTH):
                modulation(l)
                norm_out(l, 0, 0)
                norm_out(l, 0, 1)
                A_ = [group_A(l, 0), group_A(l, 1)]
                late_modulation(l, A_)
                A_, B_ = pair(*A_), both(group_B, l)
                next(A_)
                gates_B(l)
                next(A_)
                norms_C(l, 0)
                log_gates_B(l)
                next(A_, None)
                next(B_)
                next(B_)
                norms_C(l, 1)
                for group in (A_, B_):
                    for _ in group:
                        pass
                for _ in tail_B(l, 0):
                    pass
                C0, C1, B1 = group_C(l, 0), group_C(l, 1), tail_B(l, 1)
                next(C0)
                next(C1)
                next(C0)
                next(B1)
                next(C1)
                next(C0)
                next(B1)
                next(C1)
                next(B1, None)
                for _ in pair(C0, C1):
                    pass
                dve.wait_ge(state_out[l], 16 * 3)
                out_proj(l)
                norm(l, 1)
                if l == 0:
                    split_lo(first["w1", 0])
                norm_out(l, 1, 0)
                norm_out(l, 1, 1)
                if l == 0:
                    dense_ffn()
                else:
                    routing()
                    experts()


INPUTS = ['x_prompt', 'x_sample', 'c', 'cache_swa_k', 'cache_swa_v', 'cache_mla_ckv', 'cache_mla_krope',
          'state_mlstm_C', 'state_mlstm_n', 'state_mlstm_m', 'c_ctx', 'ada_w', 'ada_b', 'norm1_g', 'norm2_g', 'w_in',
          'a_qn_g', 'a_kn_g', 'a_sink', 'b_gate_b', 'b_hn_g', 'c_qa_g', 'c_kva_g', 'c_wuq', 'c_wukv', 'c_qn_g',
          'c_kn_g', 'w_out', 'ffn_w1', 'ffn_w3', 'ffn_w2', 'moe_router', 'moe_w1', 'moe_w3', 'moe_w2']
OUTPUTS = [("y_prompt", (1, TOK, D)), ("y_sample", (1, TOK, D)),
           ("new_swa_k", (1, DEPTH, TOK, A_KV, HD)), ("new_swa_v", (1, DEPTH, TOK, A_KV, HD)),
           ("new_mla_ckv", (1, DEPTH, TOK, C_KVR)), ("new_mla_krope", (1, DEPTH, TOK, C_ROPE)),
           ("new_mlstm_C", (1, DEPTH, 2, B_H, HD, HD)), ("new_mlstm_n", (1, DEPTH, 2, B_H, HD)),
           ("new_mlstm_m", (1, DEPTH, 2, B_H))]


def kernel(**inputs):
    import concourse.bacc as bacc
    from concourse.bass_utils import run_bass_kernel_spmd

    nc = bacc.Bacc("TRN2", target_bir_lowering=False, num_devices=1)
    arrays = {f"in_{n}": np.ascontiguousarray(inputs[n]) for n in INPUTS}
    arrays["in_consts"] = constants()
    ins = {n[3:]: nc.dram_tensor(n, a.shape, mybir.dt.from_np(a.dtype), kind="ExternalInput").ap()
           for n, a in arrays.items()}
    outs = {n: nc.dram_tensor(f"out_{n}", shape, mybir.dt.float32, kind="ExternalOutput").ap() for n, shape in OUTPUTS}
    build_program(nc, ins, outs)
    r = run_bass_kernel_spmd(nc, [arrays], core_ids=[0])
    return tuple(r.results[0][f"out_{n}"] for n, _ in OUTPUTS)
```
